# Optimizing a Trainium2 kernel written in Bass

```python
import jax, jax.numpy as jnp
from jax import lax
import numpy as np
import math

D_MODEL = 1024
BATCH = 1
SEQ = 512
DEPTH = 1

CHUNK = 64
N_META = 16
Q_BLOCK = 128
HEAD_DIM = 64
N_HEADS_FOX = 8
N_HEADS_SB = 8
WIDTH_FOX = N_HEADS_FOX * HEAD_DIM
WIDTH_SB = N_HEADS_SB * HEAD_DIM
D_FF = 2816
CONV_WIDTH = 3
EPS = 1e-6

SPLIT_SIZES = (WIDTH_FOX, WIDTH_FOX, WIDTH_FOX, N_HEADS_FOX,
               WIDTH_SB, WIDTH_SB, WIDTH_SB, D_MODEL, D_MODEL)
PROJ_WIDTH = sum(SPLIT_SIZES)
SPLIT_POINTS = tuple(sum(SPLIT_SIZES[:i + 1]) for i in range(len(SPLIT_SIZES) - 1))


def rms_norm(x, g):
    xf = x.astype(jnp.float32)
    y = xf * lax.rsqrt(jnp.mean(xf * xf, axis=-1, keepdims=True) + EPS)
    return (y * g.astype(jnp.float32)).astype(x.dtype)

def _split_heads(t, n_heads):
    b, l, _ = t.shape
    return t.reshape(b, l, n_heads, HEAD_DIM).transpose(0, 2, 1, 3)

def _merge_heads(t):
    b, h, l, d = t.shape
    return t.transpose(0, 2, 1, 3).reshape(b, l, h * d)

def forgetting_attention(q, k, v, log_f):
    seq_len = q.shape[2]
    scale = HEAD_DIM ** -0.5
    c = jnp.cumsum(log_f, axis=-1)
    outs = []
    for start in range(0, seq_len, Q_BLOCK):
        end = min(start + Q_BLOCK, seq_len)
        s = jnp.einsum('bhqd,bhkd->bhqk', q[:, :, start:end], k[:, :, :end],
                       preferred_element_type=jnp.float32) * scale
        s = s + c[:, :, start:end, None] - c[:, :, None, :end]
        t_pos = jnp.arange(start, end)[:, None]
        s_pos = jnp.arange(end)[None, :]
        s = jnp.where(s_pos <= t_pos, s, -jnp.inf)
        p = jax.nn.softmax(s, axis=-1)
        outs.append(jnp.einsum('bhqk,bhkd->bhqd', p.astype(v.dtype), v[:, :, :end]))
    return jnp.concatenate(outs, axis=2)

def stick_breaking_attention(q, k, v):
    seq_len = q.shape[2]
    scale = HEAD_DIM ** -0.5
    outs = []
    for start in range(0, seq_len, Q_BLOCK):
        end = min(start + Q_BLOCK, seq_len)
        z = jnp.einsum('bhqd,bhkd->bhqk', q[:, :, start:end], k[:, :, :end],
                       preferred_element_type=jnp.float32) * scale
        t_pos = jnp.arange(start, end)[:, None]
        s_pos = jnp.arange(end)[None, :]
        causal = s_pos < t_pos
        log_keep = jnp.where(causal, jax.nn.log_sigmoid(-z), 0.0)
        later = lax.cumsum(log_keep, axis=3, reverse=True) - log_keep
        a = jnp.where(causal, jnp.exp(jax.nn.log_sigmoid(z) + later), 0.0)
        outs.append(jnp.einsum('bhqk,bhkd->bhqd', a.astype(v.dtype), v[:, :, :end]))
    return jnp.concatenate(outs, axis=2)

def causal_depthwise_conv(u, w, b):
    seq_len = u.shape[1]
    up = jnp.pad(u, ((0, 0), (CONV_WIDTH - 1, 0), (0, 0)))
    out = b.astype(u.dtype)
    for i in range(CONV_WIDTH):
        out = out + w[i] * up[:, i:i + seq_len]
    return out

def first_inputs(seed: int = 0) -> dict:
    key = jax.random.key(seed)
    ks = jax.random.split(key, 13)
    x = jax.random.normal(ks[0], (BATCH, SEQ, D_MODEL), jnp.float32)
    meta_tokens = jax.random.normal(ks[1], (N_META, D_MODEL), jnp.float32)
    norm_gains = 1.0 + 0.05 * jax.random.normal(ks[2], (DEPTH, 4, D_MODEL), jnp.float32)
    w_in = jax.random.normal(ks[3], (DEPTH, D_MODEL, PROJ_WIDTH), jnp.float32) * D_MODEL ** -0.5
    b_forget = jax.random.uniform(ks[4], (DEPTH, N_HEADS_FOX), jnp.float32, minval=1.0, maxval=6.0)
    w_o_fox = jax.random.normal(ks[5], (DEPTH, WIDTH_FOX, D_MODEL), jnp.float32) * WIDTH_FOX ** -0.5
    w_o_sb = jax.random.normal(ks[6], (DEPTH, WIDTH_SB, D_MODEL), jnp.float32) * WIDTH_SB ** -0.5
    w_out = jax.random.normal(ks[7], (DEPTH, D_MODEL, D_MODEL), jnp.float32) * D_MODEL ** -0.5
    w_up = jax.random.normal(ks[8], (DEPTH, D_MODEL, 2 * D_FF), jnp.float32) * D_MODEL ** -0.5
    conv_w = jax.random.normal(ks[9], (DEPTH, CONV_WIDTH, 2 * D_FF), jnp.float32) * CONV_WIDTH ** -0.5
    conv_b = 0.02 * jax.random.normal(ks[10], (DEPTH, 2 * D_FF), jnp.float32)
    w_down = jax.random.normal(ks[11], (DEPTH, D_FF, D_MODEL), jnp.float32) * D_FF ** -0.5
    return {"x": x, "meta_tokens": meta_tokens, "norm_gains": norm_gains, "w_in": w_in,
            "b_forget": b_forget, "w_o_fox": w_o_fox, "w_o_sb": w_o_sb, "w_out": w_out,
            "w_up": w_up, "conv_w": conv_w, "conv_b": conv_b, "w_down": w_down}

def first_block(x, meta_tokens, norm_gains, w_in, b_forget, w_o_fox, w_o_sb, w_out,
              w_up, conv_w, conv_b, w_down):
    batch = x.shape[0]
    meta = jnp.broadcast_to(meta_tokens[None].astype(x.dtype), (batch, N_META, D_MODEL))
    h = jnp.concatenate([meta, x], axis=1)
    for layer in range(DEPTH):
        xn = rms_norm(h, norm_gains[layer, 0])
        proj = xn @ w_in[layer]
        q_a, k_a, v_a, f_a, q_b, k_b, v_b, g_a, g_b = jnp.split(proj, SPLIT_POINTS, axis=-1)
        log_f = jax.nn.log_sigmoid((f_a + b_forget[layer]).astype(jnp.float32))
        o_a = forgetting_attention(_split_heads(q_a, N_HEADS_FOX), _split_heads(k_a, N_HEADS_FOX),
                                   _split_heads(v_a, N_HEADS_FOX), log_f.transpose(0, 2, 1))
        o_b = stick_breaking_attention(_split_heads(q_b, N_HEADS_SB), _split_heads(k_b, N_HEADS_SB),
                                       _split_heads(v_b, N_HEADS_SB))
        y_a = _merge_heads(o_a) @ w_o_fox[layer]
        y_b = _merge_heads(o_b) @ w_o_sb[layer]
        mixed = (jax.nn.sigmoid(g_a) * y_a + jax.nn.sigmoid(g_b) * y_b) @ w_out[layer]
        h = h + rms_norm(mixed, norm_gains[layer, 1])
        xn = rms_norm(h, norm_gains[layer, 2])
        u = causal_depthwise_conv(xn @ w_up[layer], conv_w[layer], conv_b[layer])
        u_gate, u_val = jnp.split(u, 2, axis=-1)
        ffn = (jax.nn.gelu(u_gate, approximate=True) * u_val) @ w_down[layer]
        h = h + rms_norm(ffn, norm_gains[layer, 3])
    return h[:, N_META:]


PLE_DIM = 256
GLA_HEADS = 4
GLA_DK = 128
GLA_DV = 256
GLA_LOWRANK = 16
GLA_TAU = 16.0
GLA_CHUNK = 64
DSA_HEADS = 8
DSA_LATENT = 128
IDX_HEADS = 8
IDX_DIM = 64
TOPK_MAX = 256
REL_BUCKETS = 32
REL_MAX_DIST = 128

IN_SIZES = (
    GLA_HEADS * GLA_DK,
    GLA_HEADS * GLA_DK,
    GLA_HEADS * GLA_DV,
    GLA_HEADS * GLA_DV,
    GLA_LOWRANK,
    DSA_HEADS * DSA_LATENT,
    DSA_LATENT,
    IDX_HEADS * IDX_DIM,
    IDX_DIM,
    IDX_HEADS,
    2 * D_MODEL,
)
D_IN = sum(IN_SIZES)


def rms_norm_2(x, g):
    xf = x.astype(jnp.float32)
    y = xf * lax.rsqrt(jnp.mean(xf * xf, axis=-1, keepdims=True) + EPS)
    return (y * g.astype(jnp.float32)).astype(x.dtype)

def swiglu(x, w_in, w_out):
    gate, up = jnp.split(x @ w_in, 2, axis=-1)
    return (jax.nn.silu(gate) * up) @ w_out

def t5_bucket(dist):
    max_exact = REL_BUCKETS // 2
    d = jnp.maximum(dist, 0)
    ratio = jnp.maximum(d, 1).astype(jnp.float32) / max_exact
    large = max_exact + (jnp.log(ratio) / math.log(REL_MAX_DIST / max_exact)
                         * (REL_BUCKETS - max_exact)).astype(jnp.int32)
    large = jnp.minimum(large, REL_BUCKETS - 1)
    return jnp.where(d < max_exact, d, large)

def gla_chunked(q, k, v, log_a):
    B, H, S, dk = q.shape
    dv = v.shape[-1]
    C = GLA_CHUNK
    N = S // C

    def to_chunks(t):
        return jnp.moveaxis(t.reshape(B, H, N, C, t.shape[-1]), 2, 0)

    causal = jnp.tril(jnp.ones((C, C), dtype=bool))[:, :, None]

    def step(state, inp):
        qi, ki, vi, gi = inp
        b = jnp.cumsum(gi.astype(jnp.float32), axis=2)
        o_inter = jnp.einsum('bhtd,bhde->bhte', qi * jnp.exp(b), state)
        diff = b[:, :, :, None, :] - b[:, :, None, :, :]
        decay = jnp.exp(jnp.where(causal, diff, -jnp.inf))
        scores = jnp.einsum('bhtd,bhsd,bhtsd->bhts', qi, ki, decay)
        o_intra = jnp.einsum('bhts,bhse->bhte', scores, vi)
        b_last = b[:, :, -1:, :]
        k_dec = ki * jnp.exp(b_last - b)
        new_state = (jnp.exp(b_last[:, :, 0, :])[..., None] * state
                     + jnp.einsum('bhsd,bhse->bhde', k_dec, vi))
        return new_state, o_inter + o_intra

    state0 = jnp.zeros((B, H, dk, dv), jnp.float32)
    _, out = lax.scan(step, state0, (to_chunks(q), to_chunks(k), to_chunks(v), to_chunks(log_a)))
    return jnp.moveaxis(out, 0, 2).reshape(B, H, S, dv)

def dsa_attention(q, c_kv, q_idx, k_idx, w_idx, rel_bias):
    B, S, H, dc = q.shape
    top_k = min(TOPK_MAX, S // 4)
    nb = S // Q_BLOCK
    key_pos = jnp.arange(S, dtype=jnp.int32)
    bidx = jnp.arange(B)[:, None, None]

    def blocks(t):
        return jnp.moveaxis(t.reshape(B, nb, Q_BLOCK, *t.shape[2:]), 1, 0)

    def one_block(args):
        blk, qb, qib, wb = args
        q_pos = blk * Q_BLOCK + jnp.arange(Q_BLOCK, dtype=jnp.int32)
        dots = jnp.einsum('bthd,bsd->bths', qib, k_idx).astype(jnp.float32) * (IDX_DIM ** -0.5)
        w = wb.astype(jnp.float32) * (IDX_HEADS ** -0.5)
        score = jnp.einsum('bths,bth->bts', jax.nn.relu(dots), w)
        causal = key_pos[None, :] <= q_pos[:, None]
        score = jnp.where(causal[None], score, -jnp.inf)
        _, sel = lax.top_k(score, top_k)
        valid = sel <= q_pos[None, :, None]
        kv_sel = c_kv[bidx, sel]
        bias = rel_bias[t5_bucket(q_pos[None, :, None] - sel)]
        logits = (jnp.einsum('bthc,btkc->bthk', qb, kv_sel).astype(jnp.float32) * (dc ** -0.5)
                  + jnp.moveaxis(bias, -1, 2).astype(jnp.float32))
        logits = jnp.where(valid[:, :, None, :], logits, -jnp.inf)
        probs = jax.nn.softmax(logits, axis=-1)
        return jnp.einsum('bthk,btkc->bthc', probs.astype(kv_sel.dtype), kv_sel)

    out = lax.map(one_block, (jnp.arange(nb, dtype=jnp.int32), blocks(q), blocks(q_idx), blocks(w_idx)))
    return jnp.moveaxis(out, 0, 1).reshape(B, S, H, dc)

def hybrid_mixer(u, w_in, alpha_w, alpha_b, gla_norm_g, gla_w_out, ckv_g, dsa_w_out, rel_bias, w_out):
    B, S, _ = u.shape
    split_pts = np.cumsum(IN_SIZES)[:-1].tolist()
    (gq, gk, gv, gr, ga, dq, dkv, iq, ik, iw, gates) = jnp.split(u @ w_in, split_pts, axis=-1)

    def heads(t, n):
        return t.reshape(B, S, n, -1).transpose(0, 2, 1, 3)

    log_a = jax.nn.log_sigmoid((ga @ alpha_w + alpha_b).astype(jnp.float32)) / GLA_TAU
    o = gla_chunked(heads(gq, GLA_HEADS) * (GLA_DK ** -0.5), heads(gk, GLA_HEADS),
                    heads(gv, GLA_HEADS), heads(log_a, GLA_HEADS))
    o = rms_norm_2(o, gla_norm_g.reshape(GLA_HEADS, 1, GLA_DV)).astype(u.dtype)
    o = o.transpose(0, 2, 1, 3).reshape(B, S, GLA_HEADS * GLA_DV) * jax.nn.silu(gr)
    y_gla = o @ gla_w_out

    c_kv = rms_norm_2(dkv, ckv_g)
    od = dsa_attention(dq.reshape(B, S, DSA_HEADS, DSA_LATENT), c_kv,
                       iq.reshape(B, S, IDX_HEADS, IDX_DIM), ik, iw, rel_bias)
    y_dsa = od.reshape(B, S, DSA_HEADS * DSA_LATENT) @ dsa_w_out

    g_gla, g_dsa = jnp.split(jax.nn.sigmoid(gates), 2, axis=-1)
    return (g_gla * y_gla + g_dsa * y_dsa) @ w_out

def second_inputs(seed: int = 0) -> dict:
    key = jax.random.key(seed)
    ks = jax.random.split(key, 24)
    L, D, F = DEPTH, D_MODEL, D_FF

    def dense(k, shape, fan_in):
        return jax.random.normal(k, shape, jnp.float32) * (fan_in ** -0.5)

    def gain(k, shape):
        return 1.0 + 0.05 * jax.random.normal(k, shape, jnp.float32)

    return {
        "x": jax.random.normal(ks[0], (BATCH, SEQ, D), jnp.float32),
        "p": jax.random.normal(ks[1], (DEPTH, BATCH, SEQ, PLE_DIM), jnp.float32),
        "ffn1_norm": gain(ks[2], (L, D)),
        "ffn1_w_in": dense(ks[3], (L, D, 2 * F), D),
        "ffn1_w_out": dense(ks[4], (L, F, D), F),
        "mix_norm": gain(ks[5], (L, D)),
        "mix_w_in": dense(ks[6], (L, D, D_IN), D),
        "gla_alpha_w": dense(ks[7], (L, GLA_LOWRANK, GLA_HEADS * GLA_DK), GLA_LOWRANK),
        "gla_alpha_b": 0.1 * jax.random.normal(ks[8], (L, GLA_HEADS * GLA_DK), jnp.float32),
        "gla_out_norm": gain(ks[9], (L, GLA_HEADS * GLA_DV)),
        "gla_w_out": dense(ks[10], (L, GLA_HEADS * GLA_DV, D), GLA_HEADS * GLA_DV),
        "ckv_norm": gain(ks[11], (L, DSA_LATENT)),
        "dsa_w_out": dense(ks[12], (L, DSA_HEADS * DSA_LATENT, D), DSA_HEADS * DSA_LATENT),
        "rel_bias": 0.5 * jax.random.normal(ks[13], (REL_BUCKETS, DSA_HEADS), jnp.float32),
        "mix_w_out": dense(ks[14], (L, D, D), D),
        "ffn2_norm": gain(ks[15], (L, D)),
        "ffn2_w_in": dense(ks[16], (L, D, 2 * F), D),
        "ffn2_w_out": dense(ks[17], (L, F, D), F),
        "ple_norm": gain(ks[18], (L, D)),
        "ple_w_gate": dense(ks[19], (L, D, D), D),
        "ple_w_proj": dense(ks[20], (L, PLE_DIM, D), PLE_DIM),
        "final_norm": gain(ks[21], (D,)),
    }

def second_block(x, p, ffn1_norm, ffn1_w_in, ffn1_w_out, mix_norm, mix_w_in, gla_alpha_w, gla_alpha_b,
              gla_out_norm, gla_w_out, ckv_norm, dsa_w_out, rel_bias, mix_w_out, ffn2_norm, ffn2_w_in,
              ffn2_w_out, ple_norm, ple_w_gate, ple_w_proj, final_norm):
    h = x
    for i in range(DEPTH):
        h = h + 0.5 * swiglu(rms_norm_2(h, ffn1_norm[i]), ffn1_w_in[i], ffn1_w_out[i])
        h = h + hybrid_mixer(rms_norm_2(h, mix_norm[i]), mix_w_in[i], gla_alpha_w[i], gla_alpha_b[i],
                             gla_out_norm[i], gla_w_out[i], ckv_norm[i], dsa_w_out[i], rel_bias,
                             mix_w_out[i])
        h = h + 0.5 * swiglu(rms_norm_2(h, ffn2_norm[i]), ffn2_w_in[i], ffn2_w_out[i])
        hn = rms_norm_2(h, ple_norm[i])
        h = h + jax.nn.sigmoid(hn @ ple_w_gate[i]) * (p[i] @ ple_w_proj[i])
    return rms_norm_2(h, final_norm)


def setup_inputs(seed=0):
    out = dict(first_inputs(seed))
    for name, value in second_inputs(seed + 1).items():
        if name != "x":
            out[name + "_2"] = value
    return out


def reference(
    x, meta_tokens, norm_gains, w_in, b_forget, w_o_fox, w_o_sb, w_out, w_up, conv_w, conv_b,
    w_down, p_2, ffn1_norm_2, ffn1_w_in_2, ffn1_w_out_2, mix_norm_2, mix_w_in_2, gla_alpha_w_2,
    gla_alpha_b_2, gla_out_norm_2, gla_w_out_2, ckv_norm_2, dsa_w_out_2, rel_bias_2,
    mix_w_out_2, ffn2_norm_2, ffn2_w_in_2, ffn2_w_out_2, ple_norm_2, ple_w_gate_2, ple_w_proj_2,
    final_norm_2,
):
    x = first_block(
        x, meta_tokens, norm_gains, w_in, b_forget, w_o_fox, w_o_sb, w_out, w_up, conv_w,
        conv_b, w_down,
    )
    return second_block(
        x, p_2, ffn1_norm_2, ffn1_w_in_2, ffn1_w_out_2, mix_norm_2, mix_w_in_2, gla_alpha_w_2,
        gla_alpha_b_2, gla_out_norm_2, gla_w_out_2, ckv_norm_2, dsa_w_out_2, rel_bias_2,
        mix_w_out_2, ffn2_norm_2, ffn2_w_in_2, ffn2_w_out_2, ple_norm_2, ple_w_gate_2,
        ple_w_proj_2, final_norm_2,
    )


_drawn_inputs = setup_inputs


def setup_inputs(seed=0):
    import zlib

    import numpy as np

    out = dict(_drawn_inputs(seed))
    spreads = {}
    factors = {'conv_b': 3.174,
     'ffn1_norm_2': 4.269,
     'mix_norm_2': 2.676,
     'gla_alpha_b_2': 7.122,
     'gla_out_norm_2': 6.235,
     'ckv_norm_2': 8.0,
     'ffn2_norm_2': 5.075,
     'ple_norm_2': 8.0}
    for name, (base, spread) in spreads.items():
        noise = np.random.default_rng([zlib.crc32(name.encode()), seed]).standard_normal(out[name].shape)
        drawn = base * np.exp(spread * noise) if base else spread * noise
        out[name] = __import__('jax').numpy.asarray(drawn.astype(out[name].dtype))
    for name, factor in factors.items():
        out[name] = (out[name] * factor).astype(out[name].dtype)
    return out
```

```python
import math
from contextlib import ExitStack

import numpy as np

import concourse.bass as bass
from concourse import mybir

F32 = mybir.dt.float32
F32R = mybir.dt.float32r
I32 = mybir.dt.int32
ALU = mybir.AluOpType
ACT = mybir.ActivationFunctionType
AX = mybir.AxisListType

P = 128
D = 1024
KC = D // P
META = 16
SEQ = 512
T1 = SEQ + META
HALF = T1 // 2
BANK = 512
FF = 2816
FC = FF // P
EPS = 1e-6
NEG = -1e30
UT = 16

U_PROJ = 0
U_F = U_PROJ + 6
U_QKVB = U_F + 1
U_GATES = U_QKVB + 6
U_O = U_GATES + 8
U_WOUT = U_O + 4
U_UP = U_WOUT + 4
U_DOWN = U_UP + FC
U_END1 = U_DOWN + FC // 2
U_F1I = U_END1
U_F1O = U_F1I + FC
U_GQK = U_F1O + FC // 2
U_GV = U_GQK + 4
U_GR = U_GV + 4
U_SPC = U_GR + 4
U_MG1 = U_SPC + 2
U_GLAO = U_MG1 + 4
U_DQ = U_GLAO + 4
U_IQ = U_DQ + 4
U_MG2 = U_IQ + 2
U_DSAO = U_MG2 + 4
U_MIXO = U_DSAO + 4
U_F2I = U_MIXO + 4
U_F2O = U_F2I + FC
U_PLEG = U_F2O + FC // 2
U_PLEP = U_PLEG + 4
U_END = U_PLEP + 1

(G_PRE, G_MIX, G_FFN, G_POST, G_F1, G_MIX2, G_GLA, G_F2, G_PLE, G_FIN) = range(0, 80, 8)
C_CKV = 80
C_AB = 81
C_CW = 85
C_CB = C_CW + 3 * 2 * FC
C_BF = C_CB + 2 * FC
C_N = C_BF + 1


class Count:

    def __init__(self, eng, sem):
        self.eng, self.sem, self.n, self.turn = eng, sem, 0, 0

    def up(self, ins):
        ins.then_inc(self.sem, 1)
        self.n += 1
        return self.n

    def wait(self, value=None):
        self.eng.wait_ge(self.sem, self.turn + (self.n if value is None else value))

    def enter(self, turns_done, per_turn):
        self.first, self.per = self.n, per_turn
        self.turn = turns_done * per_turn

    def leave(self, turns):
        assert self.n == self.first + self.per
        self.n, self.turn = self.first + self.per * turns, 0


def std_units(w, starts):
    tiles = w.reshape(KC, P, w.shape[1])
    cut = [tiles[:, :, s:s + P] for s in starts]
    both = [np.stack(cut[i:i + 2]) for i in range(0, len(cut), 2)]
    return [np.ascontiguousarray(b.transpose(2, 0, 1, 3)).reshape(1, P, UT * P) for b in both]


def down_units(w):
    v = w.reshape(w.shape[0] // (2 * P), 2, P, D).transpose(0, 2, 1, 3)
    return [np.ascontiguousarray(v).reshape(-1, P, UT * P)]


def run_of(start, n):
    return [start + P * i for i in range(n)]


def pairs_up(w):
    starts = []
    for i in range(0, FC, 2):
        starts += [P * i, P * i + P, FF + P * i, FF + P * i + P]
    return std_units(w, starts)


def columns(v):
    return np.asarray(v).reshape(-1, P).T


def layout(v):
    w = v["w_in"][0]
    units = std_units(w, run_of(0, 12)) + std_units(w, [1536, 1536])
    units += std_units(w, run_of(1544, 28))
    units += std_units(np.concatenate([v["w_o_fox"][0], v["w_o_sb"][0]]), run_of(0, 8))
    units += std_units(v["w_out"][0], run_of(0, 8))
    units += pairs_up(v["w_up"][0]) + down_units(v["w_down"][0])
    units += pairs_up(v["ffn1_w_in_2"][0]) + down_units(v["ffn1_w_out_2"][0])
    w = v["mix_w_in_2"][0]
    units += std_units(w, run_of(0, 24))
    units += std_units(w, [3072, 4112, 4752, 4688])
    units += std_units(w, run_of(4824, 8))
    units += std_units(v["gla_w_out_2"][0], run_of(0, 8))
    units += std_units(w, run_of(3088, 8)) + std_units(w, run_of(4240, 4))
    units += std_units(w, run_of(5848, 8))
    units += std_units(v["dsa_w_out_2"][0], run_of(0, 8))
    units += std_units(v["mix_w_out_2"][0], run_of(0, 8))
    units += pairs_up(v["ffn2_w_in_2"][0]) + down_units(v["ffn2_w_out_2"][0])
    units += std_units(v["ple_w_gate_2"][0], run_of(0, 8)) + down_units(v["ple_w_proj_2"][0])
    stream = np.concatenate(units)
    assert stream.shape[0] == U_END
    if U_END % 2:
        stream = np.concatenate([stream, np.zeros((1, P, UT * P), np.float32)])
    g = v["norm_gains"][0]
    bf = np.zeros((P, 1), np.float32)
    bf[0:8, 0] = v["b_forget"][0]
    gains = [g[0], g[1], g[2], g[3], v["ffn1_norm_2"][0], v["mix_norm_2"][0], v["gla_out_norm_2"][0],
             v["ffn2_norm_2"][0], v["ple_norm_2"][0], v["final_norm_2"]]
    cvec = np.concatenate([columns(a) for a in gains] + [columns(v["ckv_norm_2"][0]), columns(v["gla_alpha_b_2"][0])]
                          + [columns(v["conv_w"][0][t]) for t in range(3)] + [columns(v["conv_b"][0]), bf], axis=1)
    ident, masks, gmask, onehot = shape_constants()
    return {"wstream": stream, "x": v["x"], "meta": v["meta_tokens"], "cvec": cvec,
            "alpha_w": v["gla_alpha_w_2"][0], "rel_bias": v["rel_bias_2"], "p2": v["p_2"],
            "ident_c": ident, "masks_c": masks, "gmask_c": gmask, "onehot_c": onehot}


def build(nc, wstream, x, meta, cvec, alpha_w, rel_bias, p2, ident_c, masks_c, gmask_c, onehot_c, out):
    n_units = wstream.shape[0]
    with ExitStack() as ctx:
        signals = {}

        def sig(name):
            if name not in signals:
                signals[name] = ctx.enter_context(nc.semaphore(name))
            return signals[name]

        place = {"at": 16512}

        def at(name, shape, dt=F32, offset=None):
            size = int(np.prod(shape[1:])) * 4
            if offset is None:
                offset = place["at"]
                place["at"] += (size + 31) // 32 * 32
            return nc.alloc_sbuf_tensor_at(name, list(shape), dt, offset=offset)

        raw = [at(f"raw{b}", [P, UT * P]) for b in range(2)]
        whi = [at(f"whi{b}", [P, UT * P], F32R) for b in range(2)]
        wlo = [at(f"wlo{b}", [P, UT * P], F32R) for b in range(2)]
        h = at("h", [P, KC, T1])
        x_at = place["at"]
        xhi = at("xhi", [P, KC, T1], F32R)
        xlo = at("xlo", [P, KC, T1], F32R)
        arena = place["at"]
        place["at"] += 2 * FC * SEQ * 4
        ident = at("ident", [P, P])
        masks_at = place["at"]
        masks = at("masks", [P, 3 * P + 32])
        cv = at("cv", [P, C_N])
        small = at("small", [P, 8])
        per = at("per", [P, 64])
        temp = place["at"]
        room = 229368 - temp

        ntri = masks[:, 0:P]
        madd = masks[:, P:2 * P]
        madds = masks[:, 2 * P:3 * P]
        madds_tail = masks[:, 3 * P:3 * P + META]
        keep_tail = masks[:, 3 * P + META:3 * P + 2 * META]
        one_col = small[:, 0:1]
        neg_col = small[:, 1:2]
        eps_col = small[:, 3:4]

        ps = ctx.enter_context(nc.psum_tensor("ps", [P, 8 * BANK], F32))
        regions = ps[:].rearrange("p (r c) -> p r c", c=2 * BANK)
        LO = BANK - HALF

        def chunks1(b, n=2):
            return regions[:, 2 * b:2 * b + n, LO:LO + T1]

        def bank(i, n=1):
            return ps[:, i * BANK:(i + n) * BANK]

        xin = at("xin", [P, 4, D], offset=arena)
        xmeta = at("xmeta", [META, D], offset=arena + 4 * 4 * D)
        qkf = at("qkf", [P, 8, T1], offset=arena)
        qkb = at("qkb", [P, 8, T1], offset=arena + 32 * T1)
        v_at = arena + 64 * T1
        vf = at("vf", [P, 4, BANK], offset=v_at)
        vf_tail = at("vf_tail", [META, BANK], offset=v_at + 8192)
        vb = at("vb", [P, 5, BANK], offset=v_at + 10240)
        gates = at("gates", [P, 16, T1], offset=v_at + 20480)
        fz, fa, fl, fm = [at(f"forget{i}", [8, T1], offset=v_at + 20480 + 4 * T1 * i) for i in range(4)]
        vfm = at("vfm", [P, 4, T1], offset=temp)
        vbm = at("vbm", [P, 4, T1], offset=temp + 16 * T1)
        negc = at("negc", [8, T1], offset=temp + 32 * T1)
        fox_p = [at(f"fox_p{i}", [P, T1], offset=temp + 4 * T1 * i) for i in range(3)]
        fox_pt = [at(f"fox_pt{i}", [P, BANK], offset=temp + 12 * T1 + 2048 * i) for i in range(2)]
        fox_c = at("fox_c", [P, 3, 40], offset=temp + 12 * T1 + 4096)
        ncb = [at(f"ncb{i}", [P, 4, T1], offset=x_at + 16 * T1 + 32 * T1 * i) for i in range(2)]
        sb_l = [at(f"sb_l{i}", [P, BANK], offset=temp + 2048 * i) for i in range(2)]
        sb_p = [at(f"sb_p{i}", [P, BANK], offset=temp + 4096 + 2048 * i) for i in range(2)]
        sb_a = [at(f"sb_a{i}", [P, BANK], offset=temp + 8192 + 2048 * i) for i in range(2)]
        keep = at("keep", [P, P], offset=temp + 12288)
        yhi = at("yhi", [P, KC, T1], F32R, offset=arena)
        ylo = at("ylo", [P, KC, T1], F32R, offset=arena + 32 * T1)
        assert 64 * T1 <= 64 * T1 + 20480
        yt = [at(f"yt{i}", [P, T1], offset=temp + 4 * T1 * i) for i in range(4)]
        mix = at("mix", [P, KC, T1], offset=x_at)
        sq = [at(f"sq{i}", [P, T1], offset=temp + 4 * T1 * i) for i in range(2)]
        nt = [at(f"nt{i}", [P, T1], offset=temp + 4 * T1 * (2 + i)) for i in range(3)]
        root = [at(f"root{i}", [P, T1], offset=temp + 4 * T1 * (5 + i)) for i in range(4)]
        hhi = at("hhi", [P, FC, SEQ], F32R, offset=arena)
        hlo = at("hlo", [P, FC, SEQ], F32R, offset=arena + 4 * FC * SEQ)
        cg = at("cg", [P, 2, SEQ], offset=temp)
        gact = at("gact", [P, 2, SEQ], offset=temp + 4096)
        cvl = at("cvl", [P, 2, SEQ], offset=temp + 8192)
        fin = at("fin", [P, KC, SEQ], offset=arena)
        outb = [at(f"outb{i}", [P, D], offset=arena + 4 * KC * SEQ + 4096 * i) for i in range(2)]
        assert room >= 19008, room
        gqk = at("gqk", [P, 8, SEQ], offset=arena)
        gvt = at("gvt", [P, 4, D], offset=arena + 16384)
        gvf = at("gvf", [P, 8, SEQ], offset=arena + 32768)
        gout = at("gout", [P, 8, SEQ], offset=arena + 32768)
        grs = at("grs", [P, 8, SEQ], offset=arena + 49152)
        nbt = at("nbt", [P, 4, SEQ], offset=arena + 65536)
        bucket = at("bucket", [32, 640], offset=arena + 65536)
        relb = at("relb", [32, 8], offset=arena + 68096)
        brow = at("brow", [8, 640], offset=arena + 68608)
        ckvf = at("ckvf", [P, SEQ], offset=arena + 73728)
        ckvt = at("ckvt", [P, 4, P], offset=arena + 75776)
        dkvf = at("dkvf", [P, SEQ], offset=arena + 77824)
        ikd = at("ikd", [P, SEQ], offset=arena + 79872)
        gaf = at("gaf", [META, SEQ], offset=arena + 81920)
        iwf = at("iwf", [P, SEQ], offset=arena + 83968)
        aw = at("aw", [META, SEQ], offset=arena + 86016)
        kx = at("kx", [P, 6, P], offset=arena + 86016)
        kx2 = at("kx2", [P, 2, P], offset=arena + 89088)
        ax = at("ax", [P, 4, SEQ], offset=temp)
        al = at("al", [P, 4, SEQ], offset=temp + 8192)
        restart = at("restart", [P, SEQ], offset=temp + 16384)
        gf = [at(f"gf{i}", [P, SEQ], offset=temp + 2048 * i) for i in range(3)]
        sd = [at(f"sd{i}", [P, 4, P], offset=temp + 6144 + 5120 * i) for i in range(2)]
        sx = [at(f"sx{i}", [P, 6, P], offset=temp + 8192 + 5120 * i) for i in range(2)]
        ga_m = at("ga_m", [P, 4 * P], mybir.dt.int8, offset=masks_at)
        gb_m = at("gb_m", [P, 3 * P], mybir.dt.int8, offset=masks_at + 1024)
        gyh = at("gyh", [P, 8, SEQ], F32R, offset=arena)
        gyl = at("gyl", [P, 8, SEQ], F32R, offset=arena + 16384)
        g1 = at("g1", [P, 8, SEQ], offset=arena + 32768)
        dq = at("dq", [P, 8, SEQ], offset=arena)
        g2 = at("g2", [P, 8, SEQ], offset=arena + 16384)
        iqf = at("iqf", [P, 4, SEQ], offset=arena + 49152)
        bias = at("bias", [P, 8, SEQ], offset=arena + 57344)
        mj = at("mj", [P, 10 * P], offset=arena + 81920)
        mj_at = [0, P, 3 * P, 6 * P]
        acc = [at(f"acc{i}", [P, SEQ], offset=temp + 2048 * i) for i in range(2)]
        rl = [at(f"rl{i}", [P, SEQ], offset=temp + 4096 + 2048 * i) for i in range(2)]
        dl = [at(f"dl{i}", [P, SEQ], offset=temp + 2048 * i) for i in range(3)]
        dpt = [at(f"dpt{i}", [P, SEQ], offset=temp + 6144 + 2048 * i) for i in range(2)]
        dst_ = at("dst", [P, 3, 32], offset=temp + 10240)
        myh = at("myh", [P, 8, SEQ], F32R, offset=arena + 49152)
        myl = at("myl", [P, 8, SEQ], F32R, offset=arena + 65536)
        dt_ = [at(f"dt{i}", [P, 2, SEQ], offset=temp + 4096 * i) for i in range(2)]
        pin = at("pin", [P, 4, 256], offset=arena + 16384)
        phi = at("phi", [P, 2, SEQ], F32R, offset=arena + 20480)
        plo = at("plo", [P, 2, SEQ], F32R, offset=arena + 24576)
        sgp = at("sgp", [P, 8, SEQ], offset=arena + 32768)
        iwt = per[:, 0:32]
        m8 = per[:, 32:40]
        ex = per[:, 40:42]
        fin_at = at("fin2", [P, KC, SEQ], offset=arena + 65536 - 16384)
        scratch = nc.dram_tensor("bias_rows", (8, 640), F32)
        GI = [(hd, kind) for hd in range(4) for kind in range(9)]
        NG = len(GI)
        DI = [(j, hd) for j in range(4) for hd in range(8)]
        ND = len(DI)

        def cross_of(hd):
            return 9 * hd + 8

        def diag_seen(q):
            return sum(1 for x in range(q + 1) if GI[x][1] < 8)


        ITEMS = [(head, i) for head in range(8) for i in range(5)]
        NI = len(ITEMS)

        def item(n):
            head, i = ITEMS[n]
            r = 64 * (head % 2)
            if i < 4:
                return head, slice(r, r + 64), head // 2, i, P * i, P, P * (i + 1)
            return head, slice(r, r + 64), head // 2, i, SEQ, META, T1

        def pair(ap):
            return ap.rearrange("p (c n) -> p c n", c=2)

        def norm_places(n):
            T, at_ = NORMS[n]
            if T == T1:
                scale = regions[:, at_, LO:LO + T1]
                return scale, [slice(0, HALF), slice(HALF, T1)]
            return bank(at_), [slice(0, SEQ)]

        up0, f1, g2_, pl = U_UP % 2, U_F1I % 2, U_GQK % 2, U_PLEG % 2
        NORMS = [(T1, 2), (T1, 2 * up0), (T1, 2 * (1 - up0)), (SEQ, 2 * (1 - f1)), (SEQ, 2 * (1 - f1) + 1),
                 (SEQ, 2 * (1 - g2_)), (SEQ, 4), (SEQ, 2 * (1 - pl)), (SEQ, 4)]

        block = ctx.enter_context(nc.Block())

        @block.sync
        def _(sp):
            sp.dma_start(ident[:], ident_c).then_inc(sig("ident_in"), 16)
            sp.dma_start(xmeta[:], meta).then_inc(sig("x_in"), 16)
            for j in range(4):
                sp.dma_start(xin[:, j, :], x[0, j * P:(j + 1) * P, :]).then_inc(sig("x_in"), 16)
            sp.dma_start(raw[0][:], wstream[0]).then_inc(sig("raw_ready0"), 16)
            sp.dma_start(cv[:], cvec).then_inc(sig("const_in"), 16)
            sp.dma_start(raw[1][:], wstream[1]).then_inc(sig("raw_ready1"), 16)
            sp.dma_start(masks[:], masks_c[:, 0:3 * P + 32]).then_inc(sig("const_in"), 16)
            with sp.Fori(1, n_units // 2) as i:
                for b in range(2):
                    sp.wait_ge(sig("lo_done"), i * 2 + (b - 1))
                    sp.dma_start(raw[b][:], wstream[bass.ds(i * 2 + b, 1)].rearrange("u p n -> (u p) n")
                                 ).then_inc(sig(f"raw_ready{b}"), 16)
            for j in range(4):
                sp.wait_ge(sig("out_copied"), j + 1)
                sp.dma_start(out[0, j * P:(j + 1) * P, :], outb[j % 2][:]).then_inc(sig(f"stored{j % 2}"), 16)
            for b in range(2):
                sp.wait_ge(sig(f"stored{b}"), 32)

        @block.gpsimd
        def _(pool):
            with pool.Fori(0, n_units // 2) as i:
                for b in range(2):
                    pool.wait_ge(sig("hi_done"), i * 2 + (b + 1))
                    nc.gpsimd.tensor_tensor(wlo[b][:], raw[b][:], whi[b][:].bitcast(F32), ALU.subtract
                                            ).then_inc(sig("lo_done"), 1)

        @block.scalar
        def _(act):
            step = Count(act, sig("act_step"))
            norms, roots = [0], [0]

            def weights_hi(b, pair, first=False):
                act.wait_ge(sig(f"raw_ready{b}"), pair * 16 + 16)
                if not first:
                    act.wait_ge(sig("unit_done"), pair * 2 + (b - 1))
                nc.scalar.copy(whi[b][:], raw[b][:]).then_inc(sig("hi_done"), 1)

            def hi_of(u):
                if u < n_units:
                    weights_hi(u % 2, u // 2, u < 2)

            def rsqrt_of(total, share):
                n = roots[0]
                roots[0] += 1
                y = root[n % 2][:, 0:total.shape[-1]]
                nc.scalar.activation(y, total, ACT.Ln, bias=eps_col, scale=share).then_inc(sig("log_done"), 1)
                act.wait_ge(sig("log_done"), n + 1)
                nc.scalar.activation(y, y, ACT.Exp, scale=-0.5).then_inc(sig("root_done"), 1)

            def squares(view, T, wait_source):
                n = norms[0]
                norms[0] += 1
                if n not in (2, 4):
                    nc.scalar.preload_act_table_set("natural_log_exp_and_others")
                for k in range(KC):
                    wait_source(k)
                    if 8 * n + k >= 2:
                        act.wait_ge(sig("sq_used"), 8 * n + k - 1)
                    nc.scalar.activation(sq[k % 2][:, 0:T], view(k), ACT.Square).then_inc(sig("sq_done"), 1)
                act.wait_ge(sig("sq_used"), 8 * n + 8)
                total, _ = norm_places(n)
                rsqrt_of(total, 1.0 / D)

            def split_x(base, T):
                for k in range(KC):
                    act.wait_ge(sig("nt_ready"), base + k + 1)
                    nc.scalar.copy(xhi[:, k, 0:T], nt[k % 3][:, 0:T]).then_inc(sig("xhi_ready"), 1)

            def out_hi(n, o_base, chunk0):
                head, rows, c, i, t0, tw, _ = item(n)
                act.wait_ge(sig("o_done"), o_base + n + 1)
                nc.scalar.copy(xhi[rows, chunk0 + c, t0:t0 + tw], bank(6 + n % 2)[rows, 0:tw]
                               ).then_inc(sig("o_hi"), 1)

            hi_of(0)
            hi_of(1)
            act.wait_ge(sig("const_in"), 32)
            squares(lambda k: h[:, k, :], T1, lambda k: act.wait_ge(sig("h_ready"), k + 1))
            split_x(0, T1)
            for u in range(U_PROJ, U_O):
                hi_of(u + 2)
                if u == U_F + 1:
                    nc.scalar.preload_act_table_set("natural_log_exp_and_others")
                    act.wait_ge(sig("f_z"), 1)
                    nc.scalar.activation(fa[:], fa[:], ACT.Exp).then_inc(sig("f_ln"), 1)
                    act.wait_ge(sig("f_ln"), 1)
                    nc.scalar.activation(fl[:], fa[:], ACT.Ln, bias=one_col[0:8]).then_inc(sig("f_ln"), 1)
                if u >= U_GATES:
                    i = u - U_GATES
                    act.wait_ge(sig("c_ready"), 1)
                    act.wait_ge(sig("evac"), u)
                    act.wait_ge(sig("unit_done"), u + 1)
                    nc.scalar.activation(gates[:, 2 * i:2 * i + 2, :], chunks1(u % 2), ACT.Sigmoid
                                         ).then_inc(sig("evac"), 1)
            nc.scalar.preload_act_table_set("natural_log_exp_and_others")
            act.wait_ge(sig("v_ready"), 10)

            for head in range(8):
                act.wait_ge(sig("c_spread"), head + 1)
                nc.scalar.copy(ncb[head // 4][:, head % 4, :], regions[:, head % 4, LO:LO + T1]
                               ).then_inc(sig("c_copied"), 1)
            for n in range(NI + 3):
                if n < NI:
                    head, rows, c, i, t0, tw, w = item(n)
                    base = (n % 2) * 2 * BANK + (BANK if i < 4 else BANK - META)
                    act.wait_ge(sig("fox_max"), n + 1)
                    if n >= 3:
                        act.wait_ge(sig("fox_t"), n - 2)
                    nc.scalar.activation(fox_p[n % 3][0:tw, 0:w], ps[0:tw, base:base + w], ACT.Exp,
                                         bias=fox_c[0:tw, 0, n:n + 1], accum_out=fox_c[0:tw, 1, n:n + 1]
                                         ).then_inc(sig("fox_exp"), 1)
                m = n - 2
                if 0 <= m < NI:
                    i = ITEMS[m][1]
                    act.wait_ge(sig("fox_t"), m + 1)
                    if m >= 2:
                        act.wait_ge(sig("o_done"), m - 1)
                    if i < 4:
                        nc.scalar.copy(fox_pt[m % 2][:, 0:P * (i + 1)], bank(4 + m % 2)[:, 0:P * (i + 1)]
                                       ).then_inc(sig("fox_pt"), 1)
                    else:
                        step.up(nc.scalar.copy(fox_pt[m % 2][:, 0:64], bank(4 + m % 2)[:, 0:64]))
                        nc.scalar.copy(fox_pt[m % 2][0:META, 64:80], bank(4 + m % 2)[0:META, 64:80]
                                       ).then_inc(sig("fox_pt"), 1)
                m = n - 3
                if 0 <= m < NI:
                    out_hi(m, 0, 0)
            for n in range(NI + 2):
                if n < NI:
                    head, rows, c, i, t0, tw, _ = item(n)
                    w = P * (i + 1) if i < 4 else 5 * META
                    act.wait_ge(sig("sb_z"), n + 1)
                    if n >= 2:
                        act.wait_ge(sig("sb_sp"), n - 1)
                    if n == 0:
                        act.wait_ge(sig("fox_t"), NI)
                    logs = sb_l[n % 2][:, 0:w]
                    step.up(nc.scalar.activation(logs, bank(n % 4)[:, 0:w], ACT.Abs))
                    step.wait()
                    step.up(nc.scalar.activation(logs, logs, ACT.Exp, scale=-1.0))
                    step.wait()
                    nc.scalar.activation(logs, logs, ACT.Ln, bias=one_col).then_inc(sig("sb_l"), 1)
                m = n - 1
                if 0 <= m < NI:
                    i = ITEMS[m][1]
                    w = P * (i + 1) if i < 4 else 5 * META
                    act.wait_ge(sig("sb_acc"), m + 1)
                    if m >= 2:
                        act.wait_ge(sig("o_done"), NI + m - 1)
                    nc.scalar.activation(sb_a[m % 2][:, 0:w], bank(m % 4)[:, 0:w], ACT.Exp
                                         ).then_inc(sig("sb_a"), 1)
                m = n - 2
                if 0 <= m < NI:
                    out_hi(m, NI, 4)
            for m in range(8):
                if m % 2 == 1:
                    hi_of(U_O + m // 2 + 2)
                act.wait_ge(sig("y_sum"), m + 1)
                nc.scalar.copy(yhi[:, m, :], yt[2 * (m % 2)][:]).then_inc(sig("y_hi"), 1)
            for u in range(U_WOUT, U_UP):
                hi_of(u + 2)
            squares(lambda k: mix[:, k, :], T1, lambda k: act.wait_ge(sig("mix_ready"), k // 2 + 1))
            squares(lambda k: h[:, k, :], T1, lambda k: act.wait_ge(sig("res_ready"), k + 1))
            split_x(8, T1)

            def hidden_act(i, first, unit0, done, func):
                b = unit0 % 2
                weights_hi(b, i + ((unit0 - b) // 2 + 1))
                act.wait_ge(sig("gate_ready"), i + (done + 1))
                if not first:
                    act.wait_ge(sig("prod"), i + done)
                return func(i)

            def conv_gate(i):
                nc.scalar.activation(gact[:], cg[:], ACT.Gelu_apprx_tanh).then_inc(sig("gate_act"), 1)

            def hidden_hi(i, unit0, done):
                b = (unit0 + 1) % 2
                weights_hi(b, i + ((unit0 + 1 - b) // 2 + 1))
                act.wait_ge(sig("prod"), i + (done + 1))
                nc.scalar.copy(hhi[:, bass.ds(i * 2, 2), :], cvl[:]).then_inc(sig("hid_hi"), 1)

            hidden_act(0, True, U_UP, 0, conv_gate)
            hidden_hi(0, U_UP, 0)
            with act.Fori(1, FC // 2) as i:
                hidden_act(i, False, U_UP, 0, conv_gate)
                hidden_hi(i, U_UP, 0)
            for u in range(U_DOWN, U_END1):
                hi_of(u + 2)
            squares(lambda k: mix[:, k, 0:SEQ], SEQ, lambda k: act.wait_ge(sig("down_evac"), k + 1))

            hview = lambda k: h[:, k, META:T1]
            squares(hview, SEQ, lambda k: act.wait_ge(sig("res_ready"), KC + k + 1))
            split_x(2 * KC, SEQ)

            def swiglu(unit0, layer):
                done = layer * (FC // 2)
                b = unit0 % 2

                def silu(i):
                    nc.scalar.activation(gact[:], pair(bank(2 * b, 2)), ACT.Silu).then_inc(sig("gate_act"), 1)

                def one(i, first):
                    weights_hi(b, i + ((unit0 - b) // 2 + 1))
                    act.wait_ge(sig("unit_done"), i * 2 + (unit0 + 1))
                    if not first:
                        act.wait_ge(sig("prod"), i + done)
                    silu(i)
                    hidden_hi(i, unit0, done)

                one(0, True)
                with act.Fori(1, FC // 2) as i:
                    one(i, False)
                for u in range(unit0 + FC, unit0 + FC + FC // 2):
                    hi_of(u + 2)

            swiglu(U_F1I, 1)
            squares(hview, SEQ, lambda k: act.wait_ge(sig("down_evac"), KC + k + 1))
            act.wait_ge(sig("unit_done"), U_GQK)
            act.dma_start(bucket[:], onehot_c).then_inc(sig("aux_in"), 16)
            act.dma_start(relb[:], rel_bias).then_inc(sig("aux_in"), 16)
            act.dma_start(aw[:], alpha_w).then_inc(sig("aux_in"), 16)
            act.dma_start(ga_m[:].bitcast(mybir.dt.int32), gmask_c[:, 0:P]).then_inc(sig("aux_in"), 16)
            act.dma_start(gb_m[:].bitcast(mybir.dt.int32), gmask_c[:, P:7 * P // 4]).then_inc(sig("aux_in"), 16)
            split_x(3 * KC, SEQ)

            def in_order(u):
                act.wait_ge(sig("unit_done"), u + 1)
                if u > U_GQK:
                    act.wait_ge(sig("evac2"), u - U_GQK)

            for u in range(U_GQK, U_MG1):
                hi_of(u + 2)
                if U_GR <= u < U_SPC:
                    i = u - U_GR
                    in_order(u)
                    nc.scalar.activation(grs[:, 2 * i:2 * i + 2, :], pair(bank(2 * (u % 2), 2)), ACT.Silu
                                         ).then_inc(sig("evac2"), 1)
            act.wait_ge(sig("brow_ready"), 1)
            act.dma_start(scratch.ap(), brow[:]).then_inc(sig("brow_out"), 16)
            act.wait_ge(sig("evac2"), U_MG1 - U_GQK)
            nc.scalar.preload_act_table_set("natural_log_exp_and_others")
            nc.scalar.activation(sq[0][:, 0:SEQ], dkvf[:], ACT.Square).then_inc(sig("ckv_sq"), 1)
            act.wait_ge(sig("ckv_sums"), 1)
            rsqrt_of(bank(1), 1.0 / P)
            act.wait_ge(sig("decay_x"), 1)
            act.wait_ge(sig("brow_out"), 16)
            step.up(nc.scalar.activation(al[:], al[:], ACT.Exp))
            step.wait()
            nc.scalar.activation(al[:], al[:], ACT.Ln, bias=one_col).then_inc(sig("decay_ln"), 1)
            for q in range(NG + 4):
                if q < NG:
                    hd, kind = GI[q]
                    if kind:
                        act.wait_ge(sig("g_d"), q - hd)
                    if kind == 8:
                        step.up(nc.scalar.activation(ex[:, 0:1], nbt[:, hd, 2 * P - 1:2 * P], ACT.Exp, scale=-1.0))
                        step.up(nc.scalar.activation(ex[:, 1:2], nbt[:, hd, 3 * P - 1:3 * P], ACT.Exp, scale=-1.0))
                        nc.scalar.activation(kx[:], kx[:], ACT.Exp).then_inc(sig("g_e"), 1)
                    elif kind:
                        nc.scalar.activation(gf[q % 3][:], gf[q % 3][:], ACT.Exp).then_inc(sig("g_e"), 1)
                m = q - 2
                if 0 <= m < NG and GI[m][1] == 8:
                    hd = GI[m][0]
                    act.wait_ge(sig("g_mm"), m + 1)
                    if hd >= 2:
                        act.wait_ge(sig("g_o"), hd - 1)
                    nc.scalar.copy(sx[hd % 2][:], ps[:, 3 * BANK:3 * BANK + 6 * P].rearrange("p (b c) -> p b c", c=P)
                                   ).then_inc(sig("g_x"), 1)
                m = q - 3
                if 0 <= m < NG and GI[m][1] == 8:
                    hd = GI[m][0]
                    act.wait_ge(sig("g_o"), hd + 1)
                    nc.scalar.copy(gout[:, 2 * hd:2 * hd + 2, :], pair(bank(5, 2))).then_inc(sig("g_out"), 1)
            act.wait_ge(sig("g_out"), 4)
            for k in range(8):
                if k >= 2:
                    act.wait_ge(sig("gn_used"), k - 1)
                nc.scalar.activation(sq[k % 2][:, 0:SEQ], gout[:, k, :], ACT.Square).then_inc(sig("gn_sq"), 1)
            for k in range(-2, 8):
                if k >= 0:
                    act.wait_ge(sig("gy_ready"), k + 1)
                    nc.scalar.copy(gyh[:, k, :], nt[k % 3][:, 0:SEQ]).then_inc(sig("gy_hi"), 1)
                hd = k + 2 if k < 0 else k // 2 + 2
                if k < 0 or (k % 2 == 1 and hd < 4):
                    act.wait_ge(sig("gn_used"), 2 * hd + 2)
                    rsqrt_of(bank(4 + hd), 1.0 / 256)
            for u in range(U_MG1, U_DSAO):
                hi_of(u + 2)
                if u < U_GLAO or u >= U_MG2:
                    i, dst = (u - U_MG1, g1) if u < U_GLAO else (u - U_MG2, g2)
                    in_order(u)
                    if u == U_MG1:
                        act.wait_ge(sig("gy_lo"), 8)
                    nc.scalar.activation(dst[:, 2 * i:2 * i + 2, :], pair(bank(2 * (u % 2), 2)), ACT.Sigmoid
                                         ).then_inc(sig("evac2"), 1)
                if u == U_DQ:
                    act.wait_ge(sig("brow_out"), 16)
                    for hd in range(8):
                        rows = bass.AP(tensor=scratch, offset=hd * 640, ap=[[1, P], [1, SEQ]])
                        act.dma_start(bias[:, hd, :], rows).then_inc(sig("bias_in"), 16)
            for m in range(24):
                j, hd = 1 + m // 8, m % 8
                act.wait_ge(sig("ix_dots"), m + 1)
                if m >= 2:
                    act.wait_ge(sig("ix_acc"), m - 1)
                nc.scalar.activation(rl[m % 2][:, 0:P * (j + 1)], bank(m % 4)[:, 0:P * (j + 1)], ACT.Relu
                                     ).then_inc(sig("ix_relu"), 1)
            act.wait_ge(sig("mask_ready"), 3)
            for n in range(ND + 3):
                if n < ND:
                    w = P * (DI[n][0] + 1)
                    act.wait_ge(sig("da_max"), n + 1)
                    nc.scalar.activation(dl[n % 3][:, 0:w], dl[n % 3][:, 0:w], ACT.Exp, bias=dst_[:, 0, n:n + 1],
                                         accum_out=dst_[:, 1, n:n + 1]).then_inc(sig("da_exp"), 1)
                m = n - 2
                if 0 <= m < ND:
                    w = P * (DI[m][0] + 1)
                    act.wait_ge(sig("da_t"), m + 1)
                    if m >= 2:
                        act.wait_ge(sig("da_o"), m - 1)
                    nc.scalar.copy(dpt[m % 2][:, 0:w], bank(4 + m % 2)[:, 0:w]).then_inc(sig("da_pt"), 1)
                m = n - 3
                if 0 <= m < ND:
                    j, hd = DI[m]
                    act.wait_ge(sig("da_o"), m + 1)
                    nc.scalar.copy(xhi[:, hd, j * P:(j + 1) * P], bank(6 + m % 2)[:, 0:P]).then_inc(sig("da_hi"), 1)
            for u in range(U_DSAO, U_F2I):
                hi_of(u + 2)
                if u < U_MIXO:
                    i = u - U_DSAO
                    act.wait_ge(sig("my_ready"), i + 1)
                    nc.scalar.copy(myh[:, 2 * i:2 * i + 2, :], dt_[i % 2][:]).then_inc(sig("my_hi"), 1)
            squares(hview, SEQ, lambda k: act.wait_ge(sig("evac2"), U_MIXO - U_GQK + k // 2 + 1))
            split_x(4 * KC, SEQ)
            swiglu(U_F2I, 2)
            squares(hview, SEQ, lambda k: act.wait_ge(sig("down_evac"), 2 * KC + k + 1))
            act.wait_ge(sig("unit_done"), U_PLEG)
            act.dma_start(pin[:], p2[0, 0].rearrange("(j p) n -> p j n", p=P)).then_inc(sig("p_in"), 16)
            split_x(5 * KC, SEQ)
            for k in range(2):
                act.wait_ge(sig("p_turned"), k + 1)
                nc.scalar.copy(phi[:, k, :], bank(4 + k)).then_inc(sig("p_hi"), 1)
            for u in range(U_PLEG, U_PLEP):
                hi_of(u + 2)
                i = u - U_PLEG
                act.wait_ge(sig("unit_done"), u + 1)
                nc.scalar.activation(sgp[:, 2 * i:2 * i + 2, :], pair(bank(2 * (u % 2), 2)), ACT.Sigmoid
                                     ).then_inc(sig("pg_evac"), 1)
            squares(hview, SEQ, lambda k: act.wait_ge(sig("ple_added"), k + 1))


        @block.vector
        def _(dve):
            step = Count(dve, sig("dve_step"))
            norms, roots = [0], [0]
            vec = nc.vector

            def refined(total, share):
                n = roots[0]
                roots[0] += 1
                y, m, a = (v[:, 0:total.shape[-1]] for v in (root[n % 2], root[2], root[3]))
                dve.wait_ge(sig("log_done"), n + 1)
                step.up(vec.tensor_scalar(m, total, -0.5 * share, -0.5 * EPS, ALU.mult, ALU.add))
                dve.wait_ge(sig("root_done"), n + 1)
                step.up(vec.tensor_tensor(a, y, y, ALU.mult))
                step.wait()
                step.up(vec.tensor_tensor(a, a, m, ALU.mult))
                step.wait()
                step.up(vec.scalar_tensor_tensor(out=y, in0=a, scalar=1.5, in1=y, op0=ALU.add, op1=ALU.mult))
                step.wait()
                return y

            def norm():
                total, _ = norm_places(norms[0])
                norms[0] += 1
                return refined(total, 1.0 / D)

            def make_x(view, gain, T, base):
                scale = norm()
                for k in range(KC + 1):
                    if k < KC:
                        if k >= 3:
                            dve.wait_ge(sig("x_ready"), base + k - 2)
                        vec.scalar_tensor_tensor(out=nt[k % 3][:, 0:T], in0=view(k),
                                                 scalar=cv[:, gain + k:gain + k + 1], in1=scale,
                                                 op0=ALU.mult, op1=ALU.mult).then_inc(sig("nt_ready"), 1)
                    if k >= 1:
                        dve.wait_ge(sig("xhi_ready"), base + k)
                        vec.tensor_tensor(xlo[:, k - 1, 0:T], nt[(k - 1) % 3][:, 0:T],
                                          xhi[:, k - 1, 0:T].bitcast(F32), ALU.subtract
                                          ).then_inc(sig("x_ready"), 1)

            def add_normed(gain, T, first_token, base):
                scale = norm()
                for k in range(KC + 1):
                    if k < KC:
                        if k >= 3:
                            dve.wait_ge(sig("res_ready"), base + k - 2)
                        step.up(vec.scalar_tensor_tensor(out=nt[k % 3][:, 0:T], in0=mix[:, k, 0:T],
                                                         scalar=cv[:, gain + k:gain + k + 1], in1=scale,
                                                         op0=ALU.mult, op1=ALU.mult))
                    if k >= 1:
                        step.wait(step.n - (1 if k < KC else 0))
                        hk = h[:, k - 1, first_token:first_token + T]
                        vec.tensor_tensor(hk, hk, nt[(k - 1) % 3][:, 0:T], ALU.add
                                          ).then_inc(sig("res_ready"), 1)

            step.up(vec.memset(small[:, 0:1], 1.0))
            step.up(vec.memset(small[:, 1:2], -1.0))
            step.up(vec.memset(small[:, 2:3], 0.0))
            vec.memset(small[:, 3:4], EPS).then_inc(sig("cols_ready"), 1)
            for k in range(KC):
                dve.wait_ge(sig("x_turned"), k + 1)
                vec.tensor_copy(h[:, k, :], regions[:, k % 4, BANK - META:2 * BANK]).then_inc(sig("h_ready"), 1)
            dve.wait_ge(sig("h_ready"), KC)
            dve.wait_ge(sig("const_in"), 32)
            make_x(lambda k: h[:, k, :], G_PRE, T1, 0)

            def evac(u, dst, scale=None):
                dve.wait_ge(sig("unit_done"), u + 1)
                if scale is None:
                    vec.tensor_copy(dst, chunks1(u % 2)).then_inc(sig("evac"), 1)
                else:
                    vec.tensor_scalar(dst, chunks1(u % 2), scale, None, ALU.mult).then_inc(sig("evac"), 1)

            def evac_qkv(u0, qk, v):
                for c in range(6):
                    if c < 4:
                        evac(u0 + c, qk[:, 2 * c:2 * c + 2, :], 0.125 if c < 2 else None)
                    else:
                        evac(u0 + c, v[:, 2 * c - 8:2 * c - 6, :])

            evac_qkv(U_PROJ, qkf, vfm)
            dve.wait_ge(sig("unit_done"), U_F + 1)
            zsrc = chunks1(U_F % 2)[0:8, 0, :]
            vec.tensor_scalar(fz[:], zsrc, cv[0:8, C_BF:C_BF + 1], None, ALU.add).then_inc(sig("evac"), 1)
            dve.wait_ge(sig("evac"), U_F + 1)
            step.up(vec.tensor_scalar(fm[:], fz[:], -1.0, 0.0, ALU.mult, ALU.max))
            vec.scalar_tensor_tensor(out=fa[:], in0=fz[:], scalar=-1.0, in1=fz[:], op0=ALU.mult, op1=ALU.min
                                     ).then_inc(sig("f_z"), 1)
            evac_qkv(U_QKVB, qkb, vbm)
            dve.wait_ge(sig("f_ln"), 2)
            dve.wait_ge(sig("f_z"), 1)
            step.up(vec.tensor_tensor(fm[:], fm[:], fl[:], ALU.add))
            step.up(vec.memset(fz[:], 1.0))
            step.wait()
            vec.tensor_tensor_scan(negc[:], fz[:], fm[:], 0.0, ALU.mult, ALU.add).then_inc(sig("c_ready"), 1)
            for j in range(10):
                dve.wait_ge(sig("v_turned"), j + 1)
                if j < 4:
                    dst, src = vf[:, j, :], bank(j % 8)
                elif j == 4:
                    dst, src = vf_tail[:], bank(j % 8)[0:META, :]
                else:
                    dst, src = vb[:, j - 5, :], bank(j % 8)
                vec.tensor_copy(dst, src).then_inc(sig("v_ready"), 1)

            def out_lo(n, base, chunk0):
                head, rows, c, i, t0, tw, _ = item(n)
                dve.wait_ge(sig("o_hi"), base + n + 1)
                dst = slice(t0, t0 + tw)
                vec.tensor_tensor(xlo[rows, chunk0 + c, dst], bank(6 + n % 2)[rows, 0:tw],
                                  xhi[rows, chunk0 + c, dst].bitcast(F32), ALU.subtract
                                  ).then_inc(sig("o_lo"), 1)

            dve.wait_ge(sig("v_ready"), 10)
            dve.wait_ge(sig("c_copied"), 8)
            for n in range(NI + 3):
                if n < NI:
                    head, rows, c, i, t0, tw, w = item(n)
                    base = (n % 2) * 2 * BANK + (BANK if i < 4 else BANK - META)
                    dve.wait_ge(sig("fox_s"), n + 1)
                    scores = ps[0:tw, base:base + w]
                    step.up(vec.tensor_tensor_reduce(scores, scores, ncb[head // 4][0:tw, head % 4, 0:w], 1.0, -3e38,
                                                     ALU.add, ALU.max, fox_c[0:tw, 2, n:n + 1]))
                    step.wait()
                    vec.tensor_scalar(fox_c[0:tw, 0, n:n + 1], fox_c[0:tw, 2, n:n + 1], -1.0, None, ALU.mult
                                      ).then_inc(sig("fox_max"), 1)
                m = n - 1
                if 0 <= m < NI:
                    head, rows, c, i, t0, tw, w = item(m)
                    dve.wait_ge(sig("fox_exp"), m + 1)
                    dve.wait_ge(sig("fox_max"), m + 1)
                    step.up(vec.reciprocal(fox_c[0:tw, 2, m:m + 1], fox_c[0:tw, 1, m:m + 1]))
                    step.wait()
                    vec.tensor_scalar(fox_p[m % 3][0:tw, 0:w], fox_p[m % 3][0:tw, 0:w],
                                      fox_c[0:tw, 2, m:m + 1], None, ALU.mult).then_inc(sig("fox_norm"), 1)
                m = n - 3
                if 0 <= m < NI:
                    out_lo(m, 0, 0)
            dve.wait_ge(sig("fox_t"), NI)
            vec.tensor_scalar(keep[:], madds, -1.0, None, ALU.is_gt).then_inc(sig("keep_ready"), 1)
            dve.wait_ge(sig("keep_ready"), 1)
            for n in range(NI + 2):
                if n < NI:
                    head, rows, c, i, t0, tw, _ = item(n)
                    w = P * (i + 1) if i < 4 else 5 * META
                    dve.wait_ge(sig("sb_l"), n + 1)
                    if n >= 2:
                        dve.wait_ge(sig("sb_acc"), n - 1)
                    sp_ = sb_p[n % 2]
                    last = sp_[:, w - tw:w]
                    step.up(vec.scalar_tensor_tensor(out=sp_[:, 0:w], in0=bank(n % 4)[:, 0:w], scalar=0.0,
                                                     in1=sb_l[n % 2][:, 0:w], op0=ALU.max, op1=ALU.add))
                    step.wait()
                    vec.tensor_tensor(last, last, keep[:] if i < 4 else keep_tail, ALU.mult
                                      ).then_inc(sig("sb_sp"), 1)
                m = n - 2
                if 0 <= m < NI:
                    out_lo(m, NI, 4)
            dve.wait_ge(sig("sb_a"), NI)
            for m in range(8):
                if m % 2 == 0:
                    dve.wait_ge(sig("o_half"), m // 2 + 1)
                else:
                    dve.wait_ge(sig("unit_done"), U_O + m // 2 + 1)
                if m >= 2:
                    dve.wait_ge(sig("y_lo"), m - 1)
                ya, yb = regions[:, 2 * (m % 2), LO:LO + T1], regions[:, 2 * (m % 2) + 1, LO:LO + T1]
                t0, t1 = yt[2 * (m % 2)], yt[2 * (m % 2) + 1]
                step.up(vec.tensor_tensor(t0[:], ya, gates[:, m, :], ALU.mult))
                vec.tensor_tensor(t1[:], yb, gates[:, 8 + m, :], ALU.mult).then_inc(sig("y_evac"), 1)
                dve.wait_ge(sig("y_evac"), m + 1)
                vec.tensor_tensor(t0[:], t0[:], t1[:], ALU.add).then_inc(sig("y_sum"), 1)
                dve.wait_ge(sig("y_hi"), m + 1)
                vec.tensor_tensor(ylo[:, m, :], t0[:], yhi[:, m, :].bitcast(F32), ALU.subtract
                                  ).then_inc(sig("y_lo"), 1)
            for j in range(4):
                u = U_WOUT + j
                dve.wait_ge(sig("unit_done"), u + 1)
                vec.tensor_copy(mix[:, 2 * j:2 * j + 2, :], chunks1(u % 2)).then_inc(sig("mix_ready"), 1)
            dve.wait_ge(sig("mix_ready"), 4)
            add_normed(G_MIX, T1, 0, 0)
            dve.wait_ge(sig("res_ready"), KC)
            make_x(lambda k: h[:, k, :], G_FFN, T1, 8)

            def conv(dst, b, i, col, done):
                for tap in range(3):
                    for c in range(2):
                        src = regions[:, 2 * b + c, LO + META - 2 + tap:LO + META - 2 + tap + SEQ]
                        wcol = cv[:, bass.ds(i * 2 + (C_CW + 2 * FC * tap + col + c), 1)]
                        if tap == 0:
                            bcol = cv[:, bass.ds(i * 2 + (C_CB + col + c), 1)]
                            ins = vec.tensor_scalar(dst[:, c, :], src, wcol, bcol, ALU.mult, ALU.add)
                        else:
                            step.wait(step.n - 1)
                            ins = vec.scalar_tensor_tensor(out=dst[:, c, :], in0=src, scalar=wcol,
                                                           in1=dst[:, c, :], op0=ALU.mult, op1=ALU.add)
                        if tap == 2 and c == 1:
                            ins.then_inc(sig(done), 1)
                        else:
                            step.up(ins)

            def hidden_conv(i, first):
                b = U_UP % 2
                dve.wait_ge(sig("unit_done"), i * 2 + (U_UP + 1))
                if not first:
                    dve.wait_ge(sig("gate_act"), i)
                conv(cg, b, i, 0, "gate_ready")
                dve.wait_ge(sig("unit_done"), i * 2 + (U_UP + 2))
                if not first:
                    dve.wait_ge(sig("hid_lo"), i)
                conv(cvl, 1 - b, i, FC, "val_ready")
                dve.wait_ge(sig("val_ready"), i + 1)
                step.wait()
                dve.wait_ge(sig("gate_act"), i + 1)
                vec.tensor_tensor(cvl[:], cvl[:], gact[:], ALU.mult).then_inc(sig("prod"), 1)
                dve.wait_ge(sig("prod"), i + 1)
                dve.wait_ge(sig("hid_hi"), i + 1)
                vec.tensor_tensor(hlo[:, bass.ds(i * 2, 2), :], cvl[:], hhi[:, bass.ds(i * 2, 2), :].bitcast(F32),
                                  ALU.subtract).then_inc(sig("hid_lo"), 1)

            hidden_conv(0, True)
            with dve.Fori(1, FC // 2) as i:
                step.enter(i - 1, 10)
                hidden_conv(i, False)
            step.leave(FC // 2 - 1)
            for m in range(KC):
                if m < KC - 1:
                    dve.wait_ge(sig("down_done"), m + 1)
                else:
                    dve.wait_ge(sig("unit_done"), U_END1)
                vec.tensor_copy(mix[:, m, 0:SEQ], bank(m)).then_inc(sig("down_evac"), 1)
            dve.wait_ge(sig("down_evac"), KC)
            add_normed(G_POST, SEQ, META, KC)

            hview = lambda k: h[:, k, META:T1]
            dve.wait_ge(sig("res_ready"), 2 * KC)
            make_x(hview, G_F1, SEQ, 2 * KC)

            def swiglu(unit0, layer):
                done = layer * (FC // 2)
                b = 1 - unit0 % 2

                def one(i, first):
                    dve.wait_ge(sig("unit_done"), i * 2 + (unit0 + 2))
                    dve.wait_ge(sig("hid_lo"), i + done)
                    dve.wait_ge(sig("gate_act"), i + (done + 1))
                    vec.tensor_tensor(cvl[:], gact[:], pair(bank(2 * b, 2)), ALU.mult).then_inc(sig("prod"), 1)
                    dve.wait_ge(sig("prod"), i + (done + 1))
                    dve.wait_ge(sig("hid_hi"), i + (done + 1))
                    vec.tensor_tensor(hlo[:, bass.ds(i * 2, 2), :], cvl[:],
                                      hhi[:, bass.ds(i * 2, 2), :].bitcast(F32), ALU.subtract
                                      ).then_inc(sig("hid_lo"), 1)

                one(0, True)
                with dve.Fori(1, FC // 2) as i:
                    one(i, False)
                for m in range(KC):
                    if m < KC - 1:
                        dve.wait_ge(sig("down_done"), (KC - 1) * layer + m + 1)
                    else:
                        dve.wait_ge(sig("unit_done"), unit0 + FC + FC // 2)
                    vec.scalar_tensor_tensor(out=hview(m), in0=bank(m), scalar=0.5, in1=hview(m),
                                             op0=ALU.mult, op1=ALU.add).then_inc(sig("down_evac"), 1)
                dve.wait_ge(sig("down_evac"), KC * (layer + 1))

            swiglu(U_F1I, 1)
            make_x(hview, G_MIX2, SEQ, 3 * KC)

            def out_of(u, dst, scale=None, src=None, last=True):
                dve.wait_ge(sig("unit_done"), u + 1)
                if u > U_GQK:
                    dve.wait_ge(sig("evac2"), u - U_GQK)
                src = pair(bank(2 * (u % 2), 2)) if src is None else src
                if scale is None:
                    ins = vec.tensor_copy(dst, src)
                else:
                    ins = vec.tensor_scalar(dst, src, scale, None, ALU.mult)
                if last:
                    ins.then_inc(sig("evac2"), 1)
                else:
                    step.up(ins)

            for c in range(4):
                out_of(U_GQK + c, gqk[:, 2 * c:2 * c + 2, :], float(np.float32(P ** -0.5)) if c < 2 else None)
            for c in range(4):
                out_of(U_GV + c, gvf[:, 2 * c:2 * c + 2, :])
            u = U_SPC
            first, second = bank(2 * (u % 2)), bank(2 * (u % 2) + 1)
            out_of(u, gaf[:], src=first[0:META], last=False)
            out_of(u, dkvf[:], src=second)
            u = U_SPC + 1
            first, second = bank(2 * (u % 2)), bank(2 * (u % 2) + 1)
            out_of(u, ikd[0:64, :], src=first[0:64], last=False)
            out_of(u, iwf[64:72, :], src=first[64:72], last=False)
            out_of(u, ikd[64:P, :], src=second[64:P])
            dve.wait_ge(sig("brow_done"), 1)
            vec.tensor_copy(brow[:], ps[0:8, 4 * BANK:4 * BANK + 640]).then_inc(sig("brow_ready"), 1)
            for j in range(4):
                dve.wait_ge(sig("gv_turned"), j + 1)
                vec.tensor_copy(gvt[:, j, :], bank(4 + 2 * (j % 2), 2)).then_inc(sig("gv_ready"), 1)
            scale = refined(bank(1), 1.0 / P)
            dve.wait_ge(sig("evac2"), U_MG1 - U_GQK)
            vec.scalar_tensor_tensor(out=ckvf[:], in0=dkvf[:], scalar=cv[:, C_CKV:C_CKV + 1], in1=scale,
                                     op0=ALU.mult, op1=ALU.mult).then_inc(sig("ckv_ready"), 1)
            dve.wait_ge(sig("ckv_turned"), 1)
            step.up(vec.tensor_copy(ckvt[:].rearrange("p j c -> p (j c)"), bank(2)))
            vec.tensor_scalar(iwt, bank(3)[:, 0:32], float(np.float32(8 ** -0.5)), None, ALU.mult
                              ).then_inc(sig("iw_ready"), 1)
            for hd in range(4):
                dve.wait_ge(sig("alpha_done"), hd + 1)
                step.up(vec.tensor_scalar(ax[:, hd, :], bank(4 + hd), cv[:, C_AB + hd:C_AB + hd + 1], None, ALU.add))
            step.wait()
            vec.scalar_tensor_tensor(out=al[:], in0=ax[:], scalar=-1.0, in1=ax[:], op0=ALU.mult, op1=ALU.min
                                     ).then_inc(sig("decay_x"), 1)
            dve.wait_ge(sig("decay_x"), 1)
            step.up(vec.tensor_scalar(ax[:], ax[:], -1.0 / 16, 0.0, ALU.mult, ALU.max))
            step.up(vec.memset(restart[:], 1.0))
            step.wait()
            step.up(vec.memset(restart[:].rearrange("p (j c) -> p j c", c=P)[:, :, 0:1], 0.0))
            dve.wait_ge(sig("decay_ln"), 1)
            step.up(vec.scalar_tensor_tensor(out=ax[:], in0=al[:], scalar=1.0 / 16, in1=ax[:],
                                             op0=ALU.mult, op1=ALU.add))
            step.wait()
            for hd in range(4):
                step.up(vec.tensor_tensor_scan(nbt[:, hd, :], restart[:], ax[:, hd, :], 0.0, ALU.mult, ALU.add))
            step.wait()

            def halves(ap, L):
                v = ap.rearrange("p (n c) -> p n c", c=2 ** L)
                return v[:, :, 0:2 ** (L - 1)], v[:, :, 2 ** (L - 1):]

            for q in range(NG + 2):
                if q < NG:
                    hd, kind = GI[q]
                    nbh = nbt[:, hd, :]
                    if 0 < kind < 8:
                        if q >= 3:
                            dve.wait_ge(sig("g_mm"), q - 2)
                        lo_n, up_n = halves(nbh, kind)
                        lo_f, up_f = halves(gf[q % 3][:], kind)
                        mid = lo_n[:, :, 2 ** (kind - 1) - 1:].to_broadcast([P, SEQ >> kind, 2 ** (kind - 1)])
                        step.up(vec.tensor_tensor(lo_f, lo_n, mid, ALU.subtract))
                        vec.tensor_tensor(up_f, mid, up_n, ALU.subtract).then_inc(sig("g_d"), 1)
                    elif kind == 8:
                        if hd:
                            dve.wait_ge(sig("g_mm"), cross_of(hd - 1) + 1)
                        tiles = nbh.rearrange("p (j c) -> p j c", c=P)
                        ends = tiles[:, 0:3, P - 1:].to_broadcast([P, 3, P])
                        step.up(vec.tensor_tensor(kx[:, 0:3, :], tiles[:, 0:3, :], ends, ALU.subtract))
                        vec.tensor_scalar(kx[:, 3:6, :], tiles[:, 1:4, :], -1.0, None, ALU.mult
                                          ).then_inc(sig("g_d"), 1)
                m = q - 1
                if 0 <= m < NG:
                    hd, kind = GI[m]
                    qh, kh = gqk[:, hd, :], gqk[:, 4 + hd, :]
                    if kind:
                        dve.wait_ge(sig("g_e"), m - hd)
                    if 0 < kind < 8:
                        lo_f, up_f = halves(gf[m % 3][:], kind)
                        step.up(vec.tensor_tensor(lo_f, lo_f, halves(kh, kind)[0], ALU.mult))
                        vec.tensor_tensor(up_f, up_f, halves(qh, kind)[1], ALU.mult).then_inc(sig("g_f"), 1)
                    elif kind == 8:
                        tiled = lambda ap: ap.rearrange("p (j c) -> p j c", c=P)
                        step.up(vec.tensor_tensor(kx[:, 0:3, :], kx[:, 0:3, :], tiled(kh)[:, 0:3, :], ALU.mult))
                        step.up(vec.tensor_tensor(kx[:, 3:6, :], kx[:, 3:6, :], tiled(qh)[:, 1:4, :], ALU.mult))
                        step.wait()
                        step.up(vec.tensor_scalar(kx2[:, 0, :], kx[:, 0, :], ex[:, 0:1], None, ALU.mult))
                        vec.tensor_scalar(kx2[:, 1, :], kx[:, 5, :], ex[:, 1:2], None, ALU.mult
                                          ).then_inc(sig("g_f"), 1)
                m = q - 2
                if 0 <= m < NG:
                    hd, kind = GI[m]
                    dve.wait_ge(sig("g_mm"), m + 1)
                    src = bank(m % 3).rearrange("p (j c) -> p j c", c=P)
                    if kind == 0:
                        if hd >= 2:
                            dve.wait_ge(sig("g_o"), hd - 1)
                        every = ident[:].rearrange("p (a c) -> p a c", a=1).to_broadcast([P, 4, P])
                        vec.tensor_tensor(sd[hd % 2][:], src, every, ALU.mult).then_inc(sig("g_cp"), 1)
                    elif kind < 8:
                        dve.wait_ge(sig("g_cp"), diag_seen(m) - 1)
                        mk = ga_m[:, (kind - 1) * P:kind * P] if kind < 5 else gb_m[:, (kind - 5) * P:(kind - 4) * P]
                        mk = mk.rearrange("p (a c) -> p a c", a=1).to_broadcast([P, 4, P])
                        vec.copy_predicated(sd[hd % 2][:], mk, src).then_inc(sig("g_cp"), 1)
            for k in range(9):
                if k < 8:
                    if k % 2 == 0:
                        scale = refined(bank(4 + k // 2), 1.0 / 256)
                    if k >= 3:
                        dve.wait_ge(sig("gy_lo"), k - 2)
                    step.up(vec.scalar_tensor_tensor(out=nt[k % 3][:, 0:SEQ], in0=gout[:, k, :],
                                                     scalar=cv[:, G_GLA + k:G_GLA + k + 1], in1=scale,
                                                     op0=ALU.mult, op1=ALU.mult))
                if k >= 1:
                    dve.wait_ge(sig("gy_hi"), k)
                    vec.tensor_tensor(gyl[:, k - 1, :], nt[(k - 1) % 3][:, 0:SEQ], gyh[:, k - 1, :].bitcast(F32),
                                      ALU.subtract).then_inc(sig("gy_lo"), 1)
                if k < 8:
                    step.wait()
                    vec.tensor_tensor(nt[k % 3][:, 0:SEQ], nt[k % 3][:, 0:SEQ], grs[:, k, :], ALU.mult
                                      ).then_inc(sig("gy_ready"), 1)
            for c in range(4):
                u = U_GLAO + c
                dve.wait_ge(sig("unit_done"), u + 1)
                dve.wait_ge(sig("evac2"), u - U_GQK)
                gc = g1[:, 2 * c:2 * c + 2, :]
                vec.tensor_tensor(gc, gc, pair(bank(2 * (u % 2), 2)), ALU.mult).then_inc(sig("evac2"), 1)
            for c in range(4):
                out_of(U_DQ + c, dq[:, 2 * c:2 * c + 2, :], float(np.float32(P ** -0.5)))
            for c in range(2):
                out_of(U_IQ + c, iqf[:, 2 * c:2 * c + 2, :], 0.125)
            dve.wait_ge(sig("iw_ready"), 1)
            for m in range(24):
                j, hd = 1 + m // 8, m % 8
                w = P * (j + 1)
                a = acc[0][:, 0:w]
                dve.wait_ge(sig("ix_relu"), m + 1)
                wcol = iwt[:, 8 * j + hd:8 * j + hd + 1]
                if hd == 0:
                    if m:
                        dve.wait_ge(sig("mask_ready"), j - 1)
                    vec.tensor_scalar(a, rl[m % 2][:, 0:w], wcol, None, ALU.mult).then_inc(sig("ix_acc"), 1)
                else:
                    dve.wait_ge(sig("ix_acc"), m)
                    vec.scalar_tensor_tensor(out=a, in0=rl[m % 2][:, 0:w], scalar=wcol, in1=a,
                                             op0=ALU.mult, op1=ALU.add).then_inc(sig("ix_acc"), 1)
                if hd == 7:
                    dve.wait_ge(sig("ix_acc"), m + 1)
                    step.up(vec.tensor_tensor(a[:, w - P:], a[:, w - P:], madd, ALU.add))
                    step.wait()
                    for r in range(16):
                        step.up(vec.max(m8, acc[r % 2][:, 0:w]))
                        step.wait()
                        step.up(vec.match_replace(acc[(r + 1) % 2][:, 0:w], m8, acc[r % 2][:, 0:w], -3e38))
                        step.wait()
                    vec.tensor_scalar(mj[:, mj_at[j]:mj_at[j] + w], a, -2e38, NEG, ALU.is_gt, ALU.mult
                                      ).then_inc(sig("mask_ready"), 1)
            dve.wait_ge(sig("mask_ready"), 3)
            dve.wait_ge(sig("bias_in"), 128)
            for n in range(ND + 3):
                if n < ND:
                    j, hd = DI[n]
                    w = P * (j + 1)
                    dve.wait_ge(sig("da_s"), n + 1)
                    if n >= 3:
                        dve.wait_ge(sig("da_t"), n - 2)
                    step.up(vec.tensor_tensor_reduce(dl[n % 3][:, 0:w], bank(n % 4)[:, 0:w],
                                                     bias[:, hd, w - 1::-1], 1.0, -3e38, ALU.add, ALU.max,
                                                     dst_[:, 2, n:n + 1]))
                    step.wait()
                    vec.tensor_scalar(dst_[:, 0, n:n + 1], dst_[:, 2, n:n + 1], -1.0, None, ALU.mult
                                      ).then_inc(sig("da_max"), 1)
                m = n - 1
                if 0 <= m < ND:
                    w = P * (DI[m][0] + 1)
                    dve.wait_ge(sig("da_exp"), m + 1)
                    dve.wait_ge(sig("da_max"), m + 1)
                    step.up(vec.reciprocal(dst_[:, 2, m:m + 1], dst_[:, 1, m:m + 1]))
                    step.wait()
                    vec.tensor_scalar(dl[m % 3][:, 0:w], dl[m % 3][:, 0:w], dst_[:, 2, m:m + 1], None, ALU.mult
                                      ).then_inc(sig("da_norm"), 1)
                m = n - 3
                if 0 <= m < ND:
                    j, hd = DI[m]
                    dve.wait_ge(sig("da_hi"), m + 1)
                    xs = slice(j * P, (j + 1) * P)
                    vec.tensor_tensor(xlo[:, hd, xs], bank(6 + m % 2)[:, 0:P], xhi[:, hd, xs].bitcast(F32),
                                      ALU.subtract).then_inc(sig("da_lo"), 1)
            for c in range(4):
                u = U_DSAO + c
                dve.wait_ge(sig("unit_done"), u + 1)
                dve.wait_ge(sig("evac2"), u - U_GQK)
                if c >= 2:
                    dve.wait_ge(sig("my_lo"), c - 1)
                tc_ = dt_[c % 2]
                vec.tensor_tensor(tc_[:], g2[:, 2 * c:2 * c + 2, :], pair(bank(2 * (u % 2), 2)), ALU.mult
                                  ).then_inc(sig("evac2"), 1)
                dve.wait_ge(sig("evac2"), u - U_GQK + 1)
                vec.tensor_tensor(tc_[:], tc_[:], g1[:, 2 * c:2 * c + 2, :], ALU.add).then_inc(sig("my_ready"), 1)
                dve.wait_ge(sig("my_hi"), c + 1)
                vec.tensor_tensor(myl[:, 2 * c:2 * c + 2, :], tc_[:], myh[:, 2 * c:2 * c + 2, :].bitcast(F32),
                                  ALU.subtract).then_inc(sig("my_lo"), 1)
            for c in range(4):
                u = U_MIXO + c
                hc = h[:, 2 * c:2 * c + 2, META:T1]
                dve.wait_ge(sig("unit_done"), u + 1)
                vec.tensor_tensor(hc, hc, pair(bank(2 * (u % 2), 2)), ALU.add).then_inc(sig("evac2"), 1)
            dve.wait_ge(sig("evac2"), U_F2I - U_GQK)
            make_x(hview, G_F2, SEQ, 4 * KC)
            swiglu(U_F2I, 2)
            make_x(hview, G_PLE, SEQ, 5 * KC)
            for k in range(2):
                dve.wait_ge(sig("p_hi"), k + 1)
                vec.tensor_tensor(plo[:, k, :], bank(4 + k), phi[:, k, :].bitcast(F32), ALU.subtract
                                  ).then_inc(sig("p_lo"), 1)
            for m in range(KC):
                if m < KC - 1:
                    dve.wait_ge(sig("ple_done"), m + 1)
                else:
                    dve.wait_ge(sig("unit_done"), U_PLEP + 1)
                step.up(vec.tensor_tensor(sgp[:, m, :], sgp[:, m, :], bank(m), ALU.mult))
                step.wait()
                vec.tensor_tensor(hview(m), hview(m), sgp[:, m, :], ALU.add).then_inc(sig("ple_added"), 1)
            dve.wait_ge(sig("ple_added"), KC)
            scale = norm()
            for k in range(KC):
                vec.scalar_tensor_tensor(out=fin[:, k, :], in0=hview(k), scalar=cv[:, G_FIN + k:G_FIN + k + 1],
                                         in1=scale, op0=ALU.mult, op1=ALU.mult).then_inc(sig("fin_ready"), 1)

            for j in range(4):
                dve.wait_ge(sig("out_turned"), j + 1)
                if j >= 2:
                    dve.wait_ge(sig(f"stored{j % 2}"), 16)
                vec.tensor_copy(outb[j % 2][:], bank(2 * (j % 2), 2)).then_inc(sig("out_copied"), 1)

        @block.tensor
        def _(pe):
            mm = nc.tensor.matmul
            norms = [0]

            def tile_products(slot, tile, places, xh, xl, first, last):
                cols = slice(tile * P, (tile + 1) * P)
                for p_, (w, xx) in enumerate(((whi, xh), (whi, xl), (wlo, xh))):
                    for dst, tok in places:
                        ins = mm(dst, w[slot][:, cols], xx(tok), start=first and p_ == 0, stop=last and p_ == 2,
                                 skip_group_check=True)
                return ins

            def places_of(b, c, T):
                if T == T1:
                    r = regions[:, 2 * b + c, :]
                    return [(r[:, LO:BANK], slice(0, HALF)), (r[:, BANK:BANK + HALF], slice(HALF, T1))]
                return [(bank(2 * b + c), slice(0, SEQ))]

            def unit(b, T, xh, xl, x_base=None):
                order = [(c, k) for c in range(2) for k in range(KC)]
                if x_base is not None:
                    order = [(c, k) for k in range(KC) for c in range(2)]
                for c, k in order:
                    if x_base is not None and c == 0:
                        pe.wait_ge(sig("x_ready"), x_base + k + 1)
                    ins = tile_products(b, c * KC + k, places_of(b, c, T),
                                        lambda tok: xh[:, k, tok], lambda tok: xl[:, k, tok],
                                        k == 0, k == KC - 1)
                ins.then_inc(sig("unit_done"), 1)

            def norm():
                n = norms[0]
                norms[0] += 1
                T, _ = NORMS[n]
                total, parts = norm_places(n)
                for k in range(KC):
                    pe.wait_ge(sig("sq_done"), 8 * n + k + 1)
                    for tok in parts:
                        ins = mm(total[:, tok], one_col.to_broadcast([P, P]), sq[k % 2][:, tok],
                                 start=(k == 0), stop=(k == KC - 1))
                    ins.then_inc(sig("sq_used"), 1)

            pe.wait_ge(sig("ident_in"), 16)
            pe.wait_ge(sig("x_in"), 80)
            for k in range(KC):
                if k >= 4:
                    pe.wait_ge(sig("h_ready"), k - 3)
                r = regions[:, k % 4, :]
                nc.tensor.transpose(r[:, BANK - META:BANK], xmeta[:, k * P:(k + 1) * P], ident[0:META, 0:META])
                for j in range(4):
                    ins = nc.tensor.transpose(r[:, BANK + j * P:BANK + (j + 1) * P], xin[:, j, k * P:(k + 1) * P],
                                              ident[:])
                ins.then_inc(sig("x_turned"), 1)
            pe.wait_ge(sig("h_ready"), 7)
            pe.wait_ge(sig("cols_ready"), 1)
            norm()
            pe.wait_ge(sig("lo_done"), 1)
            unit(0, T1, xhi, xlo, 0)
            pe.wait_ge(sig("lo_done"), 2)
            unit(1, T1, xhi, xlo)
            with pe.Fori(1, (U_O - 1) // 2) as i:
                for b in range(2):
                    pe.wait_ge(sig("lo_done"), i * 2 + (b + 1))
                    pe.wait_ge(sig("evac"), i * 2 + (b - 1))
                    unit(b, T1, xhi, xlo)
            pe.wait_ge(sig("lo_done"), U_O)
            pe.wait_ge(sig("evac"), U_O - 2)
            unit((U_O - 1) % 2, T1, xhi, xlo)
            pe.wait_ge(sig("evac"), U_O)
            for j in range(10):
                src = vfm if j < 5 else vbm
                a = (P * (j % 5), P) if j % 5 < 4 else ((SEQ, META) if j == 4 else (T1 - P, P))
                if j >= 8:
                    pe.wait_ge(sig("v_ready"), j - 7)
                for c in range(4):
                    ins = nc.tensor.transpose(bank(j % 8)[0:a[1], c * P:(c + 1) * P], src[:, c, a[0]:a[0] + a[1]],
                                              ident[:])
                ins.then_inc(sig("v_turned"), 1)
            pe.wait_ge(sig("v_ready"), 10)
            pe.wait_ge(sig("c_ready"), 1)

            for head in range(8):
                if head >= 4:
                    pe.wait_ge(sig("c_copied"), head - 3)
                for dst, tok in places_of(head // 2 % 2, head % 2, T1):
                    ins = mm(dst, ident[0:8, head:head + 1].to_broadcast([8, P]), negc[0:8, tok], start=True, stop=True)
                ins.then_inc(sig("c_spread"), 1)
            pe.wait_ge(sig("c_copied"), 8)
            for n in range(NI + 3):
                if n < NI:
                    head, rows, c, i, t0, tw, w = item(n)
                    base = (n % 2) * 2 * BANK + (BANK if i < 4 else BANK - META)
                    if n >= 2:
                        pe.wait_ge(sig("fox_exp"), n - 1)
                    cuts = [(0, w)] if i < 4 else [(0, META), (META, T1)]
                    for a, z in cuts:
                        dst = ps[0:tw, base + a:base + z]
                        mm(dst, qkf[rows, c, t0:t0 + tw], qkf[rows, 4 + c, a:z], start=True, stop=(z < w),
                           skip_group_check=True)
                    ins = mm(ps[0:tw, base + t0:base + w], ident[0:tw, 0:tw], madd[0:tw, 0:tw], start=False,
                             stop=True, skip_group_check=True)
                    ins.then_inc(sig("fox_s"), 1)
                m = n - 2
                if 0 <= m < NI:
                    head, rows, c, i, t0, tw, w = item(m)
                    pe.wait_ge(sig("fox_norm"), m + 1)
                    if m >= 2:
                        pe.wait_ge(sig("fox_pt"), m - 1)
                    pm, dst = fox_p[m % 3], bank(4 + m % 2)
                    for b in range(min(i + 1, 4)):
                        ins = nc.tensor.transpose(dst[:, b * tw:(b + 1) * tw], pm[0:tw, b * P:(b + 1) * P],
                                                  ident[0:tw, 0:tw])
                    if i == 4:
                        ins = nc.tensor.transpose(dst[0:META, 64:80], pm[0:META, SEQ:T1], ident[0:META, 0:META])
                    ins.then_inc(sig("fox_t"), 1)
                m = n - 3
                if 0 <= m < NI:
                    head, rows, c, i, t0, tw, w = item(m)
                    pe.wait_ge(sig("fox_pt"), m + 1)
                    if m >= 2:
                        pe.wait_ge(sig("o_lo"), m - 1)
                    dst = bank(6 + m % 2)[rows, 0:tw]
                    hc = slice(64 * head, 64 * head + 64)
                    nb_ = min(i + 1, 4)
                    for b in range(nb_):
                        ins = mm(dst, vf[:, b, hc], fox_pt[m % 2][:, b * tw:(b + 1) * tw], start=(b == 0),
                                 stop=(b == nb_ - 1 and i < 4), skip_group_check=True)
                    if i == 4:
                        ins = mm(dst, vf_tail[:, hc], fox_pt[m % 2][0:META, 64:80], start=False, stop=True,
                                 skip_group_check=True)
                    ins.then_inc(sig("o_done"), 1)
            pe.wait_ge(sig("o_lo"), NI)
            pe.wait_ge(sig("keep_ready"), 1)
            for n in range(NI + 2):
                if n < NI:
                    head, rows, c, i, t0, tw, _ = item(n)
                    if n >= 4:
                        pe.wait_ge(sig("sb_a"), n - 3)
                    nb_ = i + 1
                    for b in range(nb_):
                        s0 = b * P if b < 4 else T1 - P
                        ins = mm(bank(n % 4)[:, b * tw:(b + 1) * tw], qkb[rows, 4 + c, s0:s0 + P],
                                 qkb[rows, c, t0:t0 + tw], start=(b == 0), stop=False, skip_group_check=True)
                    ins.then_inc(sig("sb_z"), 1)
                m = n - 1
                if 0 <= m < NI:
                    head, rows, c, i, t0, tw, _ = item(m)
                    pe.wait_ge(sig("sb_sp"), m + 1)
                    nb_ = i + 1
                    for b in range(nb_):
                        dst = bank(m % 4)[:, b * tw:(b + 1) * tw]
                        for b2 in range(b, nb_):
                            mm(dst, ntri if b2 == b else neg_col.to_broadcast([P, P]),
                               sb_p[m % 2][:, b2 * tw:(b2 + 1) * tw], start=False, stop=False,
                               skip_group_check=True)
                    ins = mm(dst, ident[:], madds if i < 4 else madds_tail, start=False, stop=True,
                             skip_group_check=True)
                    ins.then_inc(sig("sb_acc"), 1)
                m = n - 2
                if 0 <= m < NI:
                    head, rows, c, i, t0, tw, _ = item(m)
                    pe.wait_ge(sig("sb_a"), m + 1)
                    pe.wait_ge(sig("o_lo"), NI + m - 1)
                    dst = bank(6 + m % 2)[rows, 0:tw]
                    nb_ = i + 1
                    for b in range(nb_):
                        ins = mm(dst, vb[:, b, 64 * head:64 * head + 64], sb_a[m % 2][:, b * tw:(b + 1) * tw],
                                 start=(b == 0), stop=(b == nb_ - 1), skip_group_check=True)
                    ins.then_inc(sig("o_done"), 1)
            pe.wait_ge(sig("o_lo"), 2 * NI)
            for m in range(8):
                u = U_O + m // 2
                if m % 2 == 0:
                    pe.wait_ge(sig("lo_done"), u + 1)
                if m >= 2:
                    pe.wait_ge(sig("y_evac"), m - 1)
                for side in range(2):
                    for k in range(4):
                        kk = 4 * side + k
                        ins = tile_products(u % 2, 8 * (m % 2) + kk, places_of(m % 2, side, T1),
                                            lambda tok: xhi[:, kk, tok], lambda tok: xlo[:, kk, tok],
                                            k == 0, k == 3)
                ins.then_inc(sig("o_half" if m % 2 == 0 else "unit_done"), 1)
            pe.wait_ge(sig("y_evac"), 8)
            pe.wait_ge(sig("y_lo"), 8)
            for j in range(4):
                u = U_WOUT + j
                pe.wait_ge(sig("lo_done"), u + 1)
                if j >= 2:
                    pe.wait_ge(sig("mix_ready"), j - 1)
                unit(u % 2, T1, yhi, ylo)
            pe.wait_ge(sig("mix_ready"), 3)
            norm()
            pe.wait_ge(sig("mix_ready"), 4)
            norm()

            def up_pair(i, unit0, T, done, first=False, x_base=None):
                b = unit0 % 2
                pe.wait_ge(sig("lo_done"), i * 2 + (unit0 + 1))
                if not first:
                    pe.wait_ge(sig("gate_ready" if T == T1 else "gate_act"), i + done)
                unit(b, T, xhi, xlo, x_base)
                pe.wait_ge(sig("lo_done"), i * 2 + (unit0 + 2))
                if not first:
                    pe.wait_ge(sig("val_ready" if T == T1 else "prod"), i + done)
                else:
                    pe.wait_ge(sig("x_ready"), x_base + KC)
                unit(1 - b, T, xhi, xlo)

            def down(unit0, layer):
                def two(b, j, first, last):
                    for m in range(KC):
                        for kk in range(2):
                            row = j * 2 + kk
                            ins = tile_products(b, kk * KC + m, [(bank(m), slice(0, SEQ))],
                                                lambda tok: hid_row(hhi, row, tok), lambda tok: hid_row(hlo, row, tok),
                                                first and kk == 0, last and kk == 1)
                        if last and m < KC - 1:
                            ins.then_inc(sig("down_done"), 1)
                    return ins
                b0 = unit0 % 2
                pe.wait_ge(sig("lo_done"), unit0 + 1)
                two(b0, 0, True, False).then_inc(sig("unit_done"), 1)
                with pe.Fori(0, (FC // 2 - 2) // 2) as i:
                    for b in range(2):
                        pe.wait_ge(sig("lo_done"), i * 2 + (unit0 + 2 + b))
                        two((b0 + 1 + b) % 2, i * 2 + (1 + b), False, False).then_inc(sig("unit_done"), 1)
                rest = FC // 2 - 1 - 2 * ((FC // 2 - 2) // 2)
                for q in range(rest):
                    j = FC // 2 - rest + q
                    pe.wait_ge(sig("lo_done"), unit0 + j + 1)
                    two((unit0 + j) % 2, j, False, j == FC // 2 - 1).then_inc(sig("unit_done"), 1)

            def hid_row(t, row, tok):
                if isinstance(row, int):
                    return t[:, row, tok]
                return t[:, bass.ds(row, 1), tok].rearrange("p a n -> p (a n)")

            up_pair(0, U_UP, T1, 0, True, 8)
            with pe.Fori(1, FC // 2) as i:
                up_pair(i, U_UP, T1, 0)
            pe.wait_ge(sig("hid_lo"), FC // 2)
            down(U_DOWN, 0)
            pe.wait_ge(sig("down_evac"), 4)
            norm()

            norm()

            def swiglu(unit0, layer):
                done = layer * (FC // 2)
                up_pair(0, unit0, SEQ, done, True, KC * (layer + 1 if layer == 1 else 4))
                with pe.Fori(1, FC // 2) as i:
                    up_pair(i, unit0, SEQ, done)
                pe.wait_ge(sig("hid_lo"), done + FC // 2)
                down(unit0 + FC, layer)
                pe.wait_ge(sig("down_evac"), KC * layer + 4)

            swiglu(U_F1I, 1)
            norm()

            def units(u0, n, xh, xl, x_base=None):
                def one(b, i, wait_out, base=None):
                    pe.wait_ge(sig("lo_done"), i + (u0 + 1))
                    if wait_out:
                        pe.wait_ge(sig("evac2"), i + (u0 - 1 - U_GQK))
                    unit(b, SEQ, xh, xl, base)
                peel = 2 if u0 == U_GQK else 0
                for q in range(peel):
                    one((u0 + q) % 2, q, False, x_base if q == 0 else None)
                with pe.Fori(peel // 2, n // 2) as i:
                    for q in range(2):
                        one((u0 + q) % 2, i * 2 + q, True)

            units(U_GQK, U_MG1 - U_GQK, xhi, xlo, 3 * KC)
            pe.wait_ge(sig("aux_in"), 80)
            pe.wait_ge(sig("x_ready"), 4 * KC)
            mm(bank(4)[0:8], relb[:], bucket[:, 0:BANK], start=True, stop=True)
            mm(bank(5)[0:8, 0:P], relb[:], bucket[:, BANK:BANK + P], start=True, stop=True
               ).then_inc(sig("brow_done"), 1)
            pe.wait_ge(sig("evac2"), U_MG1 - U_GQK)
            pe.wait_ge(sig("brow_ready"), 1)
            for j in range(4):
                if j >= 2:
                    pe.wait_ge(sig("gv_ready"), j - 1)
                for c in range(8):
                    ins = nc.tensor.transpose(bank(4 + 2 * (j % 2), 2)[:, c * P:(c + 1) * P],
                                              gvf[:, c, j * P:(j + 1) * P], ident[:])
                ins.then_inc(sig("gv_turned"), 1)
            pe.wait_ge(sig("ckv_sq"), 1)
            mm(bank(1), one_col.to_broadcast([P, P]), sq[0][:, 0:SEQ], start=True, stop=True
               ).then_inc(sig("ckv_sums"), 1)
            for j in range(4):
                nc.tensor.transpose(bank(3)[:, 8 * j:8 * j + 8], iwf[64:72, j * P:(j + 1) * P], ident[64:72, 64:72])
            pe.wait_ge(sig("ckv_ready"), 1)
            for j in range(4):
                ins = nc.tensor.transpose(bank(2)[:, j * P:(j + 1) * P], ckvf[:, j * P:(j + 1) * P], ident[:])
            ins.then_inc(sig("ckv_turned"), 1)
            pe.wait_ge(sig("gv_ready"), 4)
            for hd in range(4):
                mm(bank(4 + hd), aw[:, hd * P:(hd + 1) * P], gaf[:], start=True, stop=True
                   ).then_inc(sig("alpha_done"), 1)
            pe.wait_ge(sig("iw_ready"), 1)
            pe.wait_ge(sig("decay_x"), 1)
            for q in range(1, NG + 4):
                m = q - 1
                if 0 <= m < NG:
                    hd, kind = GI[m]
                    if kind:
                        pe.wait_ge(sig("g_f"), m - hd)
                    if kind < 8:
                        if m >= 3 and (seen := diag_seen(m - 3)):
                            pe.wait_ge(sig("g_cp"), seen)
                        for j in range(4):
                            tile = slice(j * P, (j + 1) * P)
                            if kind == 0:
                                left, right = gqk[:, 4 + hd, tile], gqk[:, hd, tile]
                            else:
                                left = right = gf[m % 3][:, tile]
                            ins = mm(bank(m % 3)[:, tile], left, right, start=True, stop=True)
                    else:
                        if hd:
                            pe.wait_ge(sig("g_x"), hd)
                        pairs = ((kx[:, 0], kx[:, 3]), (kx[:, 2], kx[:, 5]), (kx2[:, 0], kx[:, 4]),
                                 (kx2[:, 0], kx2[:, 1]), (kx[:, 1], kx[:, 4]), (kx[:, 1], kx2[:, 1]))
                        for b, (left, right) in enumerate(pairs):
                            ins = mm(ps[:, 3 * BANK + b * P:3 * BANK + (b + 1) * P], left, right,
                                     start=True, stop=True)
                    ins.then_inc(sig("g_mm"), 1)
                m = q - 3
                if 0 <= m < NG and GI[m][1] == 8:
                    hd = GI[m][0]
                    pe.wait_ge(sig("g_x"), hd + 1)
                    pe.wait_ge(sig("g_cp"), 8 * (hd + 1))
                    if hd:
                        pe.wait_ge(sig("g_out"), hd)
                    d, xs = sd[hd % 2], sx[hd % 2]
                    for e in range(2):
                        dst = bank(5 + e)
                        vc = slice((2 * hd + e) * P, (2 * hd + e + 1) * P)
                        plan = [(0, 0, d[:, 0]), (1, 1, d[:, 1]), (2, 2, d[:, 2]), (3, 3, d[:, 3]),
                                (0, 1, xs[:, 0]), (2, 3, xs[:, 1]), (0, 2, xs[:, 2]), (0, 3, xs[:, 3]),
                                (1, 2, xs[:, 4]), (1, 3, xs[:, 5])]
                        for x_, (s_, t_, rhs) in enumerate(plan):
                            ins = mm(dst[:, t_ * P:(t_ + 1) * P], gvt[:, s_, vc], rhs, start=(x_ == 0),
                                     stop=(x_ == len(plan) - 1), skip_group_check=True)
                    ins.then_inc(sig("g_o"), 1)
            for k in range(8):
                pe.wait_ge(sig("gn_sq"), k + 1)
                mm(bank(4 + k // 2), one_col.to_broadcast([P, P]), sq[k % 2][:, 0:SEQ], start=(k % 2 == 0),
                   stop=(k % 2 == 1)).then_inc(sig("gn_used"), 1)
            pe.wait_ge(sig("gy_lo"), 8)
            units(U_MG1, 4, xhi, xlo)
            units(U_GLAO, 4, gyh, gyl)
            units(U_DQ, U_DSAO - U_DQ, xhi, xlo)
            pe.wait_ge(sig("evac2"), U_DSAO - U_GQK)
            for m in range(24):
                j, hd = 1 + m // 8, m % 8
                rows = slice(64 * (hd % 2), 64 * (hd % 2) + 64)
                if m >= 4:
                    pe.wait_ge(sig("ix_relu"), m - 3)
                mm(bank(m % 4)[:, 0:P * (j + 1)], iqf[rows, hd // 2, j * P:(j + 1) * P], ikd[rows, 0:P * (j + 1)],
                   start=True, stop=True).then_inc(sig("ix_dots"), 1)
            pe.wait_ge(sig("ix_relu"), 24)
            for n in range(ND + 3):
                if n < ND:
                    j, hd = DI[n]
                    w = P * (j + 1)
                    if j:
                        pe.wait_ge(sig("mask_ready"), j)
                    if n >= 4:
                        pe.wait_ge(sig("da_max"), n - 3)
                    dst = bank(n % 4)[:, 0:w]
                    mm(dst, dq[:, hd, j * P:(j + 1) * P], ckvf[:, 0:w], start=True, stop=False)
                    mask = mj[:, mj_at[j]:mj_at[j] + w] if j else madd
                    mm(dst, ident[:], mask, start=False, stop=True).then_inc(sig("da_s"), 1)
                m = n - 2
                if 0 <= m < ND:
                    j, hd = DI[m]
                    pe.wait_ge(sig("da_norm"), m + 1)
                    if m >= 2:
                        pe.wait_ge(sig("da_pt"), m - 1)
                    for b in range(j + 1):
                        ins = nc.tensor.transpose(bank(4 + m % 2)[:, b * P:(b + 1) * P],
                                                  dl[m % 3][:, b * P:(b + 1) * P], ident[:])
                    ins.then_inc(sig("da_t"), 1)
                m = n - 3
                if 0 <= m < ND:
                    j, hd = DI[m]
                    pe.wait_ge(sig("da_pt"), m + 1)
                    if m >= 2:
                        pe.wait_ge(sig("da_lo"), m - 1)
                    for b in range(j + 1):
                        ins = mm(bank(6 + m % 2)[:, 0:P], ckvt[:, b, :], dpt[m % 2][:, b * P:(b + 1) * P],
                                 start=(b == 0), stop=(b == j))
                    ins.then_inc(sig("da_o"), 1)
            pe.wait_ge(sig("da_lo"), ND)
            units(U_DSAO, 4, xhi, xlo)
            pe.wait_ge(sig("my_lo"), 4)
            units(U_MIXO, 4, myh, myl)
            norm()
            swiglu(U_F2I, 2)
            norm()
            pe.wait_ge(sig("lo_done"), U_PLEG + 1)
            unit(U_PLEG % 2, SEQ, xhi, xlo, 5 * KC)
            pe.wait_ge(sig("p_in"), 16)
            for k in range(2):
                for j in range(4):
                    ins = nc.tensor.transpose(bank(4 + k)[:, j * P:(j + 1) * P], pin[:, j, k * P:(k + 1) * P], ident[:])
                ins.then_inc(sig("p_turned"), 1)
            for u in range(U_PLEG + 1, U_PLEP):
                pe.wait_ge(sig("lo_done"), u + 1)
                if u >= U_PLEG + 2:
                    pe.wait_ge(sig("pg_evac"), u - U_PLEG - 1)
                unit(u % 2, SEQ, xhi, xlo)
            pe.wait_ge(sig("lo_done"), U_PLEP + 1)
            pe.wait_ge(sig("pg_evac"), 4)
            pe.wait_ge(sig("p_lo"), 2)
            for m in range(KC):
                for kk in range(2):
                    ins = tile_products(U_PLEP % 2, kk * KC + m, [(bank(m), slice(0, SEQ))],
                                        lambda tok: phi[:, kk, tok], lambda tok: plo[:, kk, tok], kk == 0, kk == 1)
                ins.then_inc(sig("ple_done" if m < KC - 1 else "unit_done"), 1)
            pe.wait_ge(sig("ple_added"), 5)
            norm()

            for j in range(4):
                if j >= 2:
                    pe.wait_ge(sig("out_copied"), j - 1)
                for k in range(KC):
                    if j == 0:
                        pe.wait_ge(sig("fin_ready"), k + 1)
                    ins = nc.tensor.transpose(bank(2 * (j % 2), 2)[:, k * P:(k + 1) * P], fin[:, k, j * P:(j + 1) * P],
                                              ident[:])
                ins.then_inc(sig("out_turned"), 1)


_OUTS = [((1, 512, 1024), 'float32')]


def shape_constants():
    r, c = np.arange(P)[:, None], np.arange(P)[None, :]
    q = np.arange(META)[None, :]
    late = r - (P - META)
    masks = np.concatenate([
        -1.0 * (r >= c), NEG * (c > r), NEG * (r >= c),
        np.where((late >= 0) & (late < q), 0.0, NEG), 1.0 * ((late >= 0) & (late < q))], axis=1)
    differ = r ^ c
    gmask = np.concatenate([(differ >= 2 ** b) & (differ < 2 ** (b + 1)) & (r < c) for b in range(7)], axis=1)
    dist = np.maximum(np.arange(640) - (P - 1), 0)
    exact = 16
    large = exact + (np.log(np.maximum(dist, 1).astype(np.float32) / exact) / math.log(128 / exact)
                     * (32 - exact)).astype(np.int32)
    bucket = np.where(dist < exact, dist, np.minimum(large, 31))
    onehot = (np.arange(32)[:, None] == bucket[None, :]).astype(np.float32)
    return np.eye(P, dtype=np.float32), masks.astype(np.float32), np.ascontiguousarray(gmask.astype(np.int8)).view(np.int32), onehot


def kernel(**inputs):
    import numpy as _np
    import concourse.bacc as _bacc
    from concourse import mybir as _mybir
    from concourse.bass_utils import run_bass_kernel_spmd as _run

    v = {k: _np.asarray(a) for k, a in inputs.items()}
    arrays = layout(v)
    nc = _bacc.Bacc("TRN2", target_bir_lowering=False, num_devices=1)
    args = []
    for name, a in list(arrays.items()):
        a = _np.ascontiguousarray(a)
        arrays[name] = a
        args.append(nc.dram_tensor(name, a.shape, _mybir.dt.from_np(a.dtype), kind="ExternalInput").ap())
    for i, (shape, dtype) in enumerate(_OUTS):
        dt = _mybir.dt.from_np(_np.dtype(dtype))
        args.append(nc.dram_tensor(f"out_{i}_dram", shape, dt, kind="ExternalOutput").ap())
    build(nc, *args)
    r = _run(nc, [arrays], core_ids=[0])
    return r.results[0]["out_0_dram"]
```

```python
import math
from contextlib import ExitStack

import numpy as np

import concourse.bass as bass
from concourse import mybir

F32 = mybir.dt.float32
F32R = mybir.dt.float32r
I32 = mybir.dt.int32
ALU = mybir.AluOpType
ACT = mybir.ActivationFunctionType
AX = mybir.AxisListType

P = 128
D = 1024
KC = D // P
META = 16
SEQ = 512
T1 = SEQ + META
HALF = T1 // 2
BANK = 512
FF = 2816
FC = FF // P
EPS = 1e-6
NEG = -1e30
UT = 16

U_PROJ = 0
U_F = U_PROJ + 6
U_QKVB = U_F + 1
U_GATES = U_QKVB + 6
U_O = U_GATES + 8
U_WOUT = U_O + 4
U_UP = U_WOUT + 4
U_DOWN = U_UP + FC
U_END1 = U_DOWN + FC // 2
U_F1I = U_END1
U_F1O = U_F1I + FC
U_GQK = U_F1O + FC // 2
U_GV = U_GQK + 4
U_SPC = U_GV + 4
U_GR = U_SPC + 2
U_MG1 = U_GR + 4
U_GLAO = U_MG1 + 4
U_IQ = U_GLAO + 4
U_DQ = U_IQ + 2
U_MG2 = U_DQ + 4
U_DSAO = U_MG2 + 4
U_MIXO = U_DSAO + 4
U_F2I = U_MIXO + 4
U_F2O = U_F2I + FC
U_PLEG = U_F2O + FC // 2
U_PLEP = U_PLEG + 4
U_END = U_PLEP + 1

(G_PRE, G_MIX, G_FFN, G_POST, G_F1, G_MIX2, G_GLA, G_F2, G_PLE, G_FIN) = range(0, 80, 8)
C_CKV = 80
C_AB = 81
C_CW = 85
C_CB = C_CW + 3 * 2 * FC
C_BF = C_CB + 2 * FC
C_N = C_BF + 1


class Count:

    def __init__(self, eng, sem):
        self.eng, self.sem, self.n, self.turn = eng, sem, 0, 0

    def up(self, ins):
        ins.then_inc(self.sem, 1)
        self.n += 1
        return self.n

    def wait(self, value=None):
        self.eng.wait_ge(self.sem, self.turn + (self.n if value is None else value))

    def enter(self, turns_done, per_turn):
        self.first, self.per = self.n, per_turn
        self.turn = turns_done * per_turn

    def leave(self, turns):
        assert self.n == self.first + self.per
        self.n, self.turn = self.first + self.per * turns, 0


def std_units(w, starts):
    tiles = w.reshape(KC, P, w.shape[1])
    cut = [tiles[:, :, s:s + P] for s in starts]
    both = [np.stack(cut[i:i + 2]) for i in range(0, len(cut), 2)]
    return [np.ascontiguousarray(b.transpose(2, 0, 1, 3)).reshape(1, P, UT * P) for b in both]


def down_units(w):
    v = w.reshape(w.shape[0] // (2 * P), 2, P, D).transpose(0, 2, 1, 3)
    return [np.ascontiguousarray(v).reshape(-1, P, UT * P)]


def run_of(start, n):
    return [start + P * i for i in range(n)]


def pairs_up(w):
    starts = []
    for i in range(0, FC, 2):
        starts += [P * i, P * i + P, FF + P * i, FF + P * i + P]
    return std_units(w, starts)


def columns(v):
    return np.asarray(v).reshape(-1, P).T


def layout(v):
    w = v["w_in"][0]
    units = std_units(w, run_of(0, 12)) + std_units(w, [1536, 1536])
    units += std_units(w, run_of(1544, 28))
    units += std_units(np.concatenate([v["w_o_fox"][0], v["w_o_sb"][0]]), run_of(0, 8))
    units += std_units(v["w_out"][0], run_of(0, 8))
    units += pairs_up(v["w_up"][0]) + down_units(v["w_down"][0])
    units += pairs_up(v["ffn1_w_in_2"][0]) + down_units(v["ffn1_w_out_2"][0])
    w = v["mix_w_in_2"][0]
    units += std_units(w, run_of(0, 16))
    units += std_units(w, [3072, 4112, 4752, 4688])
    units += std_units(w, run_of(2048, 8))
    units += std_units(w, run_of(4824, 8))
    units += std_units(v["gla_w_out_2"][0], run_of(0, 8))
    units += std_units(w, run_of(4240, 4)) + std_units(w, run_of(3088, 8))
    units += std_units(w, run_of(5848, 8))
    units += std_units(v["dsa_w_out_2"][0], run_of(0, 8))
    units += std_units(v["mix_w_out_2"][0], run_of(0, 8))
    units += pairs_up(v["ffn2_w_in_2"][0]) + down_units(v["ffn2_w_out_2"][0])
    units += std_units(v["ple_w_gate_2"][0], run_of(0, 8)) + down_units(v["ple_w_proj_2"][0])
    stream = np.concatenate(units)
    assert stream.shape[0] == U_END
    if U_END % 2:
        stream = np.concatenate([stream, np.zeros((1, P, UT * P), np.float32)])
    g = v["norm_gains"][0]
    bf = np.zeros((P, 1), np.float32)
    bf[0:8, 0] = v["b_forget"][0]
    gains = [g[0], g[1], g[2], g[3], v["ffn1_norm_2"][0], v["mix_norm_2"][0], v["gla_out_norm_2"][0],
             v["ffn2_norm_2"][0], v["ple_norm_2"][0], v["final_norm_2"]]
    cvec = np.concatenate([columns(a) for a in gains] + [columns(v["ckv_norm_2"][0]), columns(v["gla_alpha_b_2"][0])]
                          + [columns(v["conv_w"][0][t]) for t in range(3)] + [columns(v["conv_b"][0]), bf], axis=1)
    ident, masks, gmask, onehot = shape_constants()
    return {"wstream": stream, "x": v["x"], "meta": v["meta_tokens"], "cvec": cvec,
            "alpha_w": v["gla_alpha_w_2"][0], "rel_bias": v["rel_bias_2"], "p2": v["p_2"],
            "ident_c": ident, "masks_c": masks, "gmask_c": gmask, "onehot_c": onehot}


def build(nc, wstream, x, meta, cvec, alpha_w, rel_bias, p2, ident_c, masks_c, gmask_c, onehot_c, out):
    n_units = wstream.shape[0]
    with ExitStack() as ctx:
        signals = {}

        def sig(name):
            if name not in signals:
                signals[name] = ctx.enter_context(nc.semaphore(name))
            return signals[name]

        place = {"at": 16512}

        def at(name, shape, dt=F32, offset=None):
            size = int(np.prod(shape[1:])) * 4
            if offset is None:
                offset = place["at"]
                place["at"] += (size + 31) // 32 * 32
            return nc.alloc_sbuf_tensor_at(name, list(shape), dt, offset=offset)

        raw = [at(f"raw{b}", [P, UT * P]) for b in range(2)]
        whi = [at(f"whi{b}", [P, UT * P], F32R) for b in range(2)]
        wlo = [at(f"wlo{b}", [P, UT * P], F32R) for b in range(2)]
        h = at("h", [P, KC, T1])
        x_at = place["at"]
        xhi = at("xhi", [P, KC, T1], F32R)
        xlo = at("xlo", [P, KC, T1], F32R)
        arena = place["at"]
        place["at"] += 2 * FC * SEQ * 4
        ident = at("ident", [P, P])
        masks_at = place["at"]
        masks = at("masks", [P, 3 * P + META])
        cv = at("cv", [P, C_N])
        per = at("per", [P, 48])
        small = per[:, 42:45]
        ident_r = at("ident_r", [P, P], F32R)
        temp = place["at"]
        room = 229368 - temp

        ntri = masks[:, 0:P]
        masks_r = at("masks_r", [P, 2 * P + META], F32R, offset=masks_at + 4 * P)
        madd = masks_r[:, 0:P]
        madds = masks_r[:, P:2 * P]
        madds_tail = masks_r[:, 2 * P:2 * P + META]
        one_col = small[:, 0:1]
        neg_col = small[:, 1:2]
        eps_col = small[:, 2:3]

        ps = ctx.enter_context(nc.psum_tensor("ps", [P, 8 * BANK], F32))
        regions = ps[:].rearrange("p (r c) -> p r c", c=2 * BANK)
        LO = BANK - HALF

        def chunks1(b, n=2):
            return regions[:, 2 * b:2 * b + n, LO:LO + T1]

        def bank(i, n=1):
            return ps[:, i * BANK:(i + n) * BANK]

        xin = at("xin", [P, 4, D], offset=arena)
        xmeta = at("xmeta", [META, D], offset=arena + 4 * 4 * D)
        qkf = at("qkf", [P, 8, T1], offset=arena)
        qkb = at("qkb", [P, 8, T1], offset=arena + 32 * T1)
        v_at = arena + 64 * T1
        vf = at("vf", [P, 4, BANK], offset=v_at)
        vf_tail = at("vf_tail", [META, BANK], offset=v_at + 8192)
        vb = at("vb", [P, 5, BANK], offset=v_at + 10240)
        gates = at("gates", [P, 16, T1], offset=v_at + 20480)
        fz, fa, fl, fm = [at(f"forget{i}", [8, T1], offset=v_at + 20480 + 4 * T1 * i) for i in range(4)]
        vfm = at("vfm", [P, 4, T1], offset=temp)
        vbm = at("vbm", [P, 4, T1], offset=temp + 16 * T1)
        negc = at("negc", [8, T1], offset=temp + 32 * T1)
        fox_p = [at(f"fox_p{i}", [P, T1], offset=temp + 4 * T1 * i) for i in range(3)]
        fox_pt = [at(f"fox_pt{i}", [P, BANK], offset=temp + 12 * T1 + 2048 * i) for i in range(2)]
        fox_c = at("fox_c", [P, 3, 40], offset=temp + 12 * T1 + 4096)
        ncb = [at(f"ncb{i}", [P, 4, T1], offset=x_at + 16 * T1 + 32 * T1 * i) for i in range(2)]
        sb_l = [at(f"sb_l{i}", [P, BANK], offset=temp + 2048 * i) for i in range(3)]
        sb_p = [at(f"sb_p{i}", [P, BANK], offset=temp + 6144 + 2048 * i) for i in range(3)]
        sb_a = [at(f"sb_a{i}", [P, BANK], offset=temp + 12288 + 2048 * i) for i in range(2)]
        yhi = at("yhi", [P, KC, T1], F32R, offset=arena)
        ylo = at("ylo", [P, KC, T1], F32R, offset=arena + 32 * T1)
        yt = [at(f"yt{i}", [P, T1], offset=temp + 4 * T1 * i) for i in range(4)]
        mix = at("mix", [P, KC, T1], offset=x_at)
        sq = [at(f"sq{i}", [P, T1], offset=temp + 4 * T1 * i) for i in range(2)]
        nt = [at(f"nt{i}", [P, T1], offset=temp + 4 * T1 * (2 + i)) for i in range(3)]
        sq_sum = at("sq_sum", [P, T1], offset=temp + 4 * T1 * 8)
        root = [at(f"root{i}", [P, T1], offset=temp + 4 * T1 * (5 + i)) for i in range(3)]
        hhi = at("hhi", [P, FC, SEQ], F32R, offset=arena)
        hlo = at("hlo", [P, FC, SEQ], F32R, offset=arena + 4 * FC * SEQ)
        cg = at("cg", [P, 2, SEQ], offset=temp)
        gact = at("gact", [P, 2, SEQ], offset=temp + 4096)
        cvl = at("cvl", [P, 2, SEQ], offset=temp + 8192)
        fin = at("fin", [P, KC, SEQ], offset=arena)
        outb = [at(f"outb{i}", [P, D], offset=arena + 4 * KC * SEQ + 4096 * i) for i in range(4)]
        assert room >= 19008, room
        gqk = at("gqk", [P, 8, SEQ], offset=arena)
        gvt = at("gvt", [P, 4, D], offset=arena + 16384)
        gvf = at("gvf", [P, 8, SEQ], offset=arena + 32768)
        gout = at("gout", [P, 8, SEQ], offset=arena + 32768)
        grs = at("grs", [P, 8, SEQ], offset=arena + 49152)
        nbt = at("nbt", [P, 4, SEQ], offset=arena + 65536)
        bucket = at("bucket", [32, 640], offset=arena + 65536)
        relb = at("relb", [32, 8], offset=arena + 68096)
        brow = at("brow", [8, 640], offset=arena + 68608)
        ckvf = at("ckvf", [P, SEQ], offset=arena + 73728)
        ckvt = at("ckvt", [P, 4, P], offset=arena + 75776)
        dkvf = at("dkvf", [P, SEQ], offset=arena + 77824)
        ikd = at("ikd", [P, SEQ], offset=arena + 79872)
        gaf = at("gaf", [META, SEQ], offset=arena + 81920)
        iwf = at("iwf", [P, SEQ], offset=arena + 83968)
        aw = at("aw", [META, SEQ], offset=arena + 86016)
        kx = at("kx", [P, 6, P], offset=arena + 86016)
        kx2 = at("kx2", [P, 2, P], offset=arena + 89088)
        ax = at("ax", [P, 4, SEQ], offset=temp)
        al = at("al", [P, 4, SEQ], offset=temp + 8192)
        restart = at("restart", [P, SEQ], offset=temp + 16384)
        gf = [at(f"gf{i}", [P, SEQ], offset=temp + 2048 * i) for i in range(3)]
        sd = [at(f"sd{i}", [P, 4, P], offset=temp + 6144 + 5120 * i) for i in range(2)]
        sx = [at(f"sx{i}", [P, 6, P], offset=temp + 8192 + 5120 * i) for i in range(2)]
        ga_m = at("ga_m", [P, 4 * P], mybir.dt.int8, offset=masks_at)
        gb_m = at("gb_m", [P, 3 * P], mybir.dt.int8, offset=masks_at + 1024)
        gyh = at("gyh", [P, 8, SEQ], F32R, offset=arena)
        gyl = at("gyl", [P, 8, SEQ], F32R, offset=arena + 16384)
        g1 = at("g1", [P, 8, SEQ], offset=arena + 32768)
        dq = at("dq", [P, 8, SEQ], offset=arena)
        g2 = at("g2", [P, 8, SEQ], offset=arena + 16384)
        iqf = at("iqf", [P, 4, SEQ], offset=arena + 49152)
        bias = at("bias", [P, 8, SEQ], offset=arena + 57344)
        mj = at("mj", [P, 10 * P], F32R, offset=arena + 81920)
        mj_at = [0, P, 3 * P, 6 * P]
        acc = [at(f"acc{i}", [P, SEQ], offset=temp + 2048 * i) for i in range(2)]
        rl = [at(f"rl{i}", [P, SEQ], offset=temp + 4096 + 2048 * i) for i in range(7)]
        dl = [at(f"dl{i}", [P, SEQ], offset=temp + 2048 * i) for i in range(3)]
        dpt = [at(f"dpt{i}", [P, SEQ], offset=temp + 6144 + 2048 * i) for i in range(2)]
        dst_ = at("dst", [P, 3, 32], offset=temp + 10240)
        myh = at("myh", [P, 8, SEQ], F32R, offset=arena + 49152)
        myl = at("myl", [P, 8, SEQ], F32R, offset=arena + 65536)
        dt_ = [at(f"dt{i}", [P, 2, SEQ], offset=temp + 4096 * i) for i in range(2)]
        pin = at("pin", [P, 4, 256], offset=arena + 16384)
        phi = at("phi", [P, 2, SEQ], F32R, offset=arena + 20480)
        plo = at("plo", [P, 2, SEQ], F32R, offset=arena + 24576)
        sgp = at("sgp", [P, 8, SEQ], offset=arena + 32768)
        iwt = per[:, 0:32]
        m8 = per[:, 32:40]
        ex = per[:, 40:42]
        scratch = nc.dram_tensor("bias_rows", (8, 640), F32)
        GI = [(hd, kind) for hd in range(4) for kind in range(9)]
        NG = len(GI)
        DI = [(j, hd) for j in range(4) for hd in range(8)]
        ND = len(DI)

        def cross_of(hd):
            return 9 * hd + 8

        def diag_seen(q):
            return sum(1 for x in range(q + 1) if GI[x][1] < 8)


        ITEMS = [(head, i) for head in range(8) for i in range(5)]
        NI = len(ITEMS)

        def item(n):
            head, i = ITEMS[n]
            r = 64 * (head % 2)
            if i < 4:
                return head, slice(r, r + 64), head // 2, i, P * i, P, P * (i + 1)
            return head, slice(r, r + 64), head // 2, i, SEQ, META, T1

        def sb_width(n):
            i = ITEMS[n][1]
            return P * (i + 1) if i < 4 else 5 * META

        def gr_bank(c):
            return bank(3 - c if c < 2 else 7)

        def side_at(c):
            return min(8 * ((c + 3) // 4) - 1, 23)

        def out_banks(j):
            return bank((0, 2, 6, 0)[j], 2)

        def pair(ap):
            return ap.rearrange("p (c n) -> p c n", c=2)

        def norm_places(n):
            T, at_ = NORMS[n]
            if T == T1:
                scale = regions[:, at_, LO:LO + T1]
                return scale, [slice(0, HALF), slice(HALF, T1)]
            return bank(at_), [slice(0, SEQ)]

        up0, f1, g2_, pl = U_UP % 2, U_F1I % 2, U_GQK % 2, U_PLEG % 2
        NORMS = [(T1, 2), (T1, 2 * up0), (T1, 2 * (1 - up0)), (SEQ, 2 * (1 - f1)), (SEQ, 2 * (1 - f1) + 1),
                 (SEQ, 2 * (1 - g2_)), (SEQ, 4), (SEQ, 2 * (1 - pl))]
        BY_PE = [0, 2, 4]
        BY_ADDING = [1, 3, 5, 6, 7, 8]

        block = ctx.enter_context(nc.Block())

        @block.sync
        def _(sp):
            sp.dma_start(ident[:], ident_c).then_inc(sig("ident_in"), 16)
            sp.dma_start(xmeta[:], meta).then_inc(sig("x_in0"), 16)
            for side in range(2):
                cols = slice(side * (D // 2), (side + 1) * (D // 2))
                for j in range(4):
                    sp.dma_start(xin[:, j, cols], x[0, j * P:(j + 1) * P, cols]).then_inc(sig(f"x_in{side}"), 16)
            sp.dma_start(raw[0][:], wstream[0]).then_inc(sig("raw_ready0"), 16)
            sp.dma_start(cv[:], cvec).then_inc(sig("const_in"), 16)
            sp.dma_start(raw[1][:], wstream[1]).then_inc(sig("raw_ready1"), 16)
            sp.dma_start(masks[:], masks_c).then_inc(sig("const_in"), 16)
            with sp.Fori(1, n_units // 2) as i:
                for b in range(2):
                    sp.wait_ge(sig("lo_done"), i * 2 + (b - 1))
                    sp.dma_start(raw[b][:], wstream[bass.ds(i * 2 + b, 1)].rearrange("u p n -> (u p) n")
                                 ).then_inc(sig(f"raw_ready{b}"), 16)
            for j in range(4):
                sp.wait_ge(sig("out_odd" if j % 2 else "out_even"), j // 2 + 1)
                sp.dma_start(out[0, j * P:(j + 1) * P, :], outb[j][:]).then_inc(sig("stored"), 16)
            sp.wait_ge(sig("stored"), 64)

        @block.gpsimd
        def _(pool):
            with pool.Fori(0, n_units // 2) as i:
                for b in range(2):
                    pool.wait_ge(sig("hi_done"), i * 2 + (b + 1))
                    nc.gpsimd.tensor_tensor(wlo[b][:], raw[b][:], whi[b][:].bitcast(F32), ALU.subtract
                                            ).then_inc(sig("lo_done"), 1)

            for k in range(1, KC):
                pool.wait_ge(sig("sq_done"), 8 * 8 + k + 1)
                if k >= 2:
                    pool.wait_ge(sig("sq_added"), 7 * BY_ADDING.index(8) + k - 1)
                nc.gpsimd.tensor_tensor(sq_sum[:, 0:SEQ], sq_sum[:, 0:SEQ], sq[k % 2][:, 0:SEQ], ALU.add
                                        ).then_inc(sig("sq_added"), 1)

        @block.scalar
        def _(act):
            step = Count(act, sig("act_step"))
            norms, roots = [0], [0]

            def weights_hi(b, pair, first=False):
                act.wait_ge(sig(f"raw_ready{b}"), pair * 16 + 16)
                if not first:
                    act.wait_ge(sig("unit_done"), pair * 2 + (b - 1))
                nc.scalar.copy(whi[b][:], raw[b][:]).then_inc(sig("hi_done"), 1)

            def hi_of(u):
                if u < n_units:
                    weights_hi(u % 2, u // 2, u < 2)

            def rsqrt_of(total, share):
                n = roots[0]
                roots[0] += 1
                y = root[n % 2][:, 0:total.shape[-1]]
                nc.scalar.activation(y, total, ACT.Ln, bias=eps_col, scale=share).then_inc(sig("log_done"), 1)
                act.wait_ge(sig("log_done"), n + 1)
                nc.scalar.activation(y, y, ACT.Exp, scale=-0.5).then_inc(sig("root_done"), 1)

            def squares(view, T, wait_source, late=None):
                n = norms[0]
                norms[0] += 1
                if n not in (2, 4):
                    nc.scalar.preload_act_table_set("natural_log_exp_and_others")
                for k in range(KC):
                    wait_source(k)
                    dst = sq[k % 2]
                    if n in BY_PE:
                        if k >= 2:
                            act.wait_ge(sig("sq_used"), 7 * BY_PE.index(n) + k - 1)
                    elif k == 0:
                        dst = sq_sum
                    elif k >= 3:
                        act.wait_ge(sig("sq_added"), 7 * BY_ADDING.index(n) + k - 2)
                    nc.scalar.activation(dst[:, 0:T], view(k), ACT.Square).then_inc(sig("sq_done"), 1)
                if late is not None:
                    hi_of(late)
                act.wait_ge(sig("total_done"), n + 1)
                total, _ = norm_places(n)
                rsqrt_of(total, 1.0 / D)

            def split_x(base, T, late=None):
                for k in range(KC):
                    if k == KC // 2 and late is not None:
                        hi_of(late)
                    act.wait_ge(sig("nt_ready"), base + k + 1)
                    nc.scalar.copy(xhi[:, k, 0:T], nt[k % 3][:, 0:T]).then_inc(sig("xhi_ready"), 1)

            def out_hi(n, o_base, chunk0):
                head, rows, c, i, t0, tw, _ = item(n)
                act.wait_ge(sig("o_done"), o_base + n + 1)
                nc.scalar.copy(xhi[rows, chunk0 + c, t0:t0 + tw], bank(6 + n % 2)[rows, 0:tw]
                               ).then_inc(sig("o_hi"), 1)

            squares(lambda k: h[:, k, :], T1, lambda k: act.wait_ge(sig("h_ready"), k + 1), 0)
            split_x(0, T1, 1)
            act.wait_ge(sig("const_in"), 32)
            act.wait_ge(sig("ident_in"), 16)
            nc.scalar.copy(ident_r[:], ident[:]).then_inc(sig("exact_r"), 1)
            nc.scalar.copy(masks_r[:], masks[:, P:]).then_inc(sig("exact_r"), 1)
            for u in range(U_PROJ, U_O):
                hi_of(u + 2)
                if u == U_F + 1:
                    nc.scalar.preload_act_table_set("natural_log_exp_and_others")
                    act.wait_ge(sig("f_z"), 1)
                    nc.scalar.activation(fa[:], fa[:], ACT.Exp).then_inc(sig("f_ln"), 1)
                    act.wait_ge(sig("f_ln"), 1)
                    nc.scalar.activation(fl[:], fa[:], ACT.Ln, bias=one_col[0:8]).then_inc(sig("f_ln"), 1)
                if u >= U_GATES:
                    i = u - U_GATES
                    act.wait_ge(sig("c_ready"), 1)
                    act.wait_ge(sig("evac"), u)
                    act.wait_ge(sig("unit_done"), u + 1)
                    nc.scalar.activation(gates[:, 2 * i:2 * i + 2, :], chunks1(u % 2), ACT.Sigmoid
                                         ).then_inc(sig("evac"), 1)
            nc.scalar.preload_act_table_set("natural_log_exp_and_others")
            act.wait_ge(sig("v_ready"), 10)

            for head in range(8):
                act.wait_ge(sig("c_spread"), head + 1)
                nc.scalar.copy(ncb[head // 4][:, head % 4, :], regions[:, head % 4, LO:LO + T1]
                               ).then_inc(sig("c_copied"), 1)
            for n in range(NI + 3):
                m = n - 2
                if 0 <= m < NI:
                    i = ITEMS[m][1]
                    act.wait_ge(sig("fox_t"), m + 1)
                    if m >= 2:
                        act.wait_ge(sig("o_done"), m - 1)
                    if i < 4:
                        nc.scalar.copy(fox_pt[m % 2][:, 0:P * (i + 1)], bank(4 + m % 2)[:, 0:P * (i + 1)]
                                       ).then_inc(sig("fox_pt"), 1)
                    else:
                        step.up(nc.scalar.copy(fox_pt[m % 2][:, 0:64], bank(4 + m % 2)[:, 0:64]))
                        nc.scalar.copy(fox_pt[m % 2][0:META, 64:80], bank(4 + m % 2)[0:META, 64:80]
                                       ).then_inc(sig("fox_pt"), 1)
                if n < NI:
                    head, rows, c, i, t0, tw, w = item(n)
                    base = (n % 2) * 2 * BANK + (BANK if i < 4 else BANK - META)
                    act.wait_ge(sig("fox_max"), n + 1)
                    if n >= 3:
                        act.wait_ge(sig("fox_t"), n - 2)
                    nc.scalar.activation(fox_p[n % 3][0:tw, 0:w], ps[0:tw, base:base + w], ACT.Exp,
                                         bias=fox_c[0:tw, 0, n:n + 1], accum_out=fox_c[0:tw, 1, n:n + 1]
                                         ).then_inc(sig("fox_exp"), 1)
                m = n - 3
                if 0 <= m < NI:
                    out_hi(m, 0, 0)
            for n in range(NI + 3):
                m = n - 2
                if 0 <= m < NI:
                    w = sb_width(m)
                    act.wait_ge(sig("sb_acc"), m + 1)
                    if m >= 2:
                        act.wait_ge(sig("o_done"), NI + m - 1)
                    nc.scalar.activation(sb_a[m % 2][:, 0:w], bank(m % 6)[:, 0:w], ACT.Exp
                                         ).then_inc(sig("sb_a"), 1)
                if n < NI:
                    w = sb_width(n)
                    act.wait_ge(sig("sb_abs"), n + 1)
                    logs = sb_l[n % 3][:, 0:w]
                    step.up(nc.scalar.activation(logs, logs, ACT.Exp))
                    step.wait()
                    nc.scalar.activation(logs, logs, ACT.Ln, bias=one_col).then_inc(sig("sb_l"), 1)
                m = n - 3
                if 0 <= m < NI:
                    out_hi(m, NI, 4)
            for m in range(8):
                if m % 2 == 1:
                    hi_of(U_O + m // 2 + 2)
                act.wait_ge(sig("y_sum"), m + 1)
                nc.scalar.copy(yhi[:, m, :], yt[2 * (m % 2)][:]).then_inc(sig("y_hi"), 1)
            for u in range(U_WOUT, U_UP - 1):
                hi_of(u + 2)
            squares(lambda k: mix[:, k, :], T1, lambda k: act.wait_ge(sig("mix_ready"), k // 2 + 1), U_UP + 1)
            squares(lambda k: h[:, k, :], T1, lambda k: act.wait_ge(sig("res_ready"), k + 1))
            split_x(8, T1)

            def hidden_act(i, first, unit0, done, func):
                b = unit0 % 2
                weights_hi(b, i + ((unit0 - b) // 2 + 1))
                act.wait_ge(sig("gate_ready"), i + (done + 1))
                if not first:
                    act.wait_ge(sig("prod"), i + done)
                return func(i)

            def conv_gate(i):
                nc.scalar.activation(gact[:], cg[:], ACT.Gelu_apprx_tanh).then_inc(sig("gate_act"), 1)

            def hidden_hi(i, unit0, done):
                b = (unit0 + 1) % 2
                weights_hi(b, i + ((unit0 + 1 - b) // 2 + 1))
                act.wait_ge(sig("prod"), i + (done + 1))
                nc.scalar.copy(hhi[:, bass.ds(i * 2, 2), :], cvl[:]).then_inc(sig("hid_hi"), 1)

            hidden_act(0, True, U_UP, 0, conv_gate)
            hidden_hi(0, U_UP, 0)
            with act.Fori(1, FC // 2) as i:
                hidden_act(i, False, U_UP, 0, conv_gate)
                hidden_hi(i, U_UP, 0)
            for u in range(U_DOWN, U_END1 - 1):
                hi_of(u + 2)
            squares(lambda k: mix[:, k, 0:SEQ], SEQ, lambda k: act.wait_ge(sig("down_evac"), k + 1), U_END1 + 1)

            hview = lambda k: h[:, k, META:T1]
            squares(hview, SEQ, lambda k: act.wait_ge(sig("res_ready"), KC + k + 1))
            split_x(2 * KC, SEQ)

            def swiglu(unit0, layer):
                done = layer * (FC // 2)
                b = unit0 % 2

                def silu(i):
                    nc.scalar.activation(gact[:], pair(bank(2 * b, 2)), ACT.Silu).then_inc(sig("gate_act"), 1)

                def one(i, first):
                    weights_hi(b, i + ((unit0 - b) // 2 + 1))
                    act.wait_ge(sig("unit_done"), i * 2 + (unit0 + 1))
                    if not first:
                        act.wait_ge(sig("prod"), i + done)
                    silu(i)
                    hidden_hi(i, unit0, done)

                one(0, True)
                with act.Fori(1, FC // 2) as i:
                    one(i, False)
                for u in range(unit0 + FC, unit0 + FC + FC // 2 - 1):
                    hi_of(u + 2)

            swiglu(U_F1I, 1)
            squares(hview, SEQ, lambda k: act.wait_ge(sig("down_evac"), KC + k + 1), U_GQK + 1)
            act.wait_ge(sig("unit_done"), U_GQK)
            act.dma_start(bucket[:], onehot_c).then_inc(sig("aux_in"), 16)
            act.dma_start(relb[:], rel_bias).then_inc(sig("aux_in"), 16)
            act.dma_start(aw[:], alpha_w).then_inc(sig("aux_in"), 16)
            act.dma_start(ga_m[:].bitcast(mybir.dt.int32), gmask_c[:, 0:P]).then_inc(sig("aux_in"), 16)
            act.dma_start(gb_m[:].bitcast(mybir.dt.int32), gmask_c[:, P:7 * P // 4]).then_inc(sig("aux_in"), 16)
            split_x(3 * KC, SEQ)

            def in_order(u):
                act.wait_ge(sig("unit_done"), u + 1)
                if u > U_GQK:
                    act.wait_ge(sig("evac2"), u - U_GQK)

            def side_out(u0, c, dst, src, func, scale=1.0):
                if c % 2 == 0:
                    act.wait_ge(sig("side_half"), (0 if u0 == U_GR else 4) + c // 2 + 1)
                    nc.scalar.activation(dst, src, func, scale=scale).then_inc(sig("side_out"), 1)
                else:
                    act.wait_ge(sig("unit_done"), u0 + c // 2 + 1)
                    nc.scalar.activation(dst, src, func, scale=scale).then_inc(sig("evac2"), 1)
                    hi_of(u0 + c // 2 + 2)

            for u in range(U_GQK, U_GR):
                hi_of(u + 2)
            act.wait_ge(sig("brow_ready"), 1)
            act.dma_start(scratch.ap(), brow[:]).then_inc(sig("brow_out"), 16)
            act.wait_ge(sig("evac2"), U_GR - U_GQK)
            nc.scalar.preload_act_table_set("natural_log_exp_and_others")
            nc.scalar.activation(sq[0][:, 0:SEQ], dkvf[:], ACT.Square).then_inc(sig("ckv_sq"), 1)
            act.wait_ge(sig("ckv_sums"), 1)
            rsqrt_of(bank(1), 1.0 / P)
            act.wait_ge(sig("decay_x"), 1)
            act.wait_ge(sig("brow_out"), 16)
            step.up(nc.scalar.activation(al[:], al[:], ACT.Exp))
            step.wait()
            nc.scalar.activation(al[:], al[:], ACT.Ln, bias=one_col).then_inc(sig("decay_ln"), 1)
            for c in range(2):
                side_out(U_GR, c, grs[:, c, :], gr_bank(c), ACT.Copy)
            for q in range(NG + 4):
                if q % 6 == 1 and q > 1:
                    c = q // 6 + 1
                    side_out(U_GR, c, grs[:, c, :], gr_bank(c), ACT.Copy)
                if q == NG:
                    act.wait_ge(sig("evac2"), U_GR + 3 - U_GQK)
                    act.wait_ge(sig("side_out"), 3)
                    nc.scalar.activation(grs[:, 0:6, :], grs[:, 0:6, :], ACT.Silu).then_inc(sig("grs_done"), 1)
                if q < NG:
                    hd, kind = GI[q]
                    if kind:
                        act.wait_ge(sig("g_d"), q - hd)
                    if kind == 8:
                        step.up(nc.scalar.activation(ex[:, 0:1], nbt[:, hd, 2 * P - 1:2 * P], ACT.Exp, scale=-1.0))
                        step.up(nc.scalar.activation(ex[:, 1:2], nbt[:, hd, 3 * P - 1:3 * P], ACT.Exp, scale=-1.0))
                        nc.scalar.activation(kx[:], kx[:], ACT.Exp).then_inc(sig("g_e"), 1)
                    elif kind:
                        nc.scalar.activation(gf[q % 3][:], gf[q % 3][:], ACT.Exp).then_inc(sig("g_e"), 1)
                m = q - 2
                if 0 <= m < NG and GI[m][1] == 8:
                    hd = GI[m][0]
                    act.wait_ge(sig("g_mm"), m + 1)
                    if hd >= 2:
                        act.wait_ge(sig("g_o"), hd - 1)
                    nc.scalar.copy(sx[hd % 2][:], ps[:, 3 * BANK:3 * BANK + 6 * P].rearrange("p (b c) -> p b c", c=P)
                                   ).then_inc(sig("g_x"), 1)
                m = q - 3
                if 0 <= m < NG and GI[m][1] == 8:
                    hd = GI[m][0]
                    act.wait_ge(sig("g_o"), hd + 1)
                    nc.scalar.copy(gout[:, 2 * hd:2 * hd + 2, :], pair(bank(5, 2))).then_inc(sig("g_out"), 1)
            act.wait_ge(sig("evac2"), U_MG1 - U_GQK)
            act.wait_ge(sig("side_out"), 4)
            nc.scalar.activation(grs[:, 6:8, :], grs[:, 6:8, :], ACT.Silu).then_inc(sig("grs_done"), 1)
            nc.scalar.preload_act_table_set("natural_log_exp_and_others")
            act.wait_ge(sig("g_out"), 4)
            for k in range(8):
                if k >= 2:
                    act.wait_ge(sig("gn_used"), k - 1)
                nc.scalar.activation(sq[k % 2][:, 0:SEQ], gout[:, k, :], ACT.Square).then_inc(sig("gn_sq"), 1)
            for k in range(-2, 8):
                if k >= 0:
                    act.wait_ge(sig("gy_ready"), k + 1)
                    nc.scalar.copy(gyh[:, k, :], nt[k % 3][:, 0:SEQ]).then_inc(sig("gy_hi"), 1)
                hd = k + 2 if k < 0 else k // 2 + 2
                if k < 0 or (k % 2 == 1 and hd < 4):
                    act.wait_ge(sig("gn_used"), 2 * hd + 2)
                    rsqrt_of(bank(4 + hd), 1.0 / 256)
                if k == 2:
                    hi_of(U_MG1 + 2)
            for u in range(U_MG1, U_DQ):
                if u > U_MG1:
                    hi_of(u + 2)
                if u < U_GLAO:
                    i = u - U_MG1
                    in_order(u)
                    if u == U_MG1:
                        act.wait_ge(sig("gy_lo"), 8)
                    nc.scalar.activation(g1[:, 2 * i:2 * i + 2, :], pair(bank(2 * i, 2)), ACT.Sigmoid
                                         ).then_inc(sig("evac2"), 1)
                if u == U_IQ:
                    act.wait_ge(sig("brow_out"), 16)
                    for hd in range(8):
                        rows = bass.AP(tensor=scratch, offset=hd * 640, ap=[[1, P], [1, SEQ]])
                        act.dma_start(bias[:, hd, :], rows).then_inc(sig("bias_in"), 16)

            def beside_indexer(c):
                if c < 8:
                    side_out(U_DQ, c, dq[:, c, :], bank(4 + c % 4), ACT.Copy, float(np.float32(P ** -0.5)))
                else:
                    side_out(U_DQ, c, g2[:, c - 8, :], bank(4 + c % 4), ACT.Sigmoid)

            for m in range(24):
                for c in range(16):
                    if side_at(c) == m - 1:
                        beside_indexer(c)
                j, hd = 3 - m // 8, m % 8
                act.wait_ge(sig("ix_dots"), m + 1)
                if m >= 7:
                    act.wait_ge(sig("ix_acc"), m - 6)
                nc.scalar.activation(rl[m % 7][:, 0:P * (j + 1)], bank(m % 4)[:, 0:P * (j + 1)], ACT.Relu
                                     ).then_inc(sig("ix_relu"), 1)
            for c in range(16):
                if side_at(c) == 23:
                    beside_indexer(c)
            act.wait_ge(sig("mask_ready"), 3)
            for n in range(ND + 3):
                m = n - 2
                if 0 <= m < ND:
                    w = P * (DI[m][0] + 1)
                    act.wait_ge(sig("da_t"), m + 1)
                    if m >= 2:
                        act.wait_ge(sig("da_o"), m - 1)
                    nc.scalar.copy(dpt[m % 2][:, 0:w], bank(4 + m % 2)[:, 0:w]).then_inc(sig("da_pt"), 1)
                if n < ND:
                    w = P * (DI[n][0] + 1)
                    act.wait_ge(sig("da_max"), n + 1)
                    nc.scalar.activation(dl[n % 3][:, 0:w], dl[n % 3][:, 0:w], ACT.Exp, bias=dst_[:, 0, n:n + 1],
                                         accum_out=dst_[:, 1, n:n + 1]).then_inc(sig("da_exp"), 1)
                m = n - 3
                if 0 <= m < ND:
                    j, hd = DI[m]
                    act.wait_ge(sig("da_o"), m + 1)
                    nc.scalar.copy(xhi[:, hd, j * P:(j + 1) * P], bank(6 + m % 2)[:, 0:P]).then_inc(sig("da_hi"), 1)
            for u in range(U_DSAO, U_F2I - 1):
                hi_of(u + 2)
                if u < U_MIXO:
                    i = u - U_DSAO
                    act.wait_ge(sig("my_ready"), i + 1)
                    nc.scalar.copy(myh[:, 2 * i:2 * i + 2, :], dt_[i % 2][:]).then_inc(sig("my_hi"), 1)
            squares(hview, SEQ, lambda k: act.wait_ge(sig("evac2"), U_MIXO - U_GQK + k // 2 + 1),
                    U_F2I + 1)
            split_x(4 * KC, SEQ)
            swiglu(U_F2I, 2)
            squares(hview, SEQ, lambda k: act.wait_ge(sig("down_evac"), 2 * KC + k + 1), U_PLEG + 1)
            act.wait_ge(sig("unit_done"), U_PLEG)
            act.dma_start(pin[:], p2[0, 0].rearrange("(j p) n -> p j n", p=P)).then_inc(sig("p_in"), 16)
            split_x(5 * KC, SEQ)
            for k in range(2):
                act.wait_ge(sig("p_turned"), k + 1)
                nc.scalar.copy(phi[:, k, :], bank(4 + k)).then_inc(sig("p_hi"), 1)
            for u in range(U_PLEG, U_PLEP):
                hi_of(u + 2)
                i = u - U_PLEG
                act.wait_ge(sig("unit_done"), u + 1)
                nc.scalar.activation(sgp[:, 2 * i:2 * i + 2, :], pair(bank(2 * (u % 2), 2)), ACT.Sigmoid
                                     ).then_inc(sig("pg_evac"), 1)
            nc.scalar.preload_act_table_set("natural_log_exp_and_others")
            for k in range(KC):
                act.wait_ge(sig("ple_added"), k + 1)
                if k >= 3:
                    act.wait_ge(sig("sq_added"), 7 * BY_ADDING.index(8) + k - 2)
                nc.scalar.activation(sq[k % 2][:, 0:SEQ] if k else sq_sum[:, 0:SEQ], hview(k), ACT.Square
                                     ).then_inc(sig("sq_done"), 1)
                nc.scalar.activation(fin[:, k, :], hview(k), ACT.Copy, scale=cv[:, G_FIN + k:G_FIN + k + 1]
                                     ).then_inc(sig("fin_ready"), 1)
            act.wait_ge(sig("total_done"), 9)
            rsqrt_of(bank(4)[:, 0:4], 1.0 / D)
            for j in (1, 3):
                act.wait_ge(sig("out_turned"), j + 1)
                act.wait_ge(sig("out_scale"), 1)
                nc.scalar.activation(outb[j][:], out_banks(j), ACT.Copy, scale=root[13 % 2][:, j:j + 1]
                                     ).then_inc(sig("out_odd"), 1)


        @block.vector
        def _(dve):
            step = Count(dve, sig("dve_step"))
            norms, roots = [0], [0]
            vec = nc.vector

            def add_square(n, k):
                T, _ = NORMS[n]
                dve.wait_ge(sig("sq_done"), 8 * n + k + 1)
                if k >= 2:
                    dve.wait_ge(sig("sq_added"), 7 * BY_ADDING.index(n) + k - 1)
                vec.tensor_tensor(sq_sum[:, 0:T], sq_sum[:, 0:T], sq[k % 2][:, 0:T], ALU.add
                                  ).then_inc(sig("sq_added"), 1)

            def refined(total, share, done=None):
                n = roots[0]
                roots[0] += 1
                y, m, a = (v[:, 0:total.shape[-1]] for v in (root[n % 2], root[2], sq_sum))
                dve.wait_ge(sig("log_done"), n + 1)
                step.up(vec.tensor_scalar(m, total, -0.5 * share, -0.5 * EPS, ALU.mult, ALU.add))
                dve.wait_ge(sig("root_done"), n + 1)
                step.up(vec.tensor_tensor(a, y, y, ALU.mult))
                step.wait()
                step.up(vec.tensor_tensor(a, a, m, ALU.mult))
                step.wait()
                ins = vec.scalar_tensor_tensor(out=y, in0=a, scalar=1.5, in1=y, op0=ALU.add, op1=ALU.mult)
                if done is not None:
                    ins.then_inc(sig(done), 1)
                    dve.wait_ge(sig(done), 1)
                    return y
                step.up(ins)
                step.wait()
                return y

            def norm():
                total, _ = norm_places(norms[0])
                norms[0] += 1
                return refined(total, 1.0 / D)

            def make_x(view, gain, T, base):
                scale = norm()
                for k in range(KC + 1):
                    if k < KC:
                        if k >= 3:
                            dve.wait_ge(sig("x_ready"), base + k - 2)
                        vec.scalar_tensor_tensor(out=nt[k % 3][:, 0:T], in0=view(k),
                                                 scalar=cv[:, gain + k:gain + k + 1], in1=scale,
                                                 op0=ALU.mult, op1=ALU.mult).then_inc(sig("nt_ready"), 1)
                    if k >= 1:
                        dve.wait_ge(sig("xhi_ready"), base + k)
                        vec.tensor_tensor(xlo[:, k - 1, 0:T], nt[(k - 1) % 3][:, 0:T],
                                          xhi[:, k - 1, 0:T].bitcast(F32), ALU.subtract
                                          ).then_inc(sig("x_ready"), 1)

            def add_normed(gain, T, first_token, base):
                scale = norm()
                for k in range(KC + 1):
                    if k < KC:
                        if k >= 3:
                            dve.wait_ge(sig("res_ready"), base + k - 2)
                        step.up(vec.scalar_tensor_tensor(out=nt[k % 3][:, 0:T], in0=mix[:, k, 0:T],
                                                         scalar=cv[:, gain + k:gain + k + 1], in1=scale,
                                                         op0=ALU.mult, op1=ALU.mult))
                    if k >= 1:
                        step.wait(step.n - (1 if k < KC else 0))
                        hk = h[:, k - 1, first_token:first_token + T]
                        vec.tensor_tensor(hk, hk, nt[(k - 1) % 3][:, 0:T], ALU.add
                                          ).then_inc(sig("res_ready"), 1)

            step.up(vec.memset(small[:, 0:1], 1.0))
            step.up(vec.memset(small[:, 1:2], -1.0))
            vec.memset(small[:, 2:3], EPS).then_inc(sig("cols_ready"), 1)
            for k in range(KC):
                dve.wait_ge(sig("x_turned"), k + 1)
                vec.tensor_copy(h[:, k, :], regions[:, k % 4, BANK - META:2 * BANK]).then_inc(sig("h_ready"), 1)
            dve.wait_ge(sig("h_ready"), KC)
            dve.wait_ge(sig("const_in"), 32)
            make_x(lambda k: h[:, k, :], G_PRE, T1, 0)

            def evac(u, dst, scale=None):
                dve.wait_ge(sig("unit_done"), u + 1)
                if scale is None:
                    vec.tensor_copy(dst, chunks1(u % 2)).then_inc(sig("evac"), 1)
                else:
                    vec.tensor_scalar(dst, chunks1(u % 2), scale, None, ALU.mult).then_inc(sig("evac"), 1)

            def evac_qkv(u0, qk, v):
                for c in range(6):
                    if c < 4:
                        evac(u0 + c, qk[:, 2 * c:2 * c + 2, :], 0.125 if c < 2 else None)
                    else:
                        evac(u0 + c, v[:, 2 * c - 8:2 * c - 6, :])

            evac_qkv(U_PROJ, qkf, vfm)
            dve.wait_ge(sig("unit_done"), U_F + 1)
            zsrc = chunks1(U_F % 2)[0:8, 0, :]
            vec.tensor_scalar(fz[:], zsrc, cv[0:8, C_BF:C_BF + 1], None, ALU.add).then_inc(sig("evac"), 1)
            dve.wait_ge(sig("evac"), U_F + 1)
            step.up(vec.tensor_scalar(fm[:], fz[:], -1.0, 0.0, ALU.mult, ALU.max))
            vec.scalar_tensor_tensor(out=fa[:], in0=fz[:], scalar=-1.0, in1=fz[:], op0=ALU.mult, op1=ALU.min
                                     ).then_inc(sig("f_z"), 1)
            evac_qkv(U_QKVB, qkb, vbm)
            dve.wait_ge(sig("f_ln"), 2)
            dve.wait_ge(sig("f_z"), 1)
            step.up(vec.tensor_tensor(fm[:], fm[:], fl[:], ALU.add))
            step.up(vec.memset(fz[:], 1.0))
            step.wait()
            vec.tensor_tensor_scan(negc[:], fz[:], fm[:], 0.0, ALU.mult, ALU.add).then_inc(sig("c_ready"), 1)
            for j in range(10):
                dve.wait_ge(sig("v_turned"), j + 1)
                if j < 4:
                    dst, src = vf[:, j, :], bank(j % 8)
                elif j == 4:
                    dst, src = vf_tail[:], bank(j % 8)[0:META, :]
                else:
                    dst, src = vb[:, j - 5, :], bank(j % 8)
                vec.tensor_copy(dst, src).then_inc(sig("v_ready"), 1)

            def out_lo(n, base, chunk0):
                head, rows, c, i, t0, tw, _ = item(n)
                dve.wait_ge(sig("o_hi"), base + n + 1)
                dst = slice(t0, t0 + tw)
                vec.tensor_tensor(xlo[rows, chunk0 + c, dst], bank(6 + n % 2)[rows, 0:tw],
                                  xhi[rows, chunk0 + c, dst].bitcast(F32), ALU.subtract
                                  ).then_inc(sig("o_lo"), 1)

            dve.wait_ge(sig("v_ready"), 10)
            dve.wait_ge(sig("c_copied"), 8)
            for n in range(NI + 3):
                if n < NI:
                    head, rows, c, i, t0, tw, w = item(n)
                    base = (n % 2) * 2 * BANK + (BANK if i < 4 else BANK - META)
                    dve.wait_ge(sig("fox_s"), n + 1)
                    scores = ps[0:tw, base:base + w]
                    step.up(vec.tensor_tensor_reduce(scores, scores, ncb[head // 4][0:tw, head % 4, 0:w], 1.0, -3e38,
                                                     ALU.add, ALU.max, fox_c[0:tw, 2, n:n + 1]))
                    step.wait()
                    vec.tensor_scalar(fox_c[0:tw, 0, n:n + 1], fox_c[0:tw, 2, n:n + 1], -1.0, None, ALU.mult
                                      ).then_inc(sig("fox_max"), 1)
                m = n - 1
                if 0 <= m < NI:
                    head, rows, c, i, t0, tw, w = item(m)
                    dve.wait_ge(sig("fox_exp"), m + 1)
                    dve.wait_ge(sig("fox_max"), m + 1)
                    step.up(vec.reciprocal(fox_c[0:tw, 2, m:m + 1], fox_c[0:tw, 1, m:m + 1]))
                    step.wait()
                    vec.tensor_scalar(fox_p[m % 3][0:tw, 0:w], fox_p[m % 3][0:tw, 0:w],
                                      fox_c[0:tw, 2, m:m + 1], None, ALU.mult).then_inc(sig("fox_norm"), 1)
                m = n - 3
                if 0 <= m < NI:
                    out_lo(m, 0, 0)
            dve.wait_ge(sig("o_done"), NI)
            for n in range(NI + 4):
                if n < NI:
                    w = sb_width(n)
                    dve.wait_ge(sig("sb_z"), n + 1)
                    if n >= 3:
                        dve.wait_ge(sig("sb_sp"), n - 2)
                    step.up(vec.tensor_scalar(sb_l[n % 3][:, 0:w], bank(n % 6)[:, 0:w], -1.0, None, ALU.mult))
                    step.wait()
                    vec.tensor_tensor(sb_l[n % 3][:, 0:w], sb_l[n % 3][:, 0:w], bank(n % 6)[:, 0:w], ALU.min
                                      ).then_inc(sig("sb_abs"), 1)
                m = n - 1
                if 0 <= m < NI:
                    w = sb_width(m)
                    dve.wait_ge(sig("sb_l"), m + 1)
                    if m >= 3:
                        dve.wait_ge(sig("sb_acc"), m - 2)
                    vec.scalar_tensor_tensor(out=sb_p[m % 3][:, 0:w], in0=bank(m % 6)[:, 0:w], scalar=0.0,
                                             in1=sb_l[m % 3][:, 0:w], op0=ALU.max, op1=ALU.add
                                             ).then_inc(sig("sb_sp"), 1)
                m = n - 4
                if 0 <= m < NI:
                    out_lo(m, NI, 4)
            dve.wait_ge(sig("sb_a"), NI)
            for m in range(8):
                if m % 2 == 0:
                    dve.wait_ge(sig("o_half"), m // 2 + 1)
                else:
                    dve.wait_ge(sig("unit_done"), U_O + m // 2 + 1)
                if m >= 2:
                    dve.wait_ge(sig("y_lo"), m - 1)
                ya, yb = regions[:, 2 * (m % 2), LO:LO + T1], regions[:, 2 * (m % 2) + 1, LO:LO + T1]
                t0, t1 = yt[2 * (m % 2)], yt[2 * (m % 2) + 1]
                step.up(vec.tensor_tensor(t0[:], ya, gates[:, m, :], ALU.mult))
                vec.tensor_tensor(t1[:], yb, gates[:, 8 + m, :], ALU.mult).then_inc(sig("y_evac"), 1)
                dve.wait_ge(sig("y_evac"), m + 1)
                vec.tensor_tensor(t0[:], t0[:], t1[:], ALU.add).then_inc(sig("y_sum"), 1)
                dve.wait_ge(sig("y_hi"), m + 1)
                vec.tensor_tensor(ylo[:, m, :], t0[:], yhi[:, m, :].bitcast(F32), ALU.subtract
                                  ).then_inc(sig("y_lo"), 1)
            for j in range(4):
                u = U_WOUT + j
                dve.wait_ge(sig("unit_done"), u + 1)
                vec.tensor_copy(mix[:, 2 * j:2 * j + 2, :], chunks1(u % 2)).then_inc(sig("mix_ready"), 1)
                for k in range(1, KC):
                    if j == (2 if k < 6 else 3):
                        add_square(1, k)
            dve.wait_ge(sig("mix_ready"), 4)
            add_normed(G_MIX, T1, 0, 0)
            dve.wait_ge(sig("res_ready"), KC)
            make_x(lambda k: h[:, k, :], G_FFN, T1, 8)

            def conv(dst, b, i, col, done):
                for tap in range(3):
                    for c in range(2):
                        src = regions[:, 2 * b + c, LO + META - 2 + tap:LO + META - 2 + tap + SEQ]
                        wcol = cv[:, bass.ds(i * 2 + (C_CW + 2 * FC * tap + col + c), 1)]
                        if tap == 0:
                            bcol = cv[:, bass.ds(i * 2 + (C_CB + col + c), 1)]
                            ins = vec.tensor_scalar(dst[:, c, :], src, wcol, bcol, ALU.mult, ALU.add)
                        else:
                            step.wait(step.n - 1)
                            ins = vec.scalar_tensor_tensor(out=dst[:, c, :], in0=src, scalar=wcol,
                                                           in1=dst[:, c, :], op0=ALU.mult, op1=ALU.add)
                        if tap == 2 and c == 1:
                            ins.then_inc(sig(done), 1)
                        else:
                            step.up(ins)

            def hidden_conv(i, first):
                b = U_UP % 2
                dve.wait_ge(sig("unit_done"), i * 2 + (U_UP + 1))
                if not first:
                    dve.wait_ge(sig("gate_act"), i)
                conv(cg, b, i, 0, "gate_ready")
                dve.wait_ge(sig("unit_done"), i * 2 + (U_UP + 2))
                if not first:
                    dve.wait_ge(sig("hid_lo"), i)
                conv(cvl, 1 - b, i, FC, "val_ready")
                dve.wait_ge(sig("val_ready"), i + 1)
                step.wait()
                dve.wait_ge(sig("gate_act"), i + 1)
                vec.tensor_tensor(cvl[:], cvl[:], gact[:], ALU.mult).then_inc(sig("prod"), 1)
                dve.wait_ge(sig("prod"), i + 1)
                dve.wait_ge(sig("hid_hi"), i + 1)
                vec.tensor_tensor(hlo[:, bass.ds(i * 2, 2), :], cvl[:], hhi[:, bass.ds(i * 2, 2), :].bitcast(F32),
                                  ALU.subtract).then_inc(sig("hid_lo"), 1)

            hidden_conv(0, True)
            with dve.Fori(1, FC // 2) as i:
                step.enter(i - 1, 10)
                hidden_conv(i, False)
            step.leave(FC // 2 - 1)
            for m in range(KC):
                if m < KC - 1:
                    dve.wait_ge(sig("down_done"), m + 1)
                else:
                    dve.wait_ge(sig("unit_done"), U_END1)
                vec.tensor_copy(mix[:, m, 0:SEQ], bank(m)).then_inc(sig("down_evac"), 1)
                if m >= 2:
                    add_square(3, m - 1)
            add_square(3, KC - 1)
            dve.wait_ge(sig("down_evac"), KC)
            add_normed(G_POST, SEQ, META, KC)

            hview = lambda k: h[:, k, META:T1]
            dve.wait_ge(sig("res_ready"), 2 * KC)
            make_x(hview, G_F1, SEQ, 2 * KC)

            def swiglu(unit0, layer):
                done = layer * (FC // 2)
                b = 1 - unit0 % 2

                def one(i, first):
                    dve.wait_ge(sig("unit_done"), i * 2 + (unit0 + 2))
                    dve.wait_ge(sig("hid_lo"), i + done)
                    dve.wait_ge(sig("gate_act"), i + (done + 1))
                    vec.tensor_tensor(cvl[:], gact[:], pair(bank(2 * b, 2)), ALU.mult).then_inc(sig("prod"), 1)
                    dve.wait_ge(sig("prod"), i + (done + 1))
                    dve.wait_ge(sig("hid_hi"), i + (done + 1))
                    vec.tensor_tensor(hlo[:, bass.ds(i * 2, 2), :], cvl[:],
                                      hhi[:, bass.ds(i * 2, 2), :].bitcast(F32), ALU.subtract
                                      ).then_inc(sig("hid_lo"), 1)

                one(0, True)
                with dve.Fori(1, FC // 2) as i:
                    one(i, False)
                for m in range(KC):
                    if m < KC - 1:
                        dve.wait_ge(sig("down_done"), (KC - 1) * layer + m + 1)
                    else:
                        dve.wait_ge(sig("unit_done"), unit0 + FC + FC // 2)
                    vec.scalar_tensor_tensor(out=hview(m), in0=bank(m), scalar=0.5, in1=hview(m),
                                             op0=ALU.mult, op1=ALU.add).then_inc(sig("down_evac"), 1)
                    if m >= 2:
                        add_square(3 + 2 * layer, m - 1)
                add_square(3 + 2 * layer, KC - 1)
                dve.wait_ge(sig("down_evac"), KC * (layer + 1))

            swiglu(U_F1I, 1)
            make_x(hview, G_MIX2, SEQ, 3 * KC)

            def out_of(u, dst, scale=None, src=None, last=True):
                dve.wait_ge(sig("unit_done"), u + 1)
                if u > U_GQK:
                    dve.wait_ge(sig("evac2"), u - U_GQK)
                src = pair(bank(2 * (u % 2), 2)) if src is None else src
                if scale is None:
                    ins = vec.tensor_copy(dst, src)
                else:
                    ins = vec.tensor_scalar(dst, src, scale, None, ALU.mult)
                if last:
                    ins.then_inc(sig("evac2"), 1)
                else:
                    step.up(ins)

            for c in range(4):
                out_of(U_GQK + c, gqk[:, 2 * c:2 * c + 2, :], float(np.float32(P ** -0.5)) if c < 2 else None)
            for c in range(4):
                out_of(U_GV + c, gvf[:, 2 * c:2 * c + 2, :])
            u = U_SPC
            first, second = bank(2 * (u % 2)), bank(2 * (u % 2) + 1)
            out_of(u, gaf[:], src=first[0:META], last=False)
            out_of(u, dkvf[:], src=second)
            u = U_SPC + 1
            first, second = bank(2 * (u % 2)), bank(2 * (u % 2) + 1)
            out_of(u, ikd[0:64, :], src=first[0:64], last=False)
            out_of(u, iwf[64:72, :], src=first[64:72], last=False)
            out_of(u, ikd[64:P, :], src=second[64:P])
            dve.wait_ge(sig("brow_done"), 1)
            vec.tensor_copy(brow[:], ps[0:8, 4 * BANK:4 * BANK + 640]).then_inc(sig("brow_ready"), 1)
            for j in range(4):
                dve.wait_ge(sig("gv_turned"), j + 1)
                vec.tensor_copy(gvt[:, j, :], bank(4 + 2 * (j % 2), 2)).then_inc(sig("gv_ready"), 1)
            scale = refined(bank(1), 1.0 / P)
            dve.wait_ge(sig("evac2"), U_GR - U_GQK)
            vec.scalar_tensor_tensor(out=ckvf[:], in0=dkvf[:], scalar=cv[:, C_CKV:C_CKV + 1], in1=scale,
                                     op0=ALU.mult, op1=ALU.mult).then_inc(sig("ckv_ready"), 1)
            dve.wait_ge(sig("ckv_turned"), 1)
            step.up(vec.tensor_copy(ckvt[:].rearrange("p j c -> p (j c)"), bank(2)))
            vec.tensor_scalar(iwt, bank(3)[:, 0:32], float(np.float32(8 ** -0.5)), None, ALU.mult
                              ).then_inc(sig("iw_ready"), 1)
            for hd in range(4):
                dve.wait_ge(sig("alpha_done"), hd + 1)
                step.up(vec.tensor_scalar(ax[:, hd, :], bank(4 + hd), cv[:, C_AB + hd:C_AB + hd + 1], None, ALU.add))
            step.wait()
            vec.scalar_tensor_tensor(out=al[:], in0=ax[:], scalar=-1.0, in1=ax[:], op0=ALU.mult, op1=ALU.min
                                     ).then_inc(sig("decay_x"), 1)
            dve.wait_ge(sig("decay_x"), 1)
            step.up(vec.tensor_scalar(ax[:], ax[:], -1.0 / 16, 0.0, ALU.mult, ALU.max))
            step.up(vec.memset(restart[:], 1.0))
            step.wait()
            step.up(vec.memset(restart[:].rearrange("p (j c) -> p j c", c=P)[:, :, 0:1], 0.0))
            dve.wait_ge(sig("decay_ln"), 1)
            step.up(vec.scalar_tensor_tensor(out=ax[:], in0=al[:], scalar=1.0 / 16, in1=ax[:],
                                             op0=ALU.mult, op1=ALU.add))
            step.wait()
            for hd in range(4):
                step.up(vec.tensor_tensor_scan(nbt[:, hd, :], restart[:], ax[:, hd, :], 0.0, ALU.mult, ALU.add))
            step.wait()

            def halves(ap, L):
                v = ap.rearrange("p (n c) -> p n c", c=2 ** L)
                return v[:, :, 0:2 ** (L - 1)], v[:, :, 2 ** (L - 1):]

            for q in range(NG + 2):
                if q < NG:
                    hd, kind = GI[q]
                    nbh = nbt[:, hd, :]
                    if 0 < kind < 8:
                        if q >= 3:
                            dve.wait_ge(sig("g_mm"), q - 2)
                        lo_n, up_n = halves(nbh, kind)
                        lo_f, up_f = halves(gf[q % 3][:], kind)
                        mid = lo_n[:, :, 2 ** (kind - 1) - 1:].to_broadcast([P, SEQ >> kind, 2 ** (kind - 1)])
                        step.up(vec.tensor_tensor(lo_f, lo_n, mid, ALU.subtract))
                        vec.tensor_tensor(up_f, mid, up_n, ALU.subtract).then_inc(sig("g_d"), 1)
                    elif kind == 8:
                        if hd:
                            dve.wait_ge(sig("g_mm"), cross_of(hd - 1) + 1)
                        tiles = nbh.rearrange("p (j c) -> p j c", c=P)
                        ends = tiles[:, 0:3, P - 1:].to_broadcast([P, 3, P])
                        step.up(vec.tensor_tensor(kx[:, 0:3, :], tiles[:, 0:3, :], ends, ALU.subtract))
                        vec.tensor_scalar(kx[:, 3:6, :], tiles[:, 1:4, :], -1.0, None, ALU.mult
                                          ).then_inc(sig("g_d"), 1)
                m = q - 1
                if 0 <= m < NG:
                    hd, kind = GI[m]
                    qh, kh = gqk[:, hd, :], gqk[:, 4 + hd, :]
                    if kind:
                        dve.wait_ge(sig("g_e"), m - hd)
                    if 0 < kind < 8:
                        lo_f, up_f = halves(gf[m % 3][:], kind)
                        step.up(vec.tensor_tensor(lo_f, lo_f, halves(kh, kind)[0], ALU.mult))
                        vec.tensor_tensor(up_f, up_f, halves(qh, kind)[1], ALU.mult).then_inc(sig("g_f"), 1)
                    elif kind == 8:
                        tiled = lambda ap: ap.rearrange("p (j c) -> p j c", c=P)
                        step.up(vec.tensor_tensor(kx[:, 0:3, :], kx[:, 0:3, :], tiled(kh)[:, 0:3, :], ALU.mult))
                        step.up(vec.tensor_tensor(kx[:, 3:6, :], kx[:, 3:6, :], tiled(qh)[:, 1:4, :], ALU.mult))
                        step.wait()
                        step.up(vec.tensor_scalar(kx2[:, 0, :], kx[:, 0, :], ex[:, 0:1], None, ALU.mult))
                        vec.tensor_scalar(kx2[:, 1, :], kx[:, 5, :], ex[:, 1:2], None, ALU.mult
                                          ).then_inc(sig("g_f"), 1)
                m = q - 2
                if 0 <= m < NG:
                    hd, kind = GI[m]
                    dve.wait_ge(sig("g_mm"), m + 1)
                    src = bank(m % 3).rearrange("p (j c) -> p j c", c=P)
                    if kind == 0:
                        if hd >= 2:
                            dve.wait_ge(sig("g_o"), hd - 1)
                        every = ident[:].rearrange("p (a c) -> p a c", a=1).to_broadcast([P, 4, P])
                        vec.tensor_tensor(sd[hd % 2][:], src, every, ALU.mult).then_inc(sig("g_cp"), 1)
                    elif kind < 8:
                        dve.wait_ge(sig("g_cp"), diag_seen(m) - 1)
                        mk = ga_m[:, (kind - 1) * P:kind * P] if kind < 5 else gb_m[:, (kind - 5) * P:(kind - 4) * P]
                        mk = mk.rearrange("p (a c) -> p a c", a=1).to_broadcast([P, 4, P])
                        vec.copy_predicated(sd[hd % 2][:], mk, src).then_inc(sig("g_cp"), 1)
            for k in range(9):
                if k < 8:
                    if k % 2 == 0:
                        scale = refined(bank(4 + k // 2), 1.0 / 256)
                    if k >= 3:
                        dve.wait_ge(sig("gy_lo"), k - 2)
                    step.up(vec.scalar_tensor_tensor(out=nt[k % 3][:, 0:SEQ], in0=gout[:, k, :],
                                                     scalar=cv[:, G_GLA + k:G_GLA + k + 1], in1=scale,
                                                     op0=ALU.mult, op1=ALU.mult))
                if k >= 1:
                    dve.wait_ge(sig("gy_hi"), k)
                    vec.tensor_tensor(gyl[:, k - 1, :], nt[(k - 1) % 3][:, 0:SEQ], gyh[:, k - 1, :].bitcast(F32),
                                      ALU.subtract).then_inc(sig("gy_lo"), 1)
                if k < 8:
                    step.wait()
                    if k in (0, 6):
                        dve.wait_ge(sig("grs_done"), 1 if k == 0 else 2)
                    vec.tensor_tensor(nt[k % 3][:, 0:SEQ], nt[k % 3][:, 0:SEQ], grs[:, k, :], ALU.mult
                                      ).then_inc(sig("gy_ready"), 1)
            for c in range(4):
                u = U_GLAO + c
                dve.wait_ge(sig("unit_done"), u + 1)
                dve.wait_ge(sig("evac2"), u - U_GQK)
                gc = g1[:, 2 * c:2 * c + 2, :]
                vec.tensor_tensor(gc, gc, pair(bank(2 * (u % 2), 2)), ALU.mult).then_inc(sig("evac2"), 1)
            for c in range(2):
                out_of(U_IQ + c, iqf[:, 2 * c:2 * c + 2, :], 0.125)
            dve.wait_ge(sig("iw_ready"), 1)
            for m in range(24):
                j, hd = 3 - m // 8, m % 8
                w = P * (j + 1)
                a = acc[0][:, 0:w]
                dve.wait_ge(sig("ix_relu"), m + 1)
                wcol = iwt[:, 8 * j + hd:8 * j + hd + 1]
                if hd == 0:
                    if m:
                        dve.wait_ge(sig("mask_ready"), m // 8)
                    vec.tensor_scalar(a, rl[m % 7][:, 0:w], wcol, None, ALU.mult).then_inc(sig("ix_acc"), 1)
                else:
                    dve.wait_ge(sig("ix_acc"), m)
                    vec.scalar_tensor_tensor(out=a, in0=rl[m % 7][:, 0:w], scalar=wcol, in1=a,
                                             op0=ALU.mult, op1=ALU.add).then_inc(sig("ix_acc"), 1)
                if hd == 7:
                    dve.wait_ge(sig("ix_acc"), m + 1)
                    step.up(vec.tensor_tensor(a[:, w - P:], a[:, w - P:], madd.bitcast(F32), ALU.add))
                    step.wait()
                    for r in range(16):
                        step.up(vec.max(m8, acc[r % 2][:, 0:w]))
                        step.wait()
                        step.up(vec.match_replace(acc[(r + 1) % 2][:, 0:w], m8, acc[r % 2][:, 0:w], -3e38))
                        step.wait()
                    vec.tensor_scalar(mj[:, mj_at[j]:mj_at[j] + w], a, -2e38, NEG, ALU.is_gt, ALU.mult
                                      ).then_inc(sig("mask_ready"), 1)
            dve.wait_ge(sig("mask_ready"), 3)
            dve.wait_ge(sig("bias_in"), 128)
            for n in range(ND + 3):
                if n < ND:
                    j, hd = DI[n]
                    w = P * (j + 1)
                    dve.wait_ge(sig("da_s"), n + 1)
                    if n >= 3:
                        dve.wait_ge(sig("da_t"), n - 2)
                    step.up(vec.tensor_tensor_reduce(dl[n % 3][:, 0:w], bank(n % 4)[:, 0:w],
                                                     bias[:, hd, w - 1::-1], 1.0, -3e38, ALU.add, ALU.max,
                                                     dst_[:, 2, n:n + 1]))
                    step.wait()
                    vec.tensor_scalar(dst_[:, 0, n:n + 1], dst_[:, 2, n:n + 1], -1.0, None, ALU.mult
                                      ).then_inc(sig("da_max"), 1)
                m = n - 1
                if 0 <= m < ND:
                    w = P * (DI[m][0] + 1)
                    dve.wait_ge(sig("da_exp"), m + 1)
                    dve.wait_ge(sig("da_max"), m + 1)
                    step.up(vec.reciprocal(dst_[:, 2, m:m + 1], dst_[:, 1, m:m + 1]))
                    step.wait()
                    vec.tensor_scalar(dl[m % 3][:, 0:w], dl[m % 3][:, 0:w], dst_[:, 2, m:m + 1], None, ALU.mult
                                      ).then_inc(sig("da_norm"), 1)
                m = n - 3
                if 0 <= m < ND:
                    j, hd = DI[m]
                    dve.wait_ge(sig("da_hi"), m + 1)
                    xs = slice(j * P, (j + 1) * P)
                    vec.tensor_tensor(xlo[:, hd, xs], bank(6 + m % 2)[:, 0:P], xhi[:, hd, xs].bitcast(F32),
                                      ALU.subtract).then_inc(sig("da_lo"), 1)
            for c in range(4):
                u = U_DSAO + c
                dve.wait_ge(sig("unit_done"), u + 1)
                dve.wait_ge(sig("evac2"), u - U_GQK)
                if c >= 2:
                    dve.wait_ge(sig("my_lo"), c - 1)
                tc_ = dt_[c % 2]
                vec.tensor_tensor(tc_[:], g2[:, 2 * c:2 * c + 2, :], pair(bank(2 * (u % 2), 2)), ALU.mult
                                  ).then_inc(sig("evac2"), 1)
                dve.wait_ge(sig("evac2"), u - U_GQK + 1)
                vec.tensor_tensor(tc_[:], tc_[:], g1[:, 2 * c:2 * c + 2, :], ALU.add).then_inc(sig("my_ready"), 1)
                dve.wait_ge(sig("my_hi"), c + 1)
                vec.tensor_tensor(myl[:, 2 * c:2 * c + 2, :], tc_[:], myh[:, 2 * c:2 * c + 2, :].bitcast(F32),
                                  ALU.subtract).then_inc(sig("my_lo"), 1)
            for c in range(4):
                u = U_MIXO + c
                hc = h[:, 2 * c:2 * c + 2, META:T1]
                dve.wait_ge(sig("unit_done"), u + 1)
                vec.tensor_tensor(hc, hc, pair(bank(2 * (u % 2), 2)), ALU.add).then_inc(sig("evac2"), 1)
                for k in range(1, KC):
                    if c == (2 if k < 6 else 3):
                        add_square(6, k)
            dve.wait_ge(sig("evac2"), U_F2I - U_GQK)
            make_x(hview, G_F2, SEQ, 4 * KC)
            swiglu(U_F2I, 2)
            make_x(hview, G_PLE, SEQ, 5 * KC)
            for k in range(2):
                dve.wait_ge(sig("p_hi"), k + 1)
                vec.tensor_tensor(plo[:, k, :], bank(4 + k), phi[:, k, :].bitcast(F32), ALU.subtract
                                  ).then_inc(sig("p_lo"), 1)
            for m in range(KC):
                if m < KC - 1:
                    dve.wait_ge(sig("ple_done"), m + 1)
                else:
                    dve.wait_ge(sig("unit_done"), U_PLEP + 1)
                step.up(vec.tensor_tensor(sgp[:, m, :], sgp[:, m, :], bank(m), ALU.mult))
                step.wait()
                vec.tensor_tensor(hview(m), hview(m), sgp[:, m, :], ALU.add).then_inc(sig("ple_added"), 1)
            scale = refined(bank(4)[:, 0:4], 1.0 / D, "out_scale")
            for j in (0, 2):
                dve.wait_ge(sig("out_turned"), j + 1)
                vec.tensor_scalar(outb[j][:], out_banks(j), scale[:, j:j + 1], None, ALU.mult
                                  ).then_inc(sig("out_even"), 1)

        @block.tensor
        def _(pe):
            mm = nc.tensor.matmul
            norms = [0]

            def tile_products(slot, tile, places, xh, xl, first, last):
                cols = slice(tile * P, (tile + 1) * P)
                for p_, (w, xx) in enumerate(((whi, xh), (whi, xl), (wlo, xh))):
                    for dst, tok in places:
                        ins = mm(dst, w[slot][:, cols], xx(tok), start=first and p_ == 0, stop=last and p_ == 2,
                                 skip_group_check=True)
                return ins

            def places_of(b, c, T):
                if T == T1:
                    r = regions[:, 2 * b + c, :]
                    return [(r[:, LO:BANK], slice(0, HALF)), (r[:, BANK:BANK + HALF], slice(HALF, T1))]
                return [(bank(2 * b + c), slice(0, SEQ))]

            def unit(b, T, xh, xl, x_base=None, chunks=2, x_sig="x_ready"):
                order = [(c, k) for c in range(chunks) for k in range(KC)]
                if x_base is not None:
                    order = [(c, k) for k in range(KC) for c in range(2)]
                for c, k in order:
                    if x_base is not None and c == 0:
                        pe.wait_ge(sig(x_sig), x_base + k + 1)
                    ins = tile_products(b, c * KC + k, places_of(b, c, T),
                                        lambda tok: xh[:, k, tok], lambda tok: xl[:, k, tok],
                                        k == 0, k == KC - 1)
                ins.then_inc(sig("unit_done"), 1)

            def norm():
                n = norms[0]
                norms[0] += 1
                T, _ = NORMS[n]
                total, parts = norm_places(n)
                if n in BY_ADDING:
                    pe.wait_ge(sig("sq_added"), 7 * (BY_ADDING.index(n) + 1))
                    for tok in parts:
                        ins = mm(total[:, tok], one_col.to_broadcast([P, P]), sq_sum[:, tok], start=True, stop=True)
                    ins.then_inc(sig("total_done"), 1)
                    return
                for k in range(KC):
                    pe.wait_ge(sig("sq_done"), 8 * n + k + 1)
                    for tok in parts:
                        ins = mm(total[:, tok], one_col.to_broadcast([P, P]), sq[k % 2][:, tok],
                                 start=(k == 0), stop=(k == KC - 1))
                    ins.then_inc(sig("sq_used" if k < KC - 1 else "total_done"), 1)

            pe.wait_ge(sig("ident_in"), 16)
            pe.wait_ge(sig("x_in0"), 80)
            for k in range(KC):
                if k == KC // 2:
                    pe.wait_ge(sig("x_in1"), 64)
                if k >= 4:
                    pe.wait_ge(sig("h_ready"), k - 3)
                r = regions[:, k % 4, :]
                nc.tensor.transpose(r[:, BANK - META:BANK], xmeta[:, k * P:(k + 1) * P], ident[0:META, 0:META])
                for j in range(4):
                    ins = nc.tensor.transpose(r[:, BANK + j * P:BANK + (j + 1) * P], xin[:, j, k * P:(k + 1) * P],
                                              ident[:])
                ins.then_inc(sig("x_turned"), 1)
            pe.wait_ge(sig("h_ready"), 7)
            pe.wait_ge(sig("cols_ready"), 1)
            norm()
            pe.wait_ge(sig("lo_done"), 1)
            unit(0, T1, xhi, xlo, 0)
            pe.wait_ge(sig("lo_done"), 2)
            unit(1, T1, xhi, xlo)

            def projection_pair(i, chunks=2):
                for b in range(2):
                    pe.wait_ge(sig("lo_done"), i * 2 + (b + 1))
                    pe.wait_ge(sig("evac"), i * 2 + (b - 1))
                    unit(b, T1, xhi, xlo, chunks=chunks if b == U_F % 2 else 2)

            with pe.Fori(1, U_F // 2) as i:
                projection_pair(i)
            projection_pair(U_F // 2, 1)
            with pe.Fori(U_F // 2 + 1, (U_O - 1) // 2) as i:
                projection_pair(i)
            pe.wait_ge(sig("lo_done"), U_O)
            pe.wait_ge(sig("evac"), U_O - 2)
            unit((U_O - 1) % 2, T1, xhi, xlo)
            pe.wait_ge(sig("evac"), U_O)
            for j in range(10):
                src = vfm if j < 5 else vbm
                a = (P * (j % 5), P) if j % 5 < 4 else ((SEQ, META) if j == 4 else (T1 - P, P))
                if j >= 8:
                    pe.wait_ge(sig("v_ready"), j - 7)
                for c in range(4):
                    ins = nc.tensor.transpose(bank(j % 8)[0:a[1], c * P:(c + 1) * P], src[:, c, a[0]:a[0] + a[1]],
                                              ident[:])
                ins.then_inc(sig("v_turned"), 1)
            pe.wait_ge(sig("v_ready"), 10)
            pe.wait_ge(sig("c_ready"), 1)

            for head in range(8):
                if head >= 4:
                    pe.wait_ge(sig("c_copied"), head - 3)
                for dst, tok in places_of(head // 2 % 2, head % 2, T1):
                    ins = mm(dst, ident[0:8, head:head + 1].to_broadcast([8, P]), negc[0:8, tok], start=True, stop=True)
                ins.then_inc(sig("c_spread"), 1)
            pe.wait_ge(sig("c_copied"), 8)
            pe.wait_ge(sig("exact_r"), 2)
            for n in range(NI + 3):
                if n < NI:
                    head, rows, c, i, t0, tw, w = item(n)
                    base = (n % 2) * 2 * BANK + (BANK if i < 4 else BANK - META)
                    if n >= 2:
                        pe.wait_ge(sig("fox_exp"), n - 1)
                    cuts = [(0, w)] if i < 4 else [(0, META), (META, T1)]
                    for a, z in cuts:
                        dst = ps[0:tw, base + a:base + z]
                        mm(dst, qkf[rows, c, t0:t0 + tw], qkf[rows, 4 + c, a:z], start=True, stop=(z < w),
                           skip_group_check=True)
                    ins = mm(ps[0:tw, base + t0:base + w], ident_r[0:tw, 0:tw], madd[0:tw, 0:tw], start=False,
                             stop=True, skip_group_check=True)
                    ins.then_inc(sig("fox_s"), 1)
                m = n - 2
                if 0 <= m < NI:
                    head, rows, c, i, t0, tw, w = item(m)
                    pe.wait_ge(sig("fox_norm"), m + 1)
                    if m >= 2:
                        pe.wait_ge(sig("fox_pt"), m - 1)
                    pm, dst = fox_p[m % 3], bank(4 + m % 2)
                    for b in range(min(i + 1, 4)):
                        ins = nc.tensor.transpose(dst[:, b * tw:(b + 1) * tw], pm[0:tw, b * P:(b + 1) * P],
                                                  ident[0:tw, 0:tw])
                    if i == 4:
                        ins = nc.tensor.transpose(dst[0:META, 64:80], pm[0:META, SEQ:T1], ident[0:META, 0:META])
                    ins.then_inc(sig("fox_t"), 1)
                m = n - 3
                if 0 <= m < NI:
                    head, rows, c, i, t0, tw, w = item(m)
                    pe.wait_ge(sig("fox_pt"), m + 1)
                    if m >= 2:
                        pe.wait_ge(sig("o_lo"), m - 1)
                    dst = bank(6 + m % 2)[rows, 0:tw]
                    hc = slice(64 * head, 64 * head + 64)
                    nb_ = min(i + 1, 4)
                    for b in range(nb_):
                        ins = mm(dst, vf[:, b, hc], fox_pt[m % 2][:, b * tw:(b + 1) * tw], start=(b == 0),
                                 stop=(b == nb_ - 1 and i < 4), skip_group_check=True)
                    if i == 4:
                        ins = mm(dst, vf_tail[:, hc], fox_pt[m % 2][0:META, 64:80], start=False, stop=True,
                                 skip_group_check=True)
                    ins.then_inc(sig("o_done"), 1)
            pe.wait_ge(sig("o_lo"), NI)
            for n in range(NI + 4):
                if n < NI:
                    head, rows, c, i, t0, tw, _ = item(n)
                    if n >= 6:
                        pe.wait_ge(sig("sb_a"), n - 5)
                    nb_ = i + 1
                    for b in range(nb_):
                        s0 = b * P if b < 4 else T1 - P
                        dst = bank(n % 6)[:, b * tw:(b + 1) * tw]
                        mm(dst, qkb[rows, 4 + c, s0:s0 + P], qkb[rows, c, t0:t0 + tw], start=(b == 0), stop=False,
                           skip_group_check=True)
                    mm(dst, ident_r[:], madds if i < 4 else madds_tail, start=False, stop=False,
                       skip_group_check=True).then_inc(sig("sb_z"), 1)
                m = n - 3
                if 0 <= m < NI:
                    head, rows, c, i, t0, tw, _ = item(m)
                    pe.wait_ge(sig("sb_sp"), m + 1)
                    w = sb_width(m)
                    sp_ = sb_p[m % 3][:, 0:w]
                    ins = mm(bank(m % 6)[:, 0:w], ntri, sp_, start=False, stop=(w == tw), skip_group_check=True)
                    for b in range(1, i + 1):
                        later = sp_[:, b * tw:(b + 1) * tw].rearrange("p (a c) -> p a c", a=1).to_broadcast([P, b, tw])
                        ins = mm(bank(m % 6)[:, 0:b * tw].rearrange("p (b c) -> p b c", c=tw),
                                 neg_col.to_broadcast([P, P]), later, start=False, stop=(b == i),
                                 skip_group_check=True)
                    ins.then_inc(sig("sb_acc"), 1)
                m = n - 4
                if 0 <= m < NI:
                    head, rows, c, i, t0, tw, _ = item(m)
                    pe.wait_ge(sig("sb_a"), m + 1)
                    pe.wait_ge(sig("o_lo"), NI + m - 1)
                    dst = bank(6 + m % 2)[rows, 0:tw]
                    nb_ = i + 1
                    for b in range(nb_):
                        ins = mm(dst, vb[:, b, 64 * head:64 * head + 64], sb_a[m % 2][:, b * tw:(b + 1) * tw],
                                 start=(b == 0), stop=(b == nb_ - 1), skip_group_check=True)
                    ins.then_inc(sig("o_done"), 1)
            pe.wait_ge(sig("sb_a"), NI)
            for m in range(8):
                u = U_O + m // 2
                if m % 2 == 0:
                    pe.wait_ge(sig("lo_done"), u + 1)
                if m >= 2:
                    pe.wait_ge(sig("y_evac"), m - 1)
                for side in range(2):
                    if m == 0 and side == 1:
                        pe.wait_ge(sig("o_lo"), 2 * NI)
                    for k in range(4):
                        kk = 4 * side + k
                        ins = tile_products(u % 2, 8 * (m % 2) + kk, places_of(m % 2, side, T1),
                                            lambda tok: xhi[:, kk, tok], lambda tok: xlo[:, kk, tok],
                                            k == 0, k == 3)
                ins.then_inc(sig("o_half" if m % 2 == 0 else "unit_done"), 1)
            pe.wait_ge(sig("y_evac"), 8)
            pe.wait_ge(sig("y_lo"), 8)
            for j in range(4):
                u = U_WOUT + j
                pe.wait_ge(sig("lo_done"), u + 1)
                if j >= 2:
                    pe.wait_ge(sig("mix_ready"), j - 1)
                unit(u % 2, T1, yhi, ylo)
            pe.wait_ge(sig("mix_ready"), 3)
            norm()
            pe.wait_ge(sig("mix_ready"), 4)
            norm()

            def up_pair(i, unit0, T, done, first=False, x_base=None):
                b = unit0 % 2
                pe.wait_ge(sig("lo_done"), i * 2 + (unit0 + 1))
                if not first:
                    pe.wait_ge(sig("gate_ready" if T == T1 else "gate_act"), i + done)
                unit(b, T, xhi, xlo, x_base)
                pe.wait_ge(sig("lo_done"), i * 2 + (unit0 + 2))
                if not first:
                    pe.wait_ge(sig("val_ready" if T == T1 else "prod"), i + done)
                else:
                    pe.wait_ge(sig("x_ready"), x_base + KC)
                unit(1 - b, T, xhi, xlo)

            def down(unit0, layer):
                pairs, up_b = (layer + 1) * (FC // 2), (unit0 - FC) % 2
                if layer == 0:
                    free = [(range(4 * up_b, 4 * up_b + 4), "gate_ready"),
                            (range(4 - 4 * up_b, 8 - 4 * up_b), "val_ready")]
                else:
                    free = [(range(4, 8), "hid_hi"), (range(2 * up_b, 2 * up_b + 2), "gate_act"),
                            (range(2 - 2 * up_b, 4 - 2 * up_b), "prod")]
                all_free = [(range(KC), None)]

                def two(b, j, first, last):
                    for m, freed in [(m, f) for banks, f in (free if first else all_free) for m in banks]:
                        if freed is not None:
                            pe.wait_ge(sig(freed), pairs - (1 if freed == "hid_hi" else 0))
                        for kk in range(2):
                            row = j * 2 + kk
                            ins = tile_products(b, kk * KC + m, [(bank(m), slice(0, SEQ))],
                                                lambda tok: hid_row(hhi, row, tok), lambda tok: hid_row(hlo, row, tok),
                                                first and kk == 0, last and kk == 1)
                        if last and m < KC - 1:
                            ins.then_inc(sig("down_done"), 1)
                    return ins
                b0 = unit0 % 2
                pe.wait_ge(sig("hid_lo"), pairs - 1)
                pe.wait_ge(sig("lo_done"), unit0 + 1)
                two(b0, 0, True, False).then_inc(sig("unit_done"), 1)
                with pe.Fori(0, (FC // 2 - 2) // 2) as i:
                    for b in range(2):
                        pe.wait_ge(sig("lo_done"), i * 2 + (unit0 + 2 + b))
                        two((b0 + 1 + b) % 2, i * 2 + (1 + b), False, False).then_inc(sig("unit_done"), 1)
                rest = FC // 2 - 1 - 2 * ((FC // 2 - 2) // 2)
                for q in range(rest):
                    j = FC // 2 - rest + q
                    if q == rest - 1:
                        pe.wait_ge(sig("hid_lo"), pairs)
                    pe.wait_ge(sig("lo_done"), unit0 + j + 1)
                    two((unit0 + j) % 2, j, False, j == FC // 2 - 1).then_inc(sig("unit_done"), 1)

            def hid_row(t, row, tok):
                if isinstance(row, int):
                    return t[:, row, tok]
                return t[:, bass.ds(row, 1), tok].rearrange("p a n -> p (a n)")

            up_pair(0, U_UP, T1, 0, True, 8)
            with pe.Fori(1, FC // 2) as i:
                up_pair(i, U_UP, T1, 0)
            down(U_DOWN, 0)
            pe.wait_ge(sig("down_evac"), 4)
            norm()

            norm()

            def swiglu(unit0, layer):
                done = layer * (FC // 2)
                up_pair(0, unit0, SEQ, done, True, KC * (layer + 1 if layer == 1 else 4))
                with pe.Fori(1, FC // 2) as i:
                    up_pair(i, unit0, SEQ, done)
                down(unit0 + FC, layer)
                pe.wait_ge(sig("down_evac"), KC * layer + 4)

            swiglu(U_F1I, 1)
            norm()

            def units(u0, n, xh, xl, x_base=None, x_sig="x_ready"):
                def one(b, i, wait_out, base=None):
                    pe.wait_ge(sig("lo_done"), i + (u0 + 1))
                    if wait_out:
                        pe.wait_ge(sig("evac2"), i + (u0 - 1 - U_GQK))
                    unit(b, SEQ, xh, xl, base, x_sig=x_sig)
                peel = 2 if x_base is not None else 0
                for q in range(peel):
                    one((u0 + q) % 2, q, False, x_base if q == 0 else None)
                with pe.Fori(peel // 2, n // 2) as i:
                    for q in range(2):
                        one((u0 + q) % 2, i * 2 + q, True)

            units(U_GQK, U_GR - U_GQK, xhi, xlo, 3 * KC)
            pe.wait_ge(sig("aux_in"), 80)
            pe.wait_ge(sig("x_ready"), 4 * KC)
            mm(bank(4)[0:8], relb[:], bucket[:, 0:BANK], start=True, stop=True)
            mm(bank(5)[0:8, 0:P], relb[:], bucket[:, BANK:BANK + P], start=True, stop=True
               ).then_inc(sig("brow_done"), 1)
            pe.wait_ge(sig("evac2"), U_GR - U_GQK)
            pe.wait_ge(sig("brow_ready"), 1)
            for j in range(4):
                if j >= 2:
                    pe.wait_ge(sig("gv_ready"), j - 1)
                for c in range(8):
                    ins = nc.tensor.transpose(bank(4 + 2 * (j % 2), 2)[:, c * P:(c + 1) * P],
                                              gvf[:, c, j * P:(j + 1) * P], ident[:])
                ins.then_inc(sig("gv_turned"), 1)
            pe.wait_ge(sig("ckv_sq"), 1)
            mm(bank(1), one_col.to_broadcast([P, P]), sq[0][:, 0:SEQ], start=True, stop=True
               ).then_inc(sig("ckv_sums"), 1)
            for j in range(4):
                nc.tensor.transpose(bank(3)[:, 8 * j:8 * j + 8], iwf[64:72, j * P:(j + 1) * P], ident[64:72, 64:72])
            pe.wait_ge(sig("ckv_ready"), 1)
            for j in range(4):
                ins = nc.tensor.transpose(bank(2)[:, j * P:(j + 1) * P], ckvf[:, j * P:(j + 1) * P], ident[:])
            ins.then_inc(sig("ckv_turned"), 1)
            pe.wait_ge(sig("gv_ready"), 4)
            for hd in range(4):
                mm(bank(4 + hd), aw[:, hd * P:(hd + 1) * P], gaf[:], start=True, stop=True
                   ).then_inc(sig("alpha_done"), 1)

            def side_left(u0, c):
                if c % 2:
                    pe.wait_ge(sig("evac2"), u0 + c // 2 + 1 - U_GQK)
                else:
                    pe.wait_ge(sig("side_out"), (0 if u0 == U_GR else 4) + c // 2 + 1)

            def side_tiles(u0, first, last, bank_of, before):
                for t in range(first, last):
                    u, c, k = u0 + t // UT, t // KC, t % KC
                    if t % UT == 0:
                        pe.wait_ge(sig("lo_done"), u + 1)
                    if k == 0 and before(c) is not None:
                        side_left(u0, before(c))
                    ins = tile_products(u % 2, t % UT, [(bank_of(c), slice(0, SEQ))],
                                        lambda tok: xhi[:, k, tok], lambda tok: xlo[:, k, tok], k == 0, k == KC - 1)
                    if k == KC - 1:
                        ins.then_inc(sig("side_half" if c % 2 == 0 else "unit_done"), 1)

            def gr_tiles(first, last):
                side_tiles(U_GR, first, last, gr_bank, lambda c: c - 1 if c >= 3 else None)

            pe.wait_ge(sig("iw_ready"), 1)
            gr_tiles(0, UT)
            pe.wait_ge(sig("decay_x"), 1)
            for q in range(1, NG + 4):
                if q <= NG:
                    gr_tiles(UT + 4 * (q - 1) // 3, UT + 4 * q // 3)
                m = q - 1
                if m == 2:
                    side_left(U_GR, 0)
                    side_left(U_GR, 1)
                if 0 <= m < NG:
                    hd, kind = GI[m]
                    if kind:
                        pe.wait_ge(sig("g_f"), m - hd)
                    if kind < 8:
                        if m >= 3 and (seen := diag_seen(m - 3)):
                            pe.wait_ge(sig("g_cp"), seen)
                        for j in range(4):
                            tile = slice(j * P, (j + 1) * P)
                            if kind == 0:
                                left, right = gqk[:, 4 + hd, tile], gqk[:, hd, tile]
                            else:
                                left = right = gf[m % 3][:, tile]
                            ins = mm(bank(m % 3)[:, tile], left, right, start=True, stop=True)
                    else:
                        if hd:
                            pe.wait_ge(sig("g_x"), hd)
                        pairs = ((kx[:, 0], kx[:, 3]), (kx[:, 2], kx[:, 5]), (kx2[:, 0], kx[:, 4]),
                                 (kx2[:, 0], kx2[:, 1]), (kx[:, 1], kx[:, 4]), (kx[:, 1], kx2[:, 1]))
                        for b, (left, right) in enumerate(pairs):
                            ins = mm(ps[:, 3 * BANK + b * P:3 * BANK + (b + 1) * P], left, right,
                                     start=True, stop=True)
                    ins.then_inc(sig("g_mm"), 1)
                m = q - 3
                if 0 <= m < NG and GI[m][1] == 8:
                    hd = GI[m][0]
                    pe.wait_ge(sig("g_x"), hd + 1)
                    pe.wait_ge(sig("g_cp"), 8 * (hd + 1))
                    if hd:
                        pe.wait_ge(sig("g_out"), hd)
                    d, xs = sd[hd % 2], sx[hd % 2]
                    for e in range(2):
                        dst = bank(5 + e)
                        vc = slice((2 * hd + e) * P, (2 * hd + e + 1) * P)
                        plan = [(0, 0, d[:, 0]), (1, 1, d[:, 1]), (2, 2, d[:, 2]), (3, 3, d[:, 3]),
                                (0, 1, xs[:, 0]), (2, 3, xs[:, 1]), (0, 2, xs[:, 2]), (0, 3, xs[:, 3]),
                                (1, 2, xs[:, 4]), (1, 3, xs[:, 5])]
                        for x_, (s_, t_, rhs) in enumerate(plan):
                            ins = mm(dst[:, t_ * P:(t_ + 1) * P], gvt[:, s_, vc], rhs, start=(x_ == 0),
                                     stop=(x_ == len(plan) - 1), skip_group_check=True)
                    ins.then_inc(sig("g_o"), 1)
            for k in range(8):
                pe.wait_ge(sig("gn_sq"), k + 1)
                mm(bank(4 + k // 2), one_col.to_broadcast([P, P]), sq[k % 2][:, 0:SEQ], start=(k % 2 == 0),
                   stop=(k % 2 == 1)).then_inc(sig("gn_used"), 1)
            for i in range(4):
                u = U_MG1 + i
                pe.wait_ge(sig("lo_done"), u + 1)
                if i == 2:
                    pe.wait_ge(sig("gy_ready"), 7)
                for c in range(2):
                    for k in range(KC):
                        ins = tile_products(u % 2, c * KC + k, [(bank(2 * i + c), slice(0, SEQ))],
                                            lambda tok: xhi[:, k, tok], lambda tok: xlo[:, k, tok],
                                            k == 0, k == KC - 1)
                ins.then_inc(sig("unit_done"), 1)
            pe.wait_ge(sig("gy_lo"), 8)
            units(U_GLAO, 4, gyh, gyl)
            units(U_IQ, 2, xhi, xlo)

            def beside_indexer(c):
                side_tiles(U_DQ, KC * c, KC * (c + 1), lambda c: bank(4 + c % 4), lambda c: c - 4 if c >= 4 else None)

            beside_indexer(0)
            pe.wait_ge(sig("evac2"), U_DQ - U_GQK)
            for m in range(24):
                j, hd = 3 - m // 8, m % 8
                rows = slice(64 * (hd % 2), 64 * (hd % 2) + 64)
                if m >= 4:
                    pe.wait_ge(sig("ix_relu"), m - 3)
                mm(bank(m % 4)[:, 0:P * (j + 1)], iqf[rows, hd // 2, j * P:(j + 1) * P], ikd[rows, 0:P * (j + 1)],
                   start=True, stop=True).then_inc(sig("ix_dots"), 1)
                if m % 8 == 7:
                    for c in range(1, 16):
                        if side_at(c) == m:
                            beside_indexer(c)
            for c in range(12, 16):
                side_left(U_DQ, c)
            pe.wait_ge(sig("ix_relu"), 24)
            for n in range(ND + 3):
                if n < ND:
                    j, hd = DI[n]
                    w = P * (j + 1)
                    if j:
                        pe.wait_ge(sig("mask_ready"), j)
                    if n >= 4:
                        pe.wait_ge(sig("da_max"), n - 3)
                    dst = bank(n % 4)[:, 0:w]
                    mm(dst, dq[:, hd, j * P:(j + 1) * P], ckvf[:, 0:w], start=True, stop=False)
                    mask = mj[:, mj_at[j]:mj_at[j] + w] if j else madd
                    mm(dst, ident_r[:], mask, start=False, stop=True).then_inc(sig("da_s"), 1)
                m = n - 2
                if 0 <= m < ND:
                    j, hd = DI[m]
                    pe.wait_ge(sig("da_norm"), m + 1)
                    if m >= 2:
                        pe.wait_ge(sig("da_pt"), m - 1)
                    for b in range(j + 1):
                        ins = nc.tensor.transpose(bank(4 + m % 2)[:, b * P:(b + 1) * P],
                                                  dl[m % 3][:, b * P:(b + 1) * P], ident[:])
                    ins.then_inc(sig("da_t"), 1)
                m = n - 3
                if 0 <= m < ND:
                    j, hd = DI[m]
                    pe.wait_ge(sig("da_pt"), m + 1)
                    if m >= 2:
                        pe.wait_ge(sig("da_lo"), m - 1)
                    for b in range(j + 1):
                        ins = mm(bank(6 + m % 2)[:, 0:P], ckvt[:, b, :], dpt[m % 2][:, b * P:(b + 1) * P],
                                 start=(b == 0), stop=(b == j))
                    ins.then_inc(sig("da_o"), 1)
            pe.wait_ge(sig("da_max"), ND)
            units(U_DSAO, 4, xhi, xlo, ND - KC, "da_lo")
            pe.wait_ge(sig("my_lo"), 4)
            units(U_MIXO, 4, myh, myl)
            norm()
            swiglu(U_F2I, 2)
            norm()
            pe.wait_ge(sig("lo_done"), U_PLEG + 1)
            unit(U_PLEG % 2, SEQ, xhi, xlo, 5 * KC)
            pe.wait_ge(sig("p_in"), 16)
            for k in range(2):
                for j in range(4):
                    ins = nc.tensor.transpose(bank(4 + k)[:, j * P:(j + 1) * P], pin[:, j, k * P:(k + 1) * P], ident[:])
                ins.then_inc(sig("p_turned"), 1)
            for u in range(U_PLEG + 1, U_PLEP):
                pe.wait_ge(sig("lo_done"), u + 1)
                if u >= U_PLEG + 2:
                    pe.wait_ge(sig("pg_evac"), u - U_PLEG - 1)
                unit(u % 2, SEQ, xhi, xlo)
            pe.wait_ge(sig("lo_done"), U_PLEP + 1)
            pe.wait_ge(sig("pg_evac"), 4)
            pe.wait_ge(sig("p_lo"), 2)
            for m in range(KC):
                for kk in range(2):
                    ins = tile_products(U_PLEP % 2, kk * KC + m, [(bank(m), slice(0, SEQ))],
                                        lambda tok: phi[:, kk, tok], lambda tok: plo[:, kk, tok], kk == 0, kk == 1)
                ins.then_inc(sig("ple_done" if m < KC - 1 else "unit_done"), 1)
            def turn(j, k):
                return nc.tensor.transpose(out_banks(j)[:, k * P:(k + 1) * P], fin[:, k, j * P:(j + 1) * P], ident[:])

            pe.wait_ge(sig("ple_added"), 4)
            for k in range(KC):
                pe.wait_ge(sig("fin_ready"), k + 1)
                for j in range(2):
                    ins = turn(j, k)
                    if k == KC - 1:
                        ins.then_inc(sig("out_turned"), 1)
            pe.wait_ge(sig("ple_added"), KC)
            pe.wait_ge(sig("sq_added"), 7 * len(BY_ADDING))
            for j in range(4):
                ins = mm(bank(4)[:, j:j + 1], sq_sum[:, j * P:(j + 1) * P], one_col, start=(j == 0), stop=(j == 3),
                         skip_group_check=True)
            ins.then_inc(sig("total_done"), 1)
            for j in (2, 3):
                if j == 3:
                    pe.wait_ge(sig("out_even"), 1)
                for k in range(KC):
                    ins = turn(j, k)
                ins.then_inc(sig("out_turned"), 1)


_OUTS = [((1, 512, 1024), 'float32')]


def shape_constants():
    r, c = np.arange(P)[:, None], np.arange(P)[None, :]
    q = np.arange(META)[None, :]
    late = r - (P - META)
    masks = np.concatenate([
        -1.0 * (r >= c), NEG * (c > r), NEG * (r >= c),
        np.where((late >= 0) & (late < q), 0.0, NEG)], axis=1)
    differ = r ^ c
    gmask = np.concatenate([(differ >= 2 ** b) & (differ < 2 ** (b + 1)) & (r < c) for b in range(7)], axis=1)
    dist = np.maximum(np.arange(640) - (P - 1), 0)
    exact = 16
    large = exact + (np.log(np.maximum(dist, 1).astype(np.float32) / exact) / math.log(128 / exact)
                     * (32 - exact)).astype(np.int32)
    bucket = np.where(dist < exact, dist, np.minimum(large, 31))
    onehot = (np.arange(32)[:, None] == bucket[None, :]).astype(np.float32)
    packed = np.ascontiguousarray(gmask.astype(np.int8)).view(np.int32)
    return np.eye(P, dtype=np.float32), masks.astype(np.float32), packed, onehot


def kernel(**inputs):
    import numpy as _np
    import concourse.bacc as _bacc
    from concourse import mybir as _mybir
    from concourse.bass_utils import run_bass_kernel_spmd as _run

    v = {k: _np.asarray(a) for k, a in inputs.items()}
    arrays = layout(v)
    nc = _bacc.Bacc("TRN2", target_bir_lowering=False, num_devices=1)
    args = []
    for name, a in list(arrays.items()):
        a = _np.ascontiguousarray(a)
        arrays[name] = a
        args.append(nc.dram_tensor(name, a.shape, _mybir.dt.from_np(a.dtype), kind="ExternalInput").ap())
    for i, (shape, dtype) in enumerate(_OUTS):
        dt = _mybir.dt.from_np(_np.dtype(dtype))
        args.append(nc.dram_tensor(f"out_{i}_dram", shape, dt, kind="ExternalOutput").ap())
    build(nc, *args)
    r = _run(nc, [arrays], core_ids=[0])
    return r.results[0]["out_0_dram"]
```
